# Optimizing a Trainium2 kernel written in Bass

```python
import math
import jax, jax.numpy as jnp
from jax import lax
import numpy as np

D_MODEL = 2048
BATCH = 1
SEQ = 256
DEPTH = 2

HEAD_DIM = 128
N_GROUPS = 4
GROUP_HEADS = D_MODEL // HEAD_DIM // N_GROUPS
GROUP_WIDTH = GROUP_HEADS * HEAD_DIM
Q_BLOCK = 128
ROPE_THETA = 500000.0
ROT_FRAC_DEN = 4
EPS = 1e-6

DIFF_SUB_DIM = HEAD_DIM // 2
MLA_Q_RANK = 448
MLA_KV_RANK = 128
MLA_NOPE_DIM = 128
MLA_ROPE_DIM = 64
MLA_V_DIM = HEAD_DIM
IDX_HEADS = 16
IDX_DIM = 64
TOPK_MAX = 256

IN_SIZES = ((GROUP_WIDTH,) * 3
            + (MLA_Q_RANK, MLA_KV_RANK, MLA_ROPE_DIM)
            + (GROUP_WIDTH,) * 3
            + (GROUP_WIDTH,) * 3
            + (IDX_HEADS * IDX_DIM, IDX_DIM, IDX_HEADS))
IN_WIDTH = sum(IN_SIZES)
IN_SPLITS = tuple(int(v) for v in np.cumsum(IN_SIZES)[:-1])

FFN_HIDDEN = ((8 * D_MODEL // 3 + 255) // 256) * 256

kernel_name = "hymba_style_diff_mla_stickbreak_dsa_block"

def _rms(x, g):
    xf = x.astype(jnp.float32)
    y = xf * lax.rsqrt(jnp.mean(xf * xf, axis=-1, keepdims=True) + EPS)
    return (y * g.astype(jnp.float32)).astype(x.dtype)

def _rotary(x, pos, rot_dim):
    half = rot_dim // 2
    inv = ROPE_THETA ** (-jnp.arange(half, dtype=jnp.float32) * 2.0 / rot_dim)
    ang = pos.astype(jnp.float32)[:, None] * inv[None, :]
    cos = jnp.cos(ang)[None, :, None, :]
    sin = jnp.sin(ang)[None, :, None, :]
    xf = x.astype(jnp.float32)
    x1 = xf[..., :half]
    x2 = xf[..., half:rot_dim]
    out = jnp.concatenate([x1 * cos - x2 * sin, x2 * cos + x1 * sin, xf[..., rot_dim:]], axis=-1)
    return out.astype(x.dtype)

def _sweep(fn, *q_side):
    B, S = q_side[0].shape[:2]
    nb = S // Q_BLOCK
    xs = tuple(jnp.moveaxis(a.reshape(B, nb, Q_BLOCK, *a.shape[2:]), 1, 0) for a in q_side)
    starts = jnp.arange(nb, dtype=jnp.int32) * Q_BLOCK
    out = lax.map(lambda args: fn(args[0], *args[1]), (starts, xs))
    return jnp.moveaxis(out, 0, 1).reshape(B, S, *out.shape[3:])

def _causal_softmax(q0, qb, k, scale):
    T, S = qb.shape[1], k.shape[1]
    s = jnp.einsum('bthd,bshd->bhts', qb, k).astype(jnp.float32) * scale
    mask = jnp.arange(S)[None, :] <= (q0 + jnp.arange(T))[:, None]
    return jax.nn.softmax(jnp.where(mask, s, -jnp.inf), axis=-1)

def _diff_attention(qp, kp, vp, pos, qk_norm, lam_vecs, subln, layer_idx):
    B, S, _ = qp.shape
    rot = DIFF_SUB_DIM // ROT_FRAC_DEN
    q = _rotary(_rms(qp.reshape(B, S, GROUP_HEADS * 2, DIFF_SUB_DIM), qk_norm[0]), pos, rot)
    k = _rotary(_rms(kp.reshape(B, S, GROUP_HEADS * 2, DIFF_SUB_DIM), qk_norm[1]), pos, rot)
    q = q.reshape(B, S, GROUP_HEADS, 2, DIFF_SUB_DIM)
    k = k.reshape(B, S, GROUP_HEADS, 2, DIFF_SUB_DIM)
    q1, q2 = q[..., 0, :], q[..., 1, :]
    k1, k2 = k[..., 0, :], k[..., 1, :]
    v = vp.reshape(B, S, GROUP_HEADS, HEAD_DIM)
    lam_init = 0.8 - 0.6 * math.exp(-0.3 * layer_idx)
    lv = lam_vecs.astype(jnp.float32)
    lam = jnp.exp(jnp.sum(lv[0] * lv[1])) - jnp.exp(jnp.sum(lv[2] * lv[3])) + lam_init
    scale = DIFF_SUB_DIM ** -0.5

    def block(q0, q1b, q2b):
        a = _causal_softmax(q0, q1b, k1, scale) - lam * _causal_softmax(q0, q2b, k2, scale)
        return jnp.einsum('bhts,bshd->bthd', a.astype(v.dtype), v)

    o = _sweep(block, q1, q2)
    o = _rms(o, subln) * (1.0 - lam_init)
    return o.reshape(B, S, GROUP_WIDTH)

def _mla(cq, ckv, kr, pos, q_a_norm, wq_b, kv_a_norm, wkv_b, qk_norm):
    B, S, _ = cq.shape
    qd = MLA_NOPE_DIM + MLA_ROPE_DIM
    q = (_rms(cq, q_a_norm) @ wq_b).reshape(B, S, GROUP_HEADS, qd)
    kv = (_rms(ckv, kv_a_norm) @ wkv_b).reshape(B, S, GROUP_HEADS, MLA_NOPE_DIM + MLA_V_DIM)
    k_nope, v = kv[..., :MLA_NOPE_DIM], kv[..., MLA_NOPE_DIM:]
    k_rope = jnp.broadcast_to(kr[:, :, None, :], (B, S, GROUP_HEADS, MLA_ROPE_DIM))
    k = jnp.concatenate([k_nope, k_rope], axis=-1)
    q = _rms(q, qk_norm[0])
    k = _rms(k, qk_norm[1])
    q = jnp.concatenate([q[..., :MLA_NOPE_DIM], _rotary(q[..., MLA_NOPE_DIM:], pos, MLA_ROPE_DIM)], axis=-1)
    k = jnp.concatenate([k[..., :MLA_NOPE_DIM], _rotary(k[..., MLA_NOPE_DIM:], pos, MLA_ROPE_DIM)], axis=-1)
    scale = qd ** -0.5

    def block(q0, qb):
        p = _causal_softmax(q0, qb, k, scale)
        return jnp.einsum('bhts,bshd->bthd', p.astype(v.dtype), v)

    return _sweep(block, q).reshape(B, S, GROUP_WIDTH)

def _stick_breaking(qp, kp, vp):
    B, S, _ = qp.shape
    q = qp.reshape(B, S, GROUP_HEADS, HEAD_DIM)
    k = kp.reshape(B, S, GROUP_HEADS, HEAD_DIM)
    v = vp.reshape(B, S, GROUP_HEADS, HEAD_DIM)
    scale = HEAD_DIM ** -0.5

    def block(q0, qb):
        T = qb.shape[1]
        z = jnp.einsum('bthd,bshd->bhts', qb, k).astype(jnp.float32) * scale
        mask = jnp.arange(S)[None, :] < (q0 + jnp.arange(T))[:, None]
        log_1mb = jnp.where(mask, jax.nn.log_sigmoid(-z), 0.0)
        suffix = lax.cumsum(log_1mb, axis=3, reverse=True) - log_1mb
        a = jnp.where(mask, jnp.exp(jax.nn.log_sigmoid(z) + suffix), 0.0)
        return jnp.einsum('bhts,bshd->bthd', a.astype(v.dtype), v)

    return _sweep(block, q).reshape(B, S, GROUP_WIDTH)

def _dsa(qp, kp, vp, iqp, ikp, iwp, pos, qk_norm, idx_k_norm):
    B, S, _ = qp.shape
    rot = HEAD_DIM // ROT_FRAC_DEN
    irot = IDX_DIM // ROT_FRAC_DEN
    q = _rotary(_rms(qp.reshape(B, S, GROUP_HEADS, HEAD_DIM), qk_norm[0]), pos, rot)
    k = _rotary(_rms(kp.reshape(B, S, GROUP_HEADS, HEAD_DIM), qk_norm[1]), pos, rot)
    v = vp.reshape(B, S, GROUP_HEADS, HEAD_DIM)
    iq = _rotary(iqp.reshape(B, S, IDX_HEADS, IDX_DIM), pos, irot)
    ik = _rotary(_rms(ikp, idx_k_norm)[:, :, None, :], pos, irot)[:, :, 0, :]
    topk = min(TOPK_MAX, S // 4)
    scale = HEAD_DIM ** -0.5
    gather = jax.vmap(lambda arr, ids: arr[ids])

    def block(q0, qb, iqb, iwb):
        T = qb.shape[1]
        tpos = q0 + jnp.arange(T)
        isc = jnp.einsum('bthd,bsd->bths', iqb, ik).astype(jnp.float32) * (IDX_DIM ** -0.5)
        isc = jnp.einsum('bths,bth->bts', jax.nn.relu(isc), iwb.astype(jnp.float32)) * (IDX_HEADS ** -0.5)
        admissible = jnp.arange(S)[None, :] <= tpos[:, None]
        isc = jnp.where(admissible[None], isc, -jnp.inf)
        _, idx = lax.top_k(isc, topk)
        valid = idx <= tpos[None, :, None]
        ksel = gather(k, idx)
        vsel = gather(v, idx)
        s = jnp.einsum('bthd,btkhd->bhtk', qb, ksel).astype(jnp.float32) * scale
        p = jax.nn.softmax(jnp.where(valid[:, None], s, -jnp.inf), axis=-1)
        return jnp.einsum('bhtk,btkhd->bthd', p.astype(vsel.dtype), vsel)

    return _sweep(block, q, iq, iwp).reshape(B, S, GROUP_WIDTH)

def setup_inputs(seed: int = 0) -> dict:
    key = jax.random.key(seed)
    ks = jax.random.split(key, 20)

    def nrm(k, shape, scale):
        return jax.random.normal(k, shape, jnp.float32) * scale

    def gain(k, shape):
        return 1.0 + 0.02 * jax.random.normal(k, shape, jnp.float32)

    L = DEPTH
    return {
        "x": nrm(ks[0], (BATCH, SEQ, D_MODEL), 1.0),
        "attn_norm": gain(ks[1], (L, D_MODEL)),
        "w_in": nrm(ks[2], (L, D_MODEL, IN_WIDTH), D_MODEL ** -0.5),
        "diff_qk_norm": gain(ks[3], (L, 2, DIFF_SUB_DIM)),
        "diff_lambda": nrm(ks[4], (L, 4, DIFF_SUB_DIM), 0.1),
        "diff_subln": gain(ks[5], (L, HEAD_DIM)),
        "mla_q_a_norm": gain(ks[6], (L, MLA_Q_RANK)),
        "mla_wq_b": nrm(ks[7], (L, MLA_Q_RANK, GROUP_HEADS * (MLA_NOPE_DIM + MLA_ROPE_DIM)), MLA_Q_RANK ** -0.5),
        "mla_kv_a_norm": gain(ks[8], (L, MLA_KV_RANK)),
        "mla_wkv_b": nrm(ks[9], (L, MLA_KV_RANK, GROUP_HEADS * (MLA_NOPE_DIM + MLA_V_DIM)), MLA_KV_RANK ** -0.5),
        "mla_qk_norm": gain(ks[10], (L, 2, MLA_NOPE_DIM + MLA_ROPE_DIM)),
        "dsa_qk_norm": gain(ks[11], (L, 2, HEAD_DIM)),
        "idx_k_norm": gain(ks[12], (L, IDX_DIM)),
        "w_o": nrm(ks[13], (L, N_GROUPS * GROUP_WIDTH, D_MODEL), (N_GROUPS * GROUP_WIDTH) ** -0.5),
        "ffn_norm": gain(ks[14], (L, D_MODEL)),
        "w_gate": nrm(ks[15], (L, D_MODEL, FFN_HIDDEN), D_MODEL ** -0.5),
        "w_up": nrm(ks[16], (L, D_MODEL, FFN_HIDDEN), D_MODEL ** -0.5),
        "w_down": nrm(ks[17], (L, FFN_HIDDEN, D_MODEL), FFN_HIDDEN ** -0.5),
    }

def reference(x, attn_norm, w_in, diff_qk_norm, diff_lambda, diff_subln, mla_q_a_norm, mla_wq_b,
              mla_kv_a_norm, mla_wkv_b, mla_qk_norm, dsa_qk_norm, idx_k_norm, w_o, ffn_norm,
              w_gate, w_up, w_down):
    S = x.shape[1]
    pos = jnp.arange(S, dtype=jnp.int32)
    for l in range(DEPTH):
        h = _rms(x, attn_norm[l])
        (a_q, a_k, a_v, b_cq, b_ckv, b_kr, c_q, c_k, c_v,
         d_q, d_k, d_v, d_iq, d_ik, d_iw) = jnp.split(h @ w_in[l], IN_SPLITS, axis=-1)
        o_a = _diff_attention(a_q, a_k, a_v, pos, diff_qk_norm[l], diff_lambda[l], diff_subln[l], l)
        o_b = _mla(b_cq, b_ckv, b_kr[:, :, None, :][:, :, 0, :], pos, mla_q_a_norm[l], mla_wq_b[l],
                   mla_kv_a_norm[l], mla_wkv_b[l], mla_qk_norm[l])
        o_c = _stick_breaking(c_q, c_k, c_v)
        o_d = _dsa(d_q, d_k, d_v, d_iq, d_ik, d_iw, pos, dsa_qk_norm[l], idx_k_norm[l])
        mixed = jnp.concatenate([o_a, o_b, o_c, o_d], axis=-1)
        x = x + mixed @ w_o[l]
        h = _rms(x, ffn_norm[l])
        x = x + (jax.nn.silu(h @ w_gate[l]) * (h @ w_up[l])) @ w_down[l]
    return x


_drawn_inputs = setup_inputs


def setup_inputs(seed=0):
    import zlib

    import numpy as np

    out = dict(_drawn_inputs(seed))
    spreads = {}
    factors = {'diff_qk_norm': 3.6,
     'diff_subln': 4.241,
     'mla_q_a_norm': 8.0,
     'mla_kv_a_norm': 8.0,
     'mla_qk_norm': 8.0,
     'dsa_qk_norm': 8.0,
     'idx_k_norm': 4.375}
    for name, (base, spread) in spreads.items():
        noise = np.random.default_rng([zlib.crc32(name.encode()), seed]).standard_normal(out[name].shape)
        drawn = base * np.exp(spread * noise) if base else spread * noise
        out[name] = __import__('jax').numpy.asarray(drawn.astype(out[name].dtype))
    for name, factor in factors.items():
        out[name] = (out[name] * factor).astype(out[name].dtype)
    return out
```

```python
import concourse.bass as bass
from concourse import mybir
from contextlib import ExitStack

ATTENTION = [
    ("iq1", ["hT 0; xms a; lam 0",
             "hT 1; lam 1",
             "hT 2; lam 2",
             "hT 3"]),
    ("ikw", ["E iq1",
             "",
             "",
             ""]),
    ("iq0", ["E ikw",
             "ikss",
             "iknrm",
             ""]),
    ("ckr", ["E iq0",
             "iqrope",
             "iqT 0; iqT 1",
             "iqT 2; iqT 3; ikT"]),
    ("cq", ["E ckr; idx 0",
             "idx 1; idx 2",
             "idx 3; idx 4",
             "idx 5"]),
    ("dq", ["E cq; idx 6",
             "idx 7; latss",
             "topk 0; latT 0",
             "topk 1; latT 1; ckvT"]),
    ("dk", ["E dq; topk 2",
             "topk 3; topk 4",
             "topk 5",
             "topk 6; topk 7"]),
    ("qb0", ["E dk; sel"]),
    ("qb1", ["E qb0; ss d 0"]),
    ("kvb0", ["E qb1"]),
    ("kvb1", ["E kvb0"]),
    ("dv", ["E kvb1; ss d 1",
             "nrm d 0; nrm d 1; rope d",
             "qkT d 0; qkT d 1; qkT d 2; qkT d 3; krcp; ss b 0",
             "ss b 1"]),
    ("ak", ["E dv; qk d 0; qk d 1; qk d 2; qk d 3",
             "exp d 0; exp d 1; exp d 2; nrm b 0",
             "norm d 0; norm d 1; norm d 2; exp d 3",
             "pT d 0; pT d 1; norm d 3; nrm b 1; rope b 0"]),
    ("aq", ["E ak; pv d 0; pv d 1; pT d 2; pT d 3; rope b 1",
             "pv d 2; pv d 3; qkT b 0; qkT b 1; qkT b 2; qkT b 3",
             "qkT b 4; qkT b 5",
             "qk b 0; qk b 1; qk b 2; qk b 3"]),
    ("av", ["E aq; exp b 0",
             "norm b 0; exp b 1; exp b 2; exp b 3; ss a 0",
             "pT b 0; norm b 1; norm b 2; norm b 3",
             "pv b 0; pT b 1; pT b 2; ss a 1"]),
    ("zk", ["E av; pv b 1; pv b 2; pT b 3; nrm a 0",
             "pv b 3; nrm a 1; rope a",
             "qkT a 0; qkT a 1; qkT a 2; qkT a 3",
             "qk a 0; qk a 1; qk a 2; qk a 3"]),
    ("zq", ["E zk; exp a 0",
             "exp a 1; exp a 2; exp a 3",
             "norm a 0; norm a 1",
             "pT a 0; pT a 1; qk a 4; qk a 5; qk a 6; qk a 7"]),
    ("zv", ["E zq; pv a 0; pv a 1; exp a 4",
             "exp a 5; exp a 6; qkT z 0",
             "norm a 2; exp a 7; qkT z 1; qkT z 2; qkT z 3",
             "pT a 2; norm a 3"]),
    ("wo0", ["E zv; pv a 2; pT a 3",
             "pv a 3; z 0",
             "oss; onrm; oT 0; oT 1; z 1",
             "z 2; z 3; zln; sp 0; R 0; zexp 0; pv z 0; sp 1; R 1; zexp 1; pv z 1; sp 2; R 2; zexp 2; pv z 2; sp 3; R 3; zexp 3; pv z 3"]),
    ("wo1", ["X wo 0; xsq wo 0",
             "",
             "",
             "fT 0"]),
    ("wo2", ["X wo 1; xsq wo 1",
             "fT 1",
             "",
             ""]),
    ("wo3", ["X wo 2; xsq wo 2",
             "fT 2",
             "",
             ""]),
]


def trunk_kernel(nc, x_in, attn_norm, w_in, diff_qk_norm, diff_lambda, diff_subln, mla_q_a_norm, mla_wq_b,
                 mla_kv_a_norm, mla_wkv_b, mla_qk_norm, dsa_qk_norm, idx_k_norm, w_o, ffn_norm, w_gate, w_up,
                 w_down, constants, out):
    F32, F32R, BF16 = mybir.dt.float32, mybir.dt.float32r, mybir.dt.bfloat16
    ALU, ACT, AX = mybir.AluOpType, mybir.ActivationFunctionType, mybir.AxisListType

    _, SEQ, D = x_in.shape
    DEPTH = w_in.shape[0]
    HIDDEN = w_gate.shape[2]
    P = 128
    TT = SEQ // P
    W = 512
    KD = D // P
    HD, HEADS, GW = 128, 4, 512
    SUB = HD // 2
    ROT = 64
    QD = HD + ROT
    QR, KR = mla_wq_b.shape[1], mla_wkv_b.shape[1]
    LK = QR // 4
    IH, ID = 16, 64
    TOPK = SEQ // 4
    EPS = 1e-6
    MASKED, TAKEN, LOWEST = -1e30, -3e38, -3.3e38
    assert TT == 2 and TOPK % 8 == 0 and QR == 4 * LK and KR == P

    A0, B0, C0, D0 = 0, 3 * GW, 3 * GW + QR + KR + ROT, 6 * GW + QR + KR + ROT
    I0 = D0 + 3 * GW
    COLUMNS = {"aq": A0, "ak": A0 + GW, "av": A0 + 2 * GW, "cq": B0, "ckr": B0 + QR,
               "zq": C0, "zk": C0 + GW, "zv": C0 + 2 * GW, "dq": D0, "dk": D0 + GW, "dv": D0 + 2 * GW,
               "iq0": I0, "iq1": I0 + W, "ikw": I0 + 2 * W}
    WIDTH = {"cq": QR, "ckr": KR + ROT, "ikw": ID + IH, "qb1": HEADS * QD - W}
    GROUP_ORDER = [3, 1, 0, 2]
    FIRST_TILE = {"a": 0, "b": 4, "z": 8, "d": 12}

    class Strip:
        def __init__(s, kind, name, arg=0, chunks=4):
            s.kind, s.name, s.arg = kind, name, arg
            s.width = WIDTH.get(name, W)
            s.rows = LK if name in ("qb0", "qb1") else P
            if kind == "kvb":
                s.halves = [([0], 0, W // 2), ([0], W // 2, W)]
            else:
                s.halves = [([2 * i, 2 * i + 1], 0, s.width) for i in range(2 * chunks)]

    class Position:
        def __init__(s, strip, chunk, steps):
            s.strip, s.chunk, s.steps = strip, chunk, steps

    def positions(strip, steps):
        return [Position(strip, c, steps.get(c, [])) for c in range(len(strip.halves) // 2)]

    head, tail_steps = [], []
    for name, rows in ATTENTION:
        if name[:2] == "wo":
            s = Strip("wo", name, int(name[2]))
        elif name[:2] == "qb":
            s = Strip("qb", name, int(name[2]), chunks=1)
        elif name[:3] == "kvb":
            s = Strip("kvb", name, int(name[3]))
        else:
            s = Strip("in", name)
        head += positions(s, {c: [tuple(x.split()) for x in r.split("; ") if x] for c, r in enumerate(rows)})
    PARTS = [4, 4, 3]
    assert sum(PARTS) * W == HIDDEN

    def pair_strips(part, pair):
        return Strip("gate", "gate", (part, pair)), Strip("up", "up", (part, pair))

    sections = []
    for part, pairs in enumerate(PARTS):
        gate, up = pair_strips(part, 0)
        before = {0: [("X", "wo", "3")], 1: [("fT", "3"), ("xsq", "wo", "3")], 2: [("xms", "f")]} if part == 0 else \
                 {0: [("X", f"down{part - 1}", "3")]}
        head += positions(gate, before) + positions(up, {0: [("G", "first")]})
        sections.append(("line", head))
        gate, up = pair_strips(part, 1)
        sections.append(("loop", pairs - 1,
                         positions(gate, {0: [("U", "before")], 1: [("hidT", "0", "before")], 2: [("hidT", "1", "before")]})
                         + positions(up, {0: [("G", "this")]})))
        head = []
        final = part == len(PARTS) - 1
        for s in range(4):
            strip = Strip("down", f"down{part}", (part, s), chunks=pairs)
            steps = {0: [("X", f"down{part}", str(s - 1))]} if s else \
                    {0: [("U", "last")], 1: [("hidT", "0", "last"), ("hidT", "1", "last")]}
            if s and final:
                steps[1] = [("xsq", f"down{part}", str(s - 1))]
            head += positions(strip, steps)
        if final:
            sections.append(("line", head))
            tail_steps = [("X", f"down{part}", "3"), ("xsq", f"down{part}", "3")]

    BANKS = {"hT": (2, 3), "fT": (2, 3), "iqT": (2,), "ikT": (3,), "qkT": (2,), "latT": (2,), "ckvT": (3,), "pT": (2,),
             "pv": (3,), "oT": (2,)}

    def banks(step):
        kind = step[0]
        if kind == "idx":
            return (0, 1)
        if kind in ("z", "R"):
            return (int(step[1]) % 2,)
        if kind == "qk":
            return (int(step[2]) % 2,)
        if kind == "hidT":
            return (2 + int(step[1]),)
        return BANKS.get(kind, ())

    HIGH = ("latT", "ckvT", "oT", "hidT")
    strips, use, high, ms_event = {}, {}, {}, {}
    n_half = n_strip = n_high = n_ms = 0
    n_use = [0] * 4
    pairs_seen = {}
    for section in sections:
        body = section[-1]
        turns = section[1] if section[0] == "loop" else 1
        start = (n_half, n_strip, n_high, list(n_use))
        for pos in body:
            if pos.chunk == 0:
                s = pos.strip
                s.first_half, s.parity, s.turn = n_half, n_strip % 2, n_strip // 2
                n_half += len(s.halves)
                s.last_half = n_half - 1
                n_strip += 1
                if s.kind in ("gate", "up"):
                    pairs_seen[s.kind, section[0] == "loop", s.arg[0]] = s
                else:
                    strips[s.name if s.kind != "down" else (s.name, s.arg[1])] = s
                if s.kind == "wo":
                    strips["wo", s.arg] = s
            for step in pos.steps:
                key = (step, section[0] == "loop", pos.strip.name if step[0] in ("hidT",) else "",
                       pos.strip.arg[0] if step[0] == "hidT" else 0)
                pos_key = key
                for b in banks(step):
                    use.setdefault(pos_key, {})[b] = n_use[b]
                    n_use[b] += 1
                if step[0] in ("hT", "fT"):
                    high[pos_key] = n_high
                    n_high += 2
                elif step[0] in HIGH or (step[0] == "pv" and step[1] != "a"):
                    high[pos_key] = n_high
                    n_high += 1
                if step[0] in ("xms", "ikss", "latss", "oss") or (step[0] == "ss" and step[2] == "1"):
                    ms_event[step] = n_ms
                    n_ms += 1
        if turns > 1:
            n_half += (turns - 1) * (n_half - start[0])
            n_strip += (turns - 1) * (n_strip - start[1])
            n_high += (turns - 1) * (n_high - start[2])
            for b in range(4):
                n_use[b] += (turns - 1) * (n_use[b] - start[3][b])
    HALVES, STRIPS, HIGHS, USES, MS = n_half, n_strip, n_high, n_use, n_ms
    assert HALVES % 4 == 0 and STRIPS % 2 == 0
    PAIR_HALVES = 16
    order = [step for section in sections for pos in section[-1] for step in pos.steps]

    def key_of(step, pos):
        loop = pos is not None and pos.strip.kind in ("gate", "up") and pos.strip.arg[1] == 1
        return (step, loop, pos.strip.name if step[0] == "hidT" else "", pos.strip.arg[0] if step[0] == "hidT" else 0)

    def last_of(names):
        by_parity = {}
        for s in sorted((strips[name] for name in names), key=lambda s: s.turn):
            by_parity[s.parity] = s
        return list(by_parity.values())

    def found(kind, *args):
        return ((kind, *args), False, "", 0)

    P_ORDER = [s for s in order if s[0] == "pT"]
    PV_ORDER = [s for s in order if s[0] == "pv"]
    QK_ORDER = [s for s in order if s[0] == "qk"]
    PROBS_ORDER = [s for s in order if s[0] in ("pT", "zexp")]

    def probs_slot(step):
        return PROBS_ORDER.index(step) % 2

    def pv_of(writer):
        return ("pv", "z", writer[1]) if writer[0] == "zexp" else ("pv", writer[1], writer[2])

    def writer_of(pv):
        return ("zexp", pv[2]) if pv[1] == "z" else ("pT", pv[1], pv[2])

    def slot_reader(qk):
        n, slot = order.index(qk), int(qk[2]) % 4
        for s in reversed(order[:n]):
            if s[0] == "pT" and (2 * int(s[2]) if s[1] == "a" else int(s[2])) % 4 == slot:
                return s
        return None

    MAP_DONE = [s for s in order if s[0] == "norm"]
    EXP_ORDER = [s for s in order if s[0] == "exp"]
    ROPE_ORDER = [s for s in order if s[0] in ("iqrope", "iknrm") or (s[0] == "rope" and s[1:] != ("b", "0"))]
    NRM_ORDER = [s for s in order if s[0] in ("iknrm", "onrm") or (s[0] == "nrm" and s[2] == "1")]
    SP_ORDER = [s for s in order if s[0] == "sp"]
    Z_ORDER = [s for s in order if s[0] == "R"]
    ZEXP_ORDER = [s for s in order if s[0] == "zexp"]

    ctx = ExitStack()
    with ctx:
        def sb(name, shape, dt=F32):
            return ctx.enter_context(nc.sbuf_tensor(name, shape, dt))

        def sem(name):
            return ctx.enter_context(nc.semaphore(name))

        raw = sb("raw", [P, 4, 2, W])
        w_hi, w_lo = sb("w_hi", [P, 4, 2, W], F32R), sb("w_lo", [P, 4, 2, W], F32R)
        x = sb("x", [P, TT, D])
        hT_hi, hT_lo = sb("hT_hi", [P, KD, SEQ], F32R), sb("hT_lo", [P, KD, SEQ], F32R)
        mT_hi, mT_lo = sb("mT_hi", [P, KD, SEQ], F32R), sb("mT_lo", [P, KD, SEQ], F32R)
        nat0 = sb("nat0", [P, TT, 1024])
        nat1 = sb("nat1", [P, TT, 1024])
        nat2 = sb("nat2", [P, TT, 1024])
        v_even, v_odd = sb("v_even", [P, TT, GW]), sb("v_odd", [P, TT, GW])
        T0, T1 = sb("T0", [P, 8, SEQ]), sb("T1", [P, 8, SEQ])
        Tr = sb("Tr", [P, 4, SEQ])
        SEG = [(0, P), (P, 3 * P)]
        E = sb("E", [P, 4, 3 * P])
        probs = sb("probs", [P, 2, 3 * P])
        picks, taken = (Tr[:, :, :].rearrange("p a b -> p (a b)")[:, i * 3 * P:(i + 1) * 3 * P] for i in (0, 1))
        ikT = sb("ikT", [P, SEQ])
        ikw = sb("ikw", [P, TT, ID + IH])
        ikd = sb("ikd", [P, TT, 2 * ID])
        iw = sb("iw", [P, TT, IH])
        best = sb("best", [P, TT, 8])
        junk = sb("junk", [P, 1024], BF16)
        rtmp = sb("rtmp", [P, 3, SEQ])
        stat = sb("stat", [P, 4, 4, TT])
        NG = 2 * KD + 5
        gain_rows = T1[:, 0, 0:P]
        gain_all = sb("gain_all", [P, DEPTH * NG])
        gain = sb("gain", [P, NG])
        small = sb("small", [P, 1216])
        cst = sb("cst", [P, constants.shape[1]])
        lam = sb("lam", [P, 8])
        lam_init = sb("lam_init", [P, 2])
        xsq = sb("xsq", [P, TT, 4])
        mean = sb("mean", [P, 96])
        rinv = sb("rinv", [P, 96])
        minus_half = sb("minus_half", [P, 32])
        PS = ctx.enter_context(nc.psum_tensor("PS", [P, 8, W], F32))

        R_X, R_IK, R_D, R_LAT, R_A, R_B, R_O, R_XF = 0, 2, 4, 20, 24, 56, 72, 80
        MS_COLS = {("xms", "a"): (R_X, 2), ("ikss",): (R_IK, 2), ("ss", "d", "1"): (R_D, 16), ("latss",): (R_LAT, 4),
                   ("ss", "a", "1"): (R_A, 32), ("ss", "b", "1"): (R_B, 16), ("oss",): (R_O, 8), ("xms", "f"): (R_XF, 2)}
        S_DIFF, S_SUBLN, S_MLA, S_DSA, S_IDX, S_LAM = 0, 128, 256, 640, 896, 960
        ident, bias_t = cst[:, 0:P], cst[:, P:3 * P]
        strict01, strict_neg, upper, ones = (cst[:, (3 + i) * P:(4 + i) * P] for i in range(4))
        ROPE_AT = {8: 7 * P, 16: 7 * P + 32, 32: 7 * P + 96}
        C_LAM = 7 * P + 224

        def cos_sin(half):
            a = ROPE_AT[half]
            return (cst[:, a + i * 2 * half:a + (i + 1) * 2 * half].rearrange("p (t h) -> p t h", t=TT) for i in (0, 1))

        raw_full = [sem(f"raw_full{i}") for i in range(4)]
        hi_done = sem("hi_done")
        lo_done = sem("lo_done")
        half_used = sem("half_used")
        strip_taken = [sem("strip_taken0"), sem("strip_taken1")]
        bank_full = [sem(f"bank_full{i}") for i in range(4)]
        bank_taken = [sem(f"bank_taken{i}") for i in range(4)]
        high_done = sem("high_done")
        consts_full, x_full, rows_full, small_full = sem("consts_full"), sem("x_full"), sem("rows_full"), sem("small_full")
        small_free = sem("small_free")
        init_done = sem("init_done")
        slot_seen = sem("slot_seen")
        gain_ready = sem("gain_ready")
        xsq_done = sem("xsq_done")
        ms_ready = sem("ms_ready")
        rinv_ready = sem("rinv_ready")
        nrm_done = sem("nrm_done")
        rope_done = sem("rope_done")
        relu_done = sem("relu_done")
        idx_added = sem("idx_added")
        max_done, exp_done, map_done = sem("max_done"), sem("exp_done"), sem("map_done")
        lam_sums, lam_exps = sem("lam_sums"), sem("lam_exps")
        ln_done, sp_done, z_done, zexp_done = sem("ln_done"), sem("sp_done"), sem("z_done"), sem("zexp_done")
        stored = sem("stored")

        block = ctx.enter_context(nc.Block())

        def f(ap):
            return ap.bitcast(F32)

        def w_bank(b, n=W):
            return PS[:, 4 + b, 0:n]

        def raw_source(strip, i, l, pair):
            kts, c0, c1 = strip.halves[i]
            k0, nk = kts[0], len(kts)
            if strip.kind == "in":
                c = COLUMNS[strip.name]
                src = w_in[l, k0 * P:(k0 + nk) * P, c + c0:c + c1]
            elif strip.kind == "qb":
                src = mla_wq_b[l, k0 * LK:(k0 + nk) * LK, strip.arg * W:strip.arg * W + strip.width]
            elif strip.kind == "kvb":
                src = mla_wkv_b[l, :, strip.arg * W + c0:strip.arg * W + c1]
            elif strip.kind == "wo":
                r = GROUP_ORDER[k0 // 4] * GW + (k0 % 4) * P
                src = w_o[l, r:r + nk * P, strip.arg * W:(strip.arg + 1) * W]
            elif strip.kind in ("gate", "up"):
                part, p = strip.arg
                w = w_gate if strip.kind == "gate" else w_up
                c = (sum(PARTS[:part]) + p) * W
                src = w[l, k0 * P:(k0 + nk) * P, c:c + W] if pair is None else \
                    w[l, k0 * P:(k0 + nk) * P, bass.ds(pair * W + c, W)]
            else:
                part, s = strip.arg
                r = sum(PARTS[:part]) * W + k0 * P
                src = w_down[l, r:r + nk * P, s * W:(s + 1) * W]
            return src.rearrange("(t p) n -> p t n", p=strip.rows)

        def walk(fori, line, after_loop=None):
            flat = [sec[-1] for sec in sections]
            for i, sec in enumerate(sections):
                body = sec[-1]
                nxt = flat[i + 1][0] if i + 1 < len(flat) else None
                if sec[0] == "line":
                    for j, pos in enumerate(body):
                        line(pos, body[j + 1] if j + 1 < len(body) else nxt, None)
                else:
                    with fori(0, sec[1]) as pair:
                        for j, pos in enumerate(body):
                            line(pos, body[j + 1] if j + 1 < len(body) else "again", pair)

        def halves_of(pos, first):
            return [(pos.strip, 2 * pos.chunk + i, pos.strip.first_half + 2 * pos.chunk + i) for i in (0, 1)]

        class Place:
            def __init__(s, l):
                s.l, s.pair = l, None

            def __call__(s, n, per_layer, per_pair=0):
                v = s.l * per_layer + n
                if s.pair is not None and per_pair:
                    v = v + s.pair * per_pair
                return v

            def half(s, n):
                return s(n, HALVES, PAIR_HALVES)

            def strip(s, n):
                return s(n, STRIPS, 2)

            def bank(s, b, n):
                return s(n, USES[b], 1)

            def high(s, n):
                return s(n, HIGHS, 2)

        def lead_halves(pos, nxt):
            if nxt is None:
                return [], 0
            if nxt == "again":
                base = pos.strip.first_half + len(pos.strip.halves)
                return [(pos.strip, i, base + i) for i in (0, 1)], 0
            return [(nxt.strip, 2 * nxt.chunk + i, nxt.strip.first_half + 2 * nxt.chunk + i) for i in (0, 1)], 0

        def split_view(strip, i, u):
            kts, c0, c1 = strip.halves[i]
            return slice(0, strip.rows), u % 4, slice(0, len(kts)), slice(0, c1 - c0)

        def pair_strip(kind, which, part):
            return pairs_seen[kind, False if which in ("first", "before") else True, part]

        @block.sync
        def _(sp):
            sp.dma_start(cst[:, :], constants).then_inc(consts_full, 16)
            for t in range(TT):
                sp.dma_start(x[:, t, :], x_in[0, t * P:(t + 1) * P, :]).then_inc(x_full, 16)
            sp.wait_ge(init_done, 1)
            for l in range(DEPTH):
                r = l * NG
                sp.dma_start(gain_rows[r:r + KD, :], attn_norm[l].rearrange("(k p) -> k p", p=P)).then_inc(rows_full, 16)
                sp.dma_start(gain_rows[r + KD:r + 2 * KD, :], ffn_norm[l].rearrange("(k p) -> k p", p=P)).then_inc(rows_full, 16)
                sp.dma_start(gain_rows[r + 2 * KD:r + 2 * KD + 4, 0:LK],
                             mla_q_a_norm[l].rearrange("(k p) -> k p", p=LK)).then_inc(rows_full, 16)
                sp.dma_start(gain_rows[r + 2 * KD + 4:r + 2 * KD + 5, :], mla_kv_a_norm[l:l + 1, :]).then_inc(rows_full, 16)
            with sp.Fori(0, DEPTH) as l:
                at = Place(l)
                sp.wait_ge(small_free, at(1, 1))
                for a, src in ((S_DIFF, diff_qk_norm), (S_MLA, mla_qk_norm), (S_DSA, dsa_qk_norm), (S_LAM, diff_lambda)):
                    n = src.shape[1] * src.shape[2]
                    rows = src[l].rearrange("(o a) b -> o (a b)", o=1).to_broadcast([P, n])
                    sp.dma_start(small[:, a:a + n], rows).then_inc(small_full, 16)
                for a, src in ((S_SUBLN, diff_subln), (S_IDX, idx_k_norm)):
                    n = src.shape[1]
                    rows = src[l].rearrange("(o a) -> o a", o=1).to_broadcast([P, n])
                    sp.dma_start(small[:, a:a + n], rows).then_inc(small_full, 16)

                def line(pos, nxt, pair):
                    at.pair = pair
                    for strip, i, u in halves_of(pos, None):
                        r, slot, k, c = split_view(strip, i, u)
                        sp.wait_ge(lo_done, at.half(u + 1))
                        if (strip.name, i) in (("aq", 0), ("wo0", 4)):
                            sp.sem_inc(slot_seen, 1)
                        sp.dma_start(raw[r, slot, k, c], raw_source(strip, i, l, pair)).then_inc(raw_full[slot], 16)
                    at.pair = None

                walk(sp.Fori, line)
            for s in range(4):
                strip = strips[f"down{len(PARTS) - 1}", s]
                sp.wait_ge(strip_taken[strip.parity], (DEPTH - 1) * STRIPS + 2 * strip.turn + 10)
                sp.dma_start(out[0, :, s * W:(s + 1) * W].rearrange("(t p) n -> p t n", p=P),
                             x[:, :, s * W:(s + 1) * W]).then_inc(stored, 16)
            sp.wait_ge(stored, 64)

        @block.tensor
        def _(pe):
            pe.wait_ge(consts_full, 16)
            pe.wait_ge(rows_full, 64 * DEPTH)
            pe.transpose(w_bank(0, DEPTH * NG), gain_rows[0:DEPTH * NG, :], cst[0:DEPTH * NG, 0:DEPTH * NG]).then_inc(init_done, 1)
            pe.wait_ge(x_full, 16 * TT)
            with pe.Fori(0, DEPTH) as l:
                at = Place(l)

                def begin(b, key):
                    pe.wait_ge(bank_taken[b], at.bank(b, use[key][b] + 1))

                def turn(bank, tiles, source, rows=P):
                    for j, tile in enumerate(tiles):
                        for t in range(TT):
                            o = j * SEQ + t * P
                            last = pe.transpose(PS[0:rows, 4 + bank, o:o + P], source(tile, t), ident)
                    return last

                def step(s, pos, key):
                    kind = s[0]
                    if kind in ("hT", "fT"):
                        q = int(s[1])
                        if kind == "hT":
                            d = strips[f"down{len(PARTS) - 1}", q]
                            pe.wait_ge(strip_taken[d.parity], at(2 * d.turn + 10 - STRIPS, STRIPS))
                        else:
                            d = strips["wo", q]
                            pe.wait_ge(strip_taken[d.parity], at(2 * d.turn + 10, STRIPS))
                        for i, b in enumerate((2, 3)):
                            begin(b, key)
                            turn(b, (4 * q + 2 * i, 4 * q + 2 * i + 1),
                                 lambda k, t: x[:, t, k * P:(k + 1) * P]).then_inc(bank_full[b], 1)
                    elif kind == "iqT":
                        pe.wait_ge(rope_done, at(ROPE_ORDER.index(("iqrope",)) + 1, len(ROPE_ORDER)))
                        begin(2, key)
                        i = int(s[1])
                        turn(2, (2 * i, 2 * i + 1), lambda k, t: nat0[:, t, k * P:(k + 1) * P]).then_inc(bank_full[2], 1)
                    elif kind == "ikT":
                        pe.wait_ge(rope_done, at(ROPE_ORDER.index(("iknrm",)) + 1, len(ROPE_ORDER)))
                        begin(3, key)
                        turn(3, (0,), lambda k, t: ikd[:, t, :]).then_inc(bank_full[3], 1)
                    elif kind == "idx":
                        for e in (0, 1):
                            rows = slice(e * ID, (e + 1) * ID)
                            if s[1] == "0" and e == 0:
                                pe.wait_ge(bank_taken[3], at.bank(3, use[found("ikT")][3] + 2))
                                pe.wait_ge(bank_taken[2], at.bank(2, use[found("iqT", "3")][2] + 2))
                            begin(e, key)
                            for t in range(TT):
                                a, z = SEG[t]
                                last = pe.matmul(PS[:, 4 + e, a:z], T0[rows, int(s[1]), t * P:(t + 1) * P],
                                                 ikT[rows, 0:z - a], start=True, stop=True)
                            last.then_inc(bank_full[e], 1)
                    elif kind == "qkT":
                        g, i = s[1], int(s[2])
                        if g == "z":
                            for st in last_of(("zq", "zk")):
                                pe.wait_ge(strip_taken[st.parity], at(2 * st.turn + 10, STRIPS))
                        else:
                            last_rope = ("rope", "b", "1") if g == "b" else ("rope", g)
                            pe.wait_ge(rope_done, at(ROPE_ORDER.index(last_rope) + 1, len(ROPE_ORDER)))
                        begin(2, key)
                        if g == "b":
                            nat = (nat0, nat0, nat2, nat2, nat0, nat2)[i]
                            src = (lambda k, t: nat[:, t, (k % 4) * QD:(k % 4) * QD + HD]) if i < 4 else \
                                (lambda k, t: nat[:, t, HEADS * QD + (k % 2) * P:HEADS * QD + (k % 2 + 1) * P])
                        else:
                            nat = nat0 if g == "z" else nat1
                            src = lambda k, t: nat[:, t, k * P:(k + 1) * P]
                        turn(2, (2 * i, 2 * i + 1), src).then_inc(bank_full[2], 1)
                    elif kind == "latT":
                        i = int(s[1])
                        st = strips["cq"]
                        pe.wait_ge(strip_taken[st.parity], at(2 * st.turn + 10, STRIPS))
                        begin(2, key)
                        turn(2, (2 * i, 2 * i + 1), lambda k, t: nat0[:, t, k * LK:(k + 1) * LK], rows=LK).then_inc(bank_full[2], 1)
                    elif kind == "ckvT":
                        st = strips["ckr"]
                        pe.wait_ge(strip_taken[st.parity], at(2 * st.turn + 10, STRIPS))
                        begin(3, key)
                        turn(3, (0,), lambda k, t: nat2[:, t, 832:832 + KR]).then_inc(bank_full[3], 1)
                    elif kind == "qk":
                        g, m = s[1], int(s[2])
                        b = m % 2
                        if m == 0:
                            i = 5 if g == "b" else 3
                            pe.wait_ge(bank_taken[2], at.bank(2, use[found("qkT", g, str(i))][2] + 2))
                        begin(b, key)
                        for t in range(TT):
                            a, z = SEG[t]
                            o, q = PS[:, 4 + b, a:z], slice(t * P, (t + 1) * P)
                            if g == "d":
                                last = pe.matmul(o, T1[:, m, q], T1[:, HEADS + m, 0:z - a], start=True, stop=True)
                            elif g == "a":
                                rows = slice((m % 2) * SUB, (m % 2 + 1) * SUB)
                                last = pe.matmul(o, T1[rows, m // 2, q], T1[rows, HEADS + m // 2, 0:z - a], start=True, stop=True)
                            else:
                                rows = slice((m % 2) * ROT, (m % 2 + 1) * ROT)
                                pe.matmul(o, T0[:, m, q], T0[:, HEADS + m, 0:z - a], start=True, stop=False)
                                last = pe.matmul(o, Tr[rows, m // 2, q], Tr[rows, 2 + m // 2, 0:z - a], start=False, stop=True)
                        last.then_inc(bank_full[b], 1)
                    elif kind == "pT":
                        g, h = s[1], int(s[2])
                        slot = (2 * h if g == "a" else h) % 4
                        pe.wait_ge(map_done, at(MAP_DONE.index(("norm", g, s[2])) + 1, len(MAP_DONE)))
                        begin(2, key)
                        for i in range(3):
                            last = pe.transpose(PS[:, 6, i * P:(i + 1) * P], E[:, slot, i * P:(i + 1) * P], ident)
                        last.then_inc(bank_full[2], 1)
                    elif kind == "pv":
                        g, h = s[1], int(s[2])
                        v = v_even if g in ("d", "a") else v_odd
                        for st in last_of({"d": ("dv",), "a": ("av",), "z": ("zv",), "b": ("kvb0", "kvb1")}[g]):
                            pe.wait_ge(strip_taken[st.parity], at(2 * st.turn + 10, STRIPS))
                        w = writer_of(s)
                        if g == "z":
                            pe.wait_ge(zexp_done, at(ZEXP_ORDER.index(w) + 1, len(ZEXP_ORDER)))
                        else:
                            pe.wait_ge(bank_taken[2], at.bank(2, use[found(*w)][2] + 2))
                        begin(3, key)
                        pr, cols = probs[:, probs_slot(w), :], slice(h * HD, (h + 1) * HD)
                        if g == "a":
                            pe.matmul(PS[:, 7, 0:P], pr[:, 0:P], v[:, 0, cols], start=True, stop=True)
                            pe.matmul(PS[:, 7, P:2 * P], pr[:, P:2 * P], v[:, 0, cols], start=True, stop=False)
                            last = pe.matmul(PS[:, 7, P:2 * P], pr[:, 2 * P:3 * P], v[:, 1, cols], start=False, stop=True)
                        else:
                            pe.matmul(PS[:, 7, 0:SEQ], v[:, 0, cols], pr[:, 0:SEQ], start=True, stop=False)
                            last = pe.matmul(PS[:, 7, P:SEQ], v[:, 1, cols], pr[:, SEQ:3 * P], start=False, stop=True)
                        last.then_inc(bank_full[3], 1)
                    elif kind == "oT":
                        i = int(s[1])
                        pe.wait_ge(nrm_done, at(NRM_ORDER.index(("onrm",)) + 1, len(NRM_ORDER)))
                        begin(2, key)
                        turn(2, (2 * i, 2 * i + 1), lambda k, t: nat1[:, t, k * P:(k + 1) * P]).then_inc(bank_full[2], 1)
                    elif kind == "z":
                        h = int(s[1])
                        b = h % 2
                        if h == 0:
                            pe.wait_ge(bank_taken[2], at.bank(2, use[found("qkT", "z", "3")][2] + 2))
                        begin(b, key)
                        pe.matmul(PS[:, 4 + b, 0:SEQ], T0[:, HEADS + h, 0:P], T0[:, h, :], start=True, stop=True)
                        pe.matmul(PS[:, 4 + b, SEQ:3 * P], T0[:, HEADS + h, P:SEQ], T0[:, h, P:SEQ],
                                  start=True, stop=True).then_inc(bank_full[b], 1)
                    elif kind == "R":
                        h = int(s[1])
                        b = h % 2
                        pe.wait_ge(sp_done, at(SP_ORDER.index(("sp", s[1])) + 1, len(SP_ORDER)))
                        begin(b, key)
                        pe.matmul(PS[:, 4 + b, 0:3 * P], upper, E[:, h, :], start=True, stop=False)
                        pe.matmul(PS[:, 4 + b, P:SEQ], ones, E[:, h, SEQ:3 * P], start=False, stop=True).then_inc(bank_full[b], 1)
                    elif kind == "hidT":
                        i = int(s[1])
                        up = pair_strip("up", s[2], pos.strip.arg[0])
                        turns = PARTS[up.arg[0]] - 2 if s[2] == "last" else 0
                        pe.wait_ge(strip_taken[1], at.strip(2 * (up.turn + turns) + 10))
                        begin(2 + i, key)
                        turn(2 + i, (2 * i, 2 * i + 1), lambda k, t: nat1[:, t, k * P:(k + 1) * P]).then_inc(bank_full[2 + i], 1)

                def operand(strip, kt):
                    if strip.kind in ("in", "gate", "up"):
                        return hT_hi[:, kt, :], hT_lo[:, kt, :]
                    if strip.kind == "qb":
                        return mT_hi[0:LK, 4 + kt, :], mT_lo[0:LK, 4 + kt, :]
                    if strip.kind == "kvb":
                        return mT_hi[:, 8, :], mT_lo[:, 8, :]
                    if strip.kind == "wo":
                        kt = 4 * GROUP_ORDER[kt // 4] + kt % 4
                    return mT_hi[:, kt, :], mT_lo[:, kt, :]

                def operand_wait(pos):
                    strip, c = pos.strip, pos.chunk
                    if strip is sections[0][1][0].strip:
                        k = found("hT", str(c))
                        pe.wait_ge(bank_taken[2], at.bank(2, use[k][2] + 2))
                        pe.wait_ge(bank_taken[3], at.bank(3, use[k][3] + 2))
                    elif strip.kind == "gate" and strip.arg == (0, 0):
                        k = found("fT", str(c))
                        pe.wait_ge(bank_taken[2], at.bank(2, use[k][2] + 2))
                        pe.wait_ge(bank_taken[3], at.bank(3, use[k][3] + 2))
                    elif strip.kind == "qb":
                        pe.wait_ge(bank_taken[2], at.bank(2, use[found("latT", "1")][2] + 2))
                    elif strip.kind == "kvb":
                        pe.wait_ge(bank_taken[3], at.bank(3, use[found("ckvT")][3] + 2))
                    elif strip.kind == "wo" and strip.arg == 0:
                        g = {3: "d", 1: "b", 0: "a", 2: "z"}[GROUP_ORDER[c]]
                        if g == "a":
                            pe.wait_ge(bank_taken[2], at.bank(2, use[found("oT", "1")][2] + 2))
                        else:
                            pe.wait_ge(bank_taken[3], at.bank(3, use[found("pv", g, "3")][3] + 2))
                    elif strip.kind == "down" and strip.arg[1] == 0 and c == len(strip.halves) // 2 - 1:
                        for i in (0, 1):
                            k = (("hidT", str(i), "last"), False, strip.name, strip.arg[0])
                            pe.wait_ge(bank_taken[2 + i], at.bank(2 + i, use[k][2 + i] + 2))

                def line(pos, nxt, pair):
                    at.pair = pair
                    for s in pos.steps:
                        step(s, pos, key_of(s, pos))
                    strip = pos.strip
                    if pos.chunk == 0:
                        pe.wait_ge(strip_taken[strip.parity], at.strip(2 * strip.turn + 8))
                    operand_wait(pos)
                    n = len(strip.halves)
                    for st, i, u in halves_of(pos, None):
                        r, slot, _, _ = split_view(strip, i, u)
                        kts, c0, c1 = strip.halves[i]
                        pe.wait_ge(lo_done, at.half(u + 5))
                        for j, kt in enumerate(kts):
                            hi, lo = operand(strip, kt)
                            w1, w2 = w_hi[r, slot, j, 0:c1 - c0], w_lo[r, slot, j, 0:c1 - c0]
                            first = (i == 0 and j == 0) or strip.kind == "kvb"
                            final = (i == n - 1 and j == len(kts) - 1) or strip.kind == "kvb"
                            for t in range(TT):
                                o, q = PS[:, 2 * strip.parity + t, c0:c1], slice(t * P, (t + 1) * P)
                                pe.matmul(o, hi[:, q], w1, start=first, stop=False)
                                pe.matmul(o, hi[:, q], w2, start=False, stop=False)
                                last = pe.matmul(o, lo[:, q], w1, start=False, stop=final)
                        last.then_inc(half_used, 1)
                    at.pair = None

                walk(pe.Fori, line)

        @block.scalar
        def _(act):
            def square(s):
                for t in range(TT):
                    last = act.activation(nat0[:, t, 0:W], x[:, t, s * W:(s + 1) * W], ACT.Square, accum_out=xsq[:, t, s:s + 1])
                last.then_inc(xsq_done, 1)

            act.wait_ge(x_full, 16 * TT)
            for s in range(4):
                square(s)
                act.drain()
            with act.Fori(0, DEPTH) as l:
                at = Place(l)

                def split(strip, i, u):
                    r, slot, k, c = split_view(strip, i, u)
                    act.wait_ge(raw_full[slot], at(16 * (u // 4 + 1), 4 * HALVES, 4 * PAIR_HALVES))
                    act.wait_ge(half_used, at.half(u + 1))
                    act.activation(w_hi[r, slot, k, c], raw[r, slot, k, c], ACT.Copy).then_inc(hi_done, 1)

                def full(b, key):
                    act.wait_ge(bank_full[b], at.bank(b, use[key][b] + 1))

                def step(s, pos, key):
                    kind = s[0]
                    if kind == "E":
                        st = strips[s[1]]
                        act.wait_ge(half_used, at.half(st.last_half + 5))
                        ev = ("latss",) if st.kind in ("qb", "kvb") else ("xms", "a")
                        act.wait_ge(rinv_ready, at(ms_event[ev] + 1, MS))
                        for t in range(TT):
                            src = PS[:, 2 * st.parity + t, 0:st.width]
                            col = R_X + t if st.kind == "in" else R_LAT + t + (2 if st.kind == "kvb" else 0)
                            r = rinv[:, col:col + 1]
                            if st.kind == "kvb":
                                heads = src.rearrange("p (h c) -> p h c", h=2)
                                k = nat2[:, t, 0:HEADS * QD].rearrange("p (h c) -> p h c", h=HEADS)
                                v = v_odd[:, t, :].rearrange("p (h c) -> p h c", h=HEADS)
                                hs = slice(2 * st.arg, 2 * st.arg + 2)
                                act.activation(k[:, hs, 0:HD], heads[:, :, 0:HD], ACT.Copy, scale=r)
                                last = act.activation(v[:, hs, :], heads[:, :, HD:2 * HD], ACT.Copy, scale=r)
                            else:
                                dst = {"iq0": nat0[:, t, 0:W], "iq1": nat0[:, t, W:2 * W], "ikw": ikw[:, t, :],
                                       "dq": nat1[:, t, 0:W], "dk": nat1[:, t, W:2 * W], "dv": v_even[:, t, :],
                                       "cq": nat0[:, t, 0:QR], "ckr": nat2[:, t, 832:832 + KR + ROT],
                                       "aq": nat1[:, t, 0:W], "ak": nat1[:, t, W:2 * W], "av": v_even[:, t, :],
                                       "qb0": nat0[:, t, 0:W], "qb1": nat0[:, t, W:HEADS * QD],
                                       "zq": nat0[:, t, 0:W], "zk": nat0[:, t, W:2 * W], "zv": v_odd[:, t, :]}[st.name]
                                last = act.activation(dst, src, ACT.Copy, scale=r)
                            last.then_inc(strip_taken[st.parity], 1)
                    elif kind in ("hT", "fT"):
                        q = int(s[1])
                        if kind == "hT" and q == 0:
                            act.wait_ge(gain_ready, at(1, 1))
                        for i, b in enumerate((2, 3)):
                            full(b, key)
                            for j in (0, 1):
                                k = 4 * q + 2 * i + j
                                g = k + (KD if kind == "fT" else 0)
                                last = act.activation(hT_hi[:, k, :], PS[:, 4 + b, j * SEQ:(j + 1) * SEQ], ACT.Copy,
                                                      scale=gain[:, g:g + 1])
                            last.then_inc(high_done, 1)
                    elif kind == "latT":
                        full(2, key)
                        for j in (0, 1):
                            k = 2 * int(s[1]) + j
                            last = act.activation(mT_hi[0:LK, 4 + k, :], PS[0:LK, 6, j * SEQ:(j + 1) * SEQ], ACT.Copy,
                                                  scale=gain[0:LK, 2 * KD + k:2 * KD + k + 1])
                        last.then_inc(high_done, 1)
                    elif kind == "ckvT":
                        full(3, key)
                        act.activation(mT_hi[:, 8, :], w_bank(3, SEQ), ACT.Copy,
                                       scale=gain[:, 2 * KD + 4:2 * KD + 5]).then_inc(high_done, 1)
                    elif kind in ("iqT", "qkT"):
                        full(2, key)
                        if kind == "iqT":
                            dst = T0[:, 2 * int(s[1]):2 * int(s[1]) + 2, :]
                        else:
                            g, i = s[1], int(s[2])
                            dst = Tr[:, 2 * (i - 4):2 * (i - 4) + 2, :] if i >= 4 else \
                                (T1 if g in ("d", "a") else T0)[:, 2 * i:2 * i + 2, :]
                        act.activation(dst, w_bank(2).rearrange("p (j n) -> p j n", j=2), ACT.Copy).then_inc(bank_taken[2], 1)
                    elif kind == "ikT":
                        full(3, key)
                        act.activation(ikT[:, :], w_bank(3, SEQ), ACT.Copy).then_inc(bank_taken[3], 1)
                    elif kind == "idx":
                        for e in (0, 1):
                            head = 2 * int(s[1]) + e
                            full(e, key)
                            act.wait_ge(idx_added, at(head + 1, IH))
                            act.activation(E[:, 2 + e, :], w_bank(e, 3 * P), ACT.Relu).then_inc(relu_done, 1)
                    elif kind == "lam":
                        if s[1] == "1":
                            act.wait_ge(lam_sums, at(1, 1))
                            act.activation(lam[:, 2:4], lam[:, 0:2], ACT.Exp).then_inc(lam_exps, 1)
                    elif kind == "exp":
                        g, m = s[1], int(s[2])
                        slot = m % 4
                        scale = {"d": HD, "a": SUB, "b": QD}[g] ** -0.5
                        act.wait_ge(max_done, at(QK_ORDER.index(("qk", g, s[2])) + 1, len(QK_ORDER)))
                        for t in range(TT):
                            a, z = SEG[t]
                            last = act.activation(E[:, slot, a:z], E[:, slot, a:z], ACT.Exp, bias=stat[:, slot, 1, t:t + 1],
                                                  scale=scale, accum_out=stat[:, slot, 2, t:t + 1])
                        last.then_inc(exp_done, 1)
                    elif kind == "pT":
                        full(2, key)
                        n = PROBS_ORDER.index(s)
                        if n >= 2:
                            act.wait_ge(bank_full[3], at.bank(3, use[found(*pv_of(PROBS_ORDER[n - 2]))][3] + 1))
                        act.activation(probs[:, n % 2, :], w_bank(2, 3 * P), ACT.Copy).then_inc(bank_taken[2], 1)
                    elif kind == "pv":
                        g, h = s[1], int(s[2])
                        full(3, key)
                        if g == "a":
                            act.activation(nat1[:, :, h * HD:(h + 1) * HD], w_bank(3, SEQ).rearrange("p (t d) -> p t d", t=TT),
                                           ACT.Copy).then_inc(bank_taken[3], 1)
                        else:
                            act.activation(mT_hi[:, FIRST_TILE[g] + h, :], w_bank(3, SEQ), ACT.Copy).then_inc(high_done, 1)
                    elif kind == "oT":
                        full(2, key)
                        i = int(s[1])
                        act.activation(mT_hi[:, 2 * i:2 * i + 2, :], w_bank(2).rearrange("p (j n) -> p j n", j=2),
                                       ACT.Copy).then_inc(high_done, 1)
                    elif kind == "z":
                        h = int(s[1])
                        b = h % 2
                        full(b, key)
                        logits = nat2[:, :, :].rearrange("p t n -> p (t n)")[:, h * 3 * P:(h + 1) * 3 * P]
                        act.activation(logits, w_bank(b, 3 * P), ACT.Copy, scale=HD ** -0.5)
                        act.activation(E[:, h, :], w_bank(b, 3 * P), ACT.Abs, scale=HD ** -0.5).then_inc(bank_taken[b], 1)
                        act.drain()
                        act.activation(E[:, h, :], E[:, h, :], ACT.Exp, scale=-1.0)
                    elif kind == "zln":
                        act.drain()
                        act.activation(E[:, :, :], E[:, :, :], ACT.Ln, bias=1.0).then_inc(ln_done, 1)
                    elif kind == "zexp":
                        h = int(s[1])
                        n = PROBS_ORDER.index(s)
                        logits = nat2[:, :, :].rearrange("p t n -> p (t n)")[:, h * 3 * P:(h + 1) * 3 * P]
                        act.wait_ge(z_done, at(Z_ORDER.index(("R", s[1])) + 1, len(Z_ORDER)))
                        if n >= 2:
                            act.wait_ge(bank_full[3], at.bank(3, use[found(*pv_of(PROBS_ORDER[n - 2]))][3] + 1))
                        act.activation(probs[:, n % 2, :], logits, ACT.Exp).then_inc(zexp_done, 1)
                    elif kind == "xsq":
                        d = strips[s[1], int(s[2])]
                        act.drain()
                        act.wait_ge(strip_taken[d.parity], at(2 * d.turn + 10, STRIPS))
                        square(int(s[2]))
                    elif kind == "G":
                        gate = pair_strip("gate", s[1], pos.strip.arg[0])
                        act.wait_ge(half_used, at.half(gate.last_half + 5))
                        act.wait_ge(rinv_ready, at(ms_event["xms", "f"] + 1, MS))
                        for t in range(TT):
                            act.activation(nat0[:, t, 0:W], PS[:, 2 * gate.parity + t, :], ACT.Silu,
                                           scale=rinv[:, R_XF + t:R_XF + t + 1]).then_inc(strip_taken[gate.parity], 1)
                    elif kind == "hidT":
                        i = int(s[1])
                        b = 2 + i
                        full(b, key)
                        part = pos.strip.arg[0]
                        if s[2] == "last":
                            k = 4 * (PARTS[part] - 1) + 2 * i
                            dst = mT_hi[:, k:k + 2, :]
                        else:
                            dst = mT_hi[:, bass.ds(at.pair * 4 + 2 * i, 2), :]
                        act.activation(dst, w_bank(b).rearrange("p (j n) -> p j n", j=2), ACT.Copy).then_inc(high_done, 1)

                def line(pos, nxt, pair):
                    at.pair = pair
                    early = pos is sections[0][1][0]
                    if early:
                        for half in halves_of(pos, None):
                            split(*half)
                        for s in pos.steps:
                            step(s, pos, key_of(s, pos))
                    for half in lead_halves(pos, nxt)[0]:
                        split(*half)
                    if not early:
                        for s in pos.steps:
                            step(s, pos, key_of(s, pos))
                    at.pair = None

                walk(act.Fori, line)
                for s in tail_steps:
                    step(s, None, None)

        @block.vector
        def _(dve):
            dve.sem_inc(lo_done, 4)
            dve.sem_inc(half_used, 4)
            for p in (0, 1):
                dve.sem_inc(strip_taken[p], 8)
            dve.sem_inc(small_free, 1)
            dve.sem_inc(idx_added, 2)
            dve.wait_ge(init_done, 2)
            dve.tensor_copy(gain_all[:, :], w_bank(0, DEPTH * NG))
            dve.drain()
            for b in range(4):
                dve.sem_inc(bank_taken[b], 1)
            dve.wait_ge(consts_full, 16)
            with dve.Fori(0, DEPTH) as l:
                at = Place(l)
                dve.drain()
                dve.tensor_copy(gain[:, :], gain_all[:, bass.ds(l * NG, NG)]).then_inc(gain_ready, 1)
                dve.tensor_copy(lam_init[:, :], cst[:, bass.ds(l * 2 + C_LAM, 2)])
                dve.drain()

                def split(strip, i, u):
                    r, slot, k, c = split_view(strip, i, u)
                    dve.wait_ge(hi_done, at.half(u + 1))
                    dve.tensor_tensor(w_lo[r, slot, k, c], raw[r, slot, k, c], f(w_hi[r, slot, k, c]),
                                      ALU.subtract).then_inc(lo_done, 1)

                def high_ready(key, i=0):
                    dve.wait_ge(high_done, at.high(high[key] + i + 1))

                def squares(src, n, width, col, width0=0):
                    for h in range(n):
                        v = src[:, h * width:(h + 1) * width]
                        dve.tensor_tensor_reduce(out=junk[:, h * width:(h + 1) * width], in0=v, in1=v, scale=1.0, scalar=0.0,
                                                 op0=ALU.mult, op1=ALU.add, accum_out=mean[:, col + h:col + h + 1])

                def to_mean(step, width):
                    col, n = MS_COLS[step]
                    dve.drain()
                    m = mean[:, col:col + n]
                    return dve.tensor_scalar(m, m, 1.0 / width, EPS, ALU.mult, ALU.add)

                def roots(step):
                    dve.wait_ge(rinv_ready, at(ms_event[step] + 1, MS))

                def scale_heads(src, n, width, col, g, goff):
                    for h in range(n):
                        v = src[:, h * width:(h + 1) * width]
                        last = dve.scalar_tensor_tensor(v, v, rinv[:, col + h:col + h + 1], g[:, goff:goff + width], ALU.mult, ALU.mult)
                    return last

                def step(s, pos, key):
                    kind = s[0]
                    if kind in ("hT", "fT"):
                        q = int(s[1])
                        for i, b in enumerate((2, 3)):
                            high_ready(key, i)
                            for j in (0, 1):
                                k = 4 * q + 2 * i + j
                                g = k + (KD if kind == "fT" else 0)
                                last = dve.scalar_tensor_tensor(hT_lo[:, k, :], PS[:, 4 + b, j * SEQ:(j + 1) * SEQ], gain[:, g:g + 1],
                                                                f(hT_hi[:, k, :]), ALU.mult, ALU.subtract)
                            last.then_inc(bank_taken[b], 1)
                    elif kind == "latT":
                        high_ready(key)
                        for j in (0, 1):
                            k = 2 * int(s[1]) + j
                            last = dve.scalar_tensor_tensor(mT_lo[0:LK, 4 + k, :], PS[0:LK, 6, j * SEQ:(j + 1) * SEQ],
                                                            gain[0:LK, 2 * KD + k:2 * KD + k + 1], f(mT_hi[0:LK, 4 + k, :]),
                                                            ALU.mult, ALU.subtract)
                        last.then_inc(bank_taken[2], 1)
                    elif kind == "ckvT":
                        high_ready(key)
                        dve.scalar_tensor_tensor(mT_lo[:, 8, :], w_bank(3, SEQ), gain[:, 2 * KD + 4:2 * KD + 5], f(mT_hi[:, 8, :]),
                                                 ALU.mult, ALU.subtract).then_inc(bank_taken[3], 1)
                    elif kind == "xms":
                        fours = {"a": 1, "f": 2}[s[1]]
                        col = MS_COLS[s][0]
                        dve.wait_ge(xsq_done, at(4 * fours, 8))
                        dve.tensor_reduce(mean[:, col:col + TT], xsq[:, :, :], AX.X, ALU.add)
                        to_mean(s, D).then_inc(ms_ready, 1)
                    elif kind == "lam":
                        if s[1] == "0":
                            dve.wait_ge(small_full, at(96, 96))
                            for i in (0, 1):
                                a = S_LAM + 2 * i * SUB
                                dve.tensor_tensor_reduce(out=junk[:, i * SUB:(i + 1) * SUB], in0=small[:, a:a + SUB],
                                                         in1=small[:, a + SUB:a + 2 * SUB], scale=1.0, scalar=0.0,
                                                         op0=ALU.mult, op1=ALU.add, accum_out=lam[:, i:i + 1])
                            dve.drain()
                            sub = small[:, S_SUBLN:S_SUBLN + HD]
                            dve.tensor_scalar(sub, sub, lam_init[:, 1:2], None, ALU.mult).then_inc(lam_sums, 1)
                        elif s[1] == "2":
                            dve.wait_ge(lam_exps, at(1, 1))
                            dve.tensor_tensor(lam[:, 5:6], lam[:, 3:4], lam[:, 2:3], ALU.subtract)
                            dve.drain()
                            dve.tensor_tensor(lam[:, 4:5], lam[:, 5:6], lam_init[:, 0:1], ALU.subtract)
                            dve.drain()
                    elif kind == "ikss":
                        dve.drain()
                        st = strips["ikw"]
                        dve.wait_ge(strip_taken[st.parity], at(2 * st.turn + 10, STRIPS))
                        for t in range(TT):
                            v = ikw[:, t, 0:ID]
                            dve.tensor_tensor_reduce(out=junk[:, t * ID:(t + 1) * ID], in0=v, in1=v, scale=1.0, scalar=0.0,
                                                     op0=ALU.mult, op1=ALU.add, accum_out=mean[:, R_IK + t:R_IK + t + 1])
                        to_mean(s, ID).then_inc(ms_ready, 1)
                    elif kind == "iknrm":
                        roots(("ikss",))
                        for t in range(TT):
                            dve.scalar_tensor_tensor(ikd[:, t, 0:ID], ikw[:, t, 0:ID], rinv[:, R_IK + t:R_IK + t + 1],
                                                     small[:, S_IDX:S_IDX + ID], ALU.mult, ALU.mult)
                        dve.tensor_scalar(iw[:, :, :], ikw[:, :, ID:ID + IH], ID ** -0.5 * IH ** -0.5, None, ALU.mult).then_inc(nrm_done, 1)
                    elif kind == "idx":
                        dve.drain()
                        for e in (0, 1):
                            head = 2 * int(s[1]) + e
                            acc = (picks, taken)[e]
                            dve.wait_ge(relu_done, at(head + 1, IH))
                            for t in range(TT):
                                a, z = SEG[t]
                                r, w = E[:, 2 + e, a:z], iw[:, t, head:head + 1]
                                if s[1] == "0":
                                    last = dve.tensor_scalar(acc[:, a:z], r, w, None, ALU.mult)
                                else:
                                    last = dve.scalar_tensor_tensor(acc[:, a:z], r, w, acc[:, a:z], ALU.mult, ALU.add)
                            last.then_inc(idx_added, 1)
                            dve.sem_inc(bank_taken[e], 1)
                    elif kind == "topk":
                        if s[1] == "0":
                            dve.drain()
                            dve.tensor_tensor(taken[:, :], taken[:, :], picks[:, :], ALU.add)
                            dve.drain()
                            dve.tensor_tensor(taken[:, 0:P], taken[:, 0:P], bias_t[:, P:2 * P], ALU.add)
                            dve.tensor_tensor(taken[:, P:3 * P], taken[:, P:3 * P], bias_t, ALU.add)
                        dve.drain()
                        for t in range(TT):
                            a, z = SEG[t]
                            dve.max(best[:, t, :], taken[:, a:z])
                        dve.drain()
                        for t in range(TT):
                            a, z = SEG[t]
                            dve.match_replace(taken[:, a:z], best[:, t, :], taken[:, a:z], TAKEN)
                    elif kind == "sel":
                        dve.drain()
                        dve.tensor_scalar(picks[:, :], taken[:, :], TAKEN / 2, MASKED, ALU.is_gt, ALU.mult)
                        dve.drain()
                        dve.tensor_tensor(picks[:, 0:P], picks[:, 0:P], bias_t[:, P:2 * P], ALU.add)
                        dve.tensor_tensor(picks[:, P:3 * P], picks[:, P:3 * P], bias_t, ALU.add)
                        dve.drain()
                    elif kind == "ss":
                        g, t = s[1], int(s[2])
                        dve.drain()
                        for st in last_of({"d": ("dq", "dk"), "a": ("aq", "ak"), "b": ("qb0", "qb1", "kvb0", "kvb1")}[g]):
                            dve.wait_ge(strip_taken[st.parity], at(2 * st.turn + 10, STRIPS))
                        if g == "d":
                            squares(nat1[:, t, :], 2 * HEADS, HD, R_D + t * 8)
                        elif g == "a":
                            squares(nat1[:, t, :], 4 * HEADS, SUB, R_A + t * 16)
                        else:
                            squares(nat0[:, t, :], HEADS, QD, R_B + t * 8)
                            dve.drain()
                            squares(nat2[:, t, :], HEADS, QD, R_B + t * 8 + 4)
                        if t == 1:
                            to_mean(s, {"d": HD, "a": SUB, "b": QD}[g]).then_inc(ms_ready, 1)
                    elif kind == "nrm":
                        g, t = s[1], int(s[2])
                        dve.drain()
                        roots(("ss", g, "1"))
                        if g == "d":
                            scale_heads(nat1[:, t, 0:W], HEADS, HD, R_D + t * 8, small, S_DSA)
                            last = scale_heads(nat1[:, t, W:2 * W], HEADS, HD, R_D + t * 8 + 4, small, S_DSA + HD)
                        elif g == "a":
                            scale_heads(nat1[:, t, 0:W], 2 * HEADS, SUB, R_A + t * 16, small, S_DIFF)
                            last = scale_heads(nat1[:, t, W:2 * W], 2 * HEADS, SUB, R_A + t * 16 + 8, small, S_DIFF + SUB)
                        else:
                            scale_heads(nat0[:, t, :], HEADS, QD, R_B + t * 8, small, S_MLA)
                            last = scale_heads(nat2[:, t, :], HEADS, QD, R_B + t * 8 + 4, small, S_MLA + QD)
                        if t == 1:
                            last.then_inc(nrm_done, 1)
                    elif kind == "latss":
                        dve.drain()
                        for st in last_of(("cq", "ckr")):
                            dve.wait_ge(strip_taken[st.parity], at(2 * st.turn + 10, STRIPS))
                        for t in range(TT):
                            for src, o, c in ((nat0[:, t, 0:QR], 0, R_LAT + t), (nat2[:, t, 832:832 + KR], QR, R_LAT + 2 + t)):
                                n = src.shape[1]
                                j = junk[:, o:o + n] if t == 0 else junk[:, o:o + n]
                                if t == 1 and o == 0:
                                    dve.drain()
                                dve.tensor_tensor_reduce(out=j, in0=src, in1=src, scale=1.0, scalar=0.0, op0=ALU.mult,
                                                         op1=ALU.add, accum_out=mean[:, c:c + 1])
                        dve.drain()
                        dve.tensor_scalar(mean[:, R_LAT:R_LAT + 2], mean[:, R_LAT:R_LAT + 2], 1.0 / QR, EPS, ALU.mult, ALU.add)
                        dve.tensor_scalar(mean[:, R_LAT + 2:R_LAT + 4], mean[:, R_LAT + 2:R_LAT + 4], 1.0 / KR, EPS,
                                          ALU.mult, ALU.add).then_inc(ms_ready, 1)
                    elif kind == "krcp":
                        for st in last_of(("ckr", "kvb0", "kvb1")):
                            dve.wait_ge(strip_taken[st.parity], at(2 * st.turn + 10, STRIPS))
                        for t in range(TT):
                            k = nat2[:, t, 0:HEADS * QD].rearrange("p (h c) -> p h c", h=HEADS)
                            kr = nat2[:, t, 832 + KR:832 + KR + ROT].unsqueeze(1).to_broadcast([P, HEADS, ROT])
                            dve.tensor_copy(k[:, :, HD:QD], kr)
                        dve.drain()
                    elif kind == "qk":
                        g, m = s[1], int(s[2])
                        b, slot = m % 2, m % 4
                        scale = {"d": HD, "a": SUB, "b": QD}[g] ** -0.5
                        reader = slot_reader(s)
                        dve.drain()
                        if reader is not None:
                            dve.wait_ge(bank_full[2], at.bank(2, use[found(*reader)][2] + 1))
                        dve.wait_ge(bank_full[b], at.bank(b, use[key][b] + 1))
                        dve.memset(stat[:, slot, 0, :], LOWEST)
                        dve.drain()
                        for t in range(TT):
                            a, z = SEG[t]
                            mask = picks[:, a:z] if g == "d" else (bias_t[:, P:2 * P] if t == 0 else bias_t)
                            last = dve.tensor_tensor_reduce(out=E[:, slot, a:z], in0=PS[:, 4 + b, a:z], in1=mask, scale=1.0,
                                                            scalar=LOWEST, op0=ALU.add, op1=ALU.max,
                                                            accum_out=stat[:, slot, 0, t:t + 1])
                        last.then_inc(bank_taken[b], 1)
                        dve.drain()
                        dve.tensor_scalar(stat[:, slot, 1, :], stat[:, slot, 0, :], -scale, None, ALU.mult).then_inc(max_done, 1)
                    elif kind == "norm":
                        g, h = s[1], int(s[2])
                        if g == "a":
                            dve.wait_ge(exp_done, at(EXP_ORDER.index(("exp", "a", str(2 * h + 1))) + 1, len(EXP_ORDER)))
                            e1, e2 = (2 * h) % 4, (2 * h + 1) % 4
                            dve.reciprocal(stat[:, e1, 3, :], stat[:, e1, 2, :])
                            dve.reciprocal(stat[:, e2, 3, :], stat[:, e2, 2, :])
                            dve.drain()
                            dve.tensor_scalar(stat[:, e2, 3, :], stat[:, e2, 3, :], lam[:, 4:5], None, ALU.mult)
                            for t in range(TT):
                                a, z = SEG[t]
                                dve.tensor_scalar(E[:, e1, a:z], E[:, e1, a:z], stat[:, e1, 3, t:t + 1], None, ALU.mult)
                            dve.drain()
                            for t in range(TT):
                                a, z = SEG[t]
                                last = dve.scalar_tensor_tensor(E[:, e1, a:z], E[:, e2, a:z], stat[:, e2, 3, t:t + 1],
                                                                E[:, e1, a:z], ALU.mult, ALU.add)
                        else:
                            dve.wait_ge(exp_done, at(EXP_ORDER.index(("exp", g, s[2])) + 1, len(EXP_ORDER)))
                            slot = h % 4
                            dve.reciprocal(stat[:, slot, 3, :], stat[:, slot, 2, :])
                            dve.drain()
                            for t in range(TT):
                                a, z = SEG[t]
                                last = dve.tensor_scalar(E[:, slot, a:z], E[:, slot, a:z], stat[:, slot, 3, t:t + 1], None, ALU.mult)
                        last.then_inc(map_done, 1)
                    elif kind == "pv":
                        g, h = s[1], int(s[2])
                        if g != "a":
                            high_ready(key)
                            k = FIRST_TILE[g] + h
                            dve.tensor_tensor(mT_lo[:, k, :], w_bank(3, SEQ), f(mT_hi[:, k, :]), ALU.subtract).then_inc(bank_taken[3], 1)
                    elif kind == "oss":
                        dve.drain()
                        dve.wait_ge(bank_taken[3], at.bank(3, use[found("pv", "a", "3")][3] + 2))
                        for t in range(TT):
                            o = t * 4 * HD
                            for h in range(HEADS):
                                v = nat1[:, t, h * HD:(h + 1) * HD]
                                dve.tensor_tensor_reduce(out=junk[:, o + h * HD:o + (h + 1) * HD], in0=v, in1=v, scale=1.0, scalar=0.0,
                                                         op0=ALU.mult, op1=ALU.add, accum_out=mean[:, R_O + 4 * t + h:R_O + 4 * t + h + 1])
                        to_mean(s, HD).then_inc(ms_ready, 1)
                    elif kind == "onrm":
                        roots(("oss",))
                        for t in range(TT):
                            last = scale_heads(nat1[:, t, 0:GW], HEADS, HD, R_O + 4 * t, small, S_SUBLN)
                        last.then_inc(nrm_done, 1)
                        dve.drain()
                        dve.sem_inc(small_free, 1)
                    elif kind == "oT":
                        high_ready(key)
                        i = int(s[1])
                        dve.tensor_tensor(mT_lo[:, 2 * i:2 * i + 2, :], w_bank(2).rearrange("p (j n) -> p j n", j=2),
                                          f(mT_hi[:, 2 * i:2 * i + 2, :]), ALU.subtract).then_inc(bank_taken[2], 1)
                    elif kind == "sp":
                        h = int(s[1])
                        logits = nat2[:, :, :].rearrange("p t n -> p (t n)")[:, h * 3 * P:(h + 1) * 3 * P]
                        dve.wait_ge(ln_done, at(1, 1))
                        dve.scalar_tensor_tensor(E[:, h, :], logits, 0.0, E[:, h, :], ALU.max, ALU.add)
                        dve.drain()
                        dve.tensor_tensor(E[:, h, 0:P], E[:, h, 0:P], strict01, ALU.mult)
                        dve.tensor_tensor(E[:, h, SEQ:3 * P], E[:, h, SEQ:3 * P], strict01, ALU.mult).then_inc(sp_done, 1)
                    elif kind == "R":
                        h = int(s[1])
                        b = h % 2
                        logits = nat2[:, :, :].rearrange("p t n -> p (t n)")[:, h * 3 * P:(h + 1) * 3 * P]
                        dve.wait_ge(bank_full[b], at.bank(b, use[key][b] + 1))
                        dve.tensor_tensor(logits, logits, w_bank(b, 3 * P), ALU.subtract).then_inc(bank_taken[b], 1)
                        dve.drain()
                        dve.tensor_tensor(logits[:, 0:P], logits[:, 0:P], strict_neg, ALU.add)
                        dve.tensor_tensor(logits[:, SEQ:3 * P], logits[:, SEQ:3 * P], strict_neg, ALU.add).then_inc(z_done, 1)
                    elif kind == "X":
                        st = strips[s[1], int(s[2])]
                        q = int(s[2])
                        dve.drain()
                        dve.wait_ge(half_used, at.half(st.last_half + 5))
                        for t in range(TT):
                            v = x[:, t, q * W:(q + 1) * W]
                            dve.tensor_tensor(v, v, PS[:, 2 * st.parity + t, :], ALU.add).then_inc(strip_taken[st.parity], 1)
                    elif kind == "U":
                        part = pos.strip.arg[0]
                        gate, up = pair_strip("gate", s[1], part), pair_strip("up", s[1], part)
                        turns = PARTS[part] - 2 if s[1] == "last" else 0
                        dve.wait_ge(half_used, at.half(up.last_half + PAIR_HALVES * turns + 5))
                        dve.wait_ge(strip_taken[0], at.strip(2 * (gate.turn + turns) + 10))
                        for t in range(TT):
                            dve.scalar_tensor_tensor(nat1[:, t, 0:W], PS[:, 2 * up.parity + t, :], rinv[:, R_XF + t:R_XF + t + 1],
                                                     nat0[:, t, 0:W], ALU.mult, ALU.mult).then_inc(strip_taken[up.parity], 1)
                    elif kind == "hidT":
                        i = int(s[1])
                        high_ready(key)
                        part = pos.strip.arg[0]
                        if s[2] == "last":
                            k = 4 * (PARTS[part] - 1) + 2 * i
                            hi, lo = mT_hi[:, k:k + 2, :], mT_lo[:, k:k + 2, :]
                        else:
                            ks = bass.ds(at.pair * 4 + 2 * i, 2)
                            hi, lo = mT_hi[:, ks, :], mT_lo[:, ks, :]
                        dve.tensor_tensor(lo, w_bank(2 + i).rearrange("p (j n) -> p j n", j=2), f(hi), ALU.subtract).then_inc(bank_taken[2 + i], 1)

                def line(pos, nxt, pair):
                    at.pair = pair
                    early = pos is sections[0][1][0]
                    if early:
                        for half in halves_of(pos, None):
                            split(*half)
                        for s in pos.steps:
                            step(s, pos, key_of(s, pos))
                    for half in lead_halves(pos, nxt)[0]:
                        split(*half)
                    if not early:
                        for s in pos.steps:
                            step(s, pos, key_of(s, pos))
                    at.pair = None

                walk(dve.Fori, line)
                for s in tail_steps:
                    step(s, None, None)

        @block.gpsimd
        def _(pool):
            pool.memset(gain_rows, 0.0).then_inc(init_done, 1)
            pool.memset(minus_half[:, :], -0.5)
            pool.drain()
            pool.wait_ge(consts_full, 16)
            with pool.Fori(0, DEPTH) as l:
                at = Place(l)

                def rotate(x1, x2, y1, y2, half, heads):
                    cos, sin = (c.unsqueeze(2).to_broadcast([P, TT, heads, half]) for c in cos_sin(half))
                    n = heads * half
                    t0, t1, t2 = (rtmp[:, i, 0:TT * n].rearrange("p (t h c) -> p t h c", t=TT, h=heads) for i in range(3))
                    pool.tensor_tensor(t0, x1, cos, ALU.mult)
                    pool.tensor_tensor(t1, x2, sin, ALU.mult)
                    pool.tensor_tensor(t2, x1, sin, ALU.mult)
                    pool.drain()
                    pool.tensor_tensor(x2, x2, cos, ALU.mult)
                    pool.tensor_tensor(y1, t0, t1, ALU.subtract)
                    pool.drain()
                    return pool.tensor_tensor(y2, x2, t2, ALU.add)

                def step(s):
                    kind = s[0]
                    if kind in ("iqrope", "iknrm", "rope"):
                        pool.drain()
                    if s in ms_event:
                        col, n = MS_COLS[s]
                        pool.wait_ge(ms_ready, at(ms_event[s] + 1, MS))
                        pool.tensor_tensor(rinv[:, col:col + n], mean[:, col:col + n], minus_half[:, 0:n], ALU.pow).then_inc(rinv_ready, 1)
                    elif kind == "iqrope":
                        for st in last_of(("iq0", "iq1")):
                            pool.wait_ge(strip_taken[st.parity], at(2 * st.turn + 10, STRIPS))
                        v = nat0[:, :, :].rearrange("p t (h c) -> p t h c", h=IH)
                        rotate(v[:, :, :, 0:8], v[:, :, :, 8:16], v[:, :, :, 0:8], v[:, :, :, 8:16], 8, IH).then_inc(rope_done, 1)
                    elif kind == "iknrm":
                        pool.wait_ge(nrm_done, at(NRM_ORDER.index(s) + 1, len(NRM_ORDER)))
                        v = ikd[:, :, :].rearrange("p t (h c) -> p t h c", h=2)[:, :, 0:1, :]
                        rotate(v[:, :, :, 0:8], v[:, :, :, 8:16], v[:, :, :, 0:8], v[:, :, :, 8:16], 8, 1)
                        pool.drain()
                        pool.tensor_copy(ikd[:, :, ID:2 * ID], ikd[:, :, 0:ID]).then_inc(rope_done, 1)
                    elif kind == "rope":
                        g = s[1]
                        pool.wait_ge(nrm_done, at(NRM_ORDER.index(("nrm", g, "1")) + 1, len(NRM_ORDER)))
                        if g == "b":
                            nat = (nat0, nat2)[int(s[2])]
                            v = nat[:, :, 0:HEADS * QD].rearrange("p t (h c) -> p t h c", h=HEADS)
                            y = nat[:, :, HEADS * QD:HEADS * (QD + ROT)].rearrange("p t (h c) -> p t h c", h=HEADS)
                            last = rotate(v[:, :, :, HD:HD + 32], v[:, :, :, HD + 32:QD], y[:, :, :, 0:32], y[:, :, :, 32:64], 32, HEADS)
                            if s[2] == "1":
                                last.then_inc(rope_done, 1)
                        else:
                            n, half = (2 * HEADS, 16) if g == "d" else (4 * HEADS, 8)
                            v = nat1[:, :, :].rearrange("p t (h c) -> p t h c", h=n)
                            rotate(v[:, :, :, 0:half], v[:, :, :, half:2 * half], v[:, :, :, 0:half], v[:, :, :, half:2 * half],
                                   half, n).then_inc(rope_done, 1)

                for section in sections:
                    if section[0] == "line":
                        for pos in section[1]:
                            for s in pos.steps:
                                step(s)


_INS = ["x", "attn_norm", "w_in", "diff_qk_norm", "diff_lambda", "diff_subln", "mla_q_a_norm", "mla_wq_b", "mla_kv_a_norm",
        "mla_wkv_b", "mla_qk_norm", "dsa_qk_norm", "idx_k_norm", "w_o", "ffn_norm", "w_gate", "w_up", "w_down"]
_OUT = ((1, 256, 2048), "float32")


def _constants():
    import math
    import numpy as np
    P, MASKED = 128, -1e30
    r, c = np.arange(P)[:, None], np.arange(P)[None, :]
    parts = [np.eye(P), np.zeros((P, P)), np.where(c <= r, 0.0, MASKED), np.where(r < c, 1.0, 0.0),
             np.where(r < c, 0.0, MASKED), np.where(r >= c, 1.0, 0.0), np.ones((P, P))]
    for half in (8, 16, 32):
        inv = np.float32(500000.0) ** (-np.arange(half, dtype=np.float32) * np.float32(2.0) / np.float32(2 * half))
        ang = np.arange(2 * P, dtype=np.float32)[:, None] * inv.astype(np.float32)[None, :]
        for fn in (np.cos, np.sin):
            table = fn(ang.astype(np.float64))
            parts.append(table.reshape(2, P, half).transpose(1, 0, 2).reshape(P, 2 * half))
    for layer in range(2):
        start = 0.8 - 0.6 * math.exp(-0.3 * layer)
        parts.append(np.tile([[start, 1.0 - start]], (P, 1)))
    return np.ascontiguousarray(np.concatenate(parts, axis=1).astype(np.float32))


def kernel(**inputs):
    import numpy as _np
    import concourse.bacc as _bacc
    from concourse import mybir as _mybir
    from concourse.bass_utils import run_bass_kernel_spmd as _run

    nc = _bacc.Bacc("TRN2", target_bir_lowering=False, num_devices=1)
    arrays, args = {}, []
    for name in _INS + ["constants"]:
        a = _constants() if name == "constants" else _np.ascontiguousarray(inputs[name])
        arrays[f"in_{name}_dram"] = a
        args.append(nc.dram_tensor(f"in_{name}_dram", a.shape, _mybir.dt.from_np(a.dtype), kind="ExternalInput").ap())
    args.append(nc.dram_tensor("out_0_dram", _OUT[0], _mybir.dt.from_np(_np.dtype(_OUT[1])), kind="ExternalOutput").ap())
    trunk_kernel(nc, *args)
    r = _run(nc, [arrays], core_ids=[0])
    return r.results[0]["out_0_dram"]
```

```python
import concourse.bass as bass
from concourse import mybir
from contextlib import ExitStack

ATTENTION = [
    ("iq1", ["xms a; hT 0",
            "hT 1; lam 0",
            "",
            "hT 2; lam 1; lam 2",
            "",
            "hT 3",
            "",
            ""]),
    ("dk", ["",
           "E iq1",
           "",
           "",
           "",
           "",
           "",
           ""]),
    ("iq0", ["",
            "E dk",
            "",
            "",
            "",
            "",
            "",
            ""]),
    ("ikw", ["",
            "",
            "",
            "",
            "",
            "",
            "",
            "E iq0; iqrope"]),
    ("dq", ["E ikw; ikss",
           "",
           "",
           "iqT 0; iknrm",
           "iqT 1; ikT",
           "iqT 2",
           "iqT 3",
           ""]),
    ("ckr", ["",
            "",
            "",
            "",
            "",
            "",
            "E dq",
            "idx 0"]),
    ("cq", ["E ckr; ss d 0",
           "idx 1; ckvT",
           "ss d 1",
           "idx 2",
           "nrm d 0",
           "idx 3",
           "nrm d 1; rope d",
           "idx 4"]),
    ("dv", ["E cq; latss",
           "idx 5; latT 0",
           "",
           "idx 6; qkT d 0",
           "idx 7; latT 1; topk 0",
           "topk 1",
           "qkT d 1",
           "qkT d 2"]),
    ("kvb0", ["",
             ""]),
    ("kvb1", ["E dv",
             "E kvb0; qkT d 3; topk 2; topk 3"]),
    ("aq", ["E kvb1; krcp",
           "topk 4; topk 5",
           "topk 6",
           "topk 7",
           "sel",
           "",
           "",
           "qk d 0"]),
    ("qb1", ["qk d 1",
            "E aq; exp d 0; exp d 1; norm d 0; norm d 1; qk d 2"]),
    ("qb0", ["E qb1; exp d 2; norm d 2; pT d 0",
            "qk d 3"]),
    ("ak", ["E qb0; exp d 3; norm d 3; pT d 1; ss b 0; pv d 0",
           "pT d 2; ss b 1",
           "pv d 1; pT d 3; nrm b 0",
           "",
           "nrm b 1; rope b 0; rope b 1; pv d 2",
           "",
           "pv d 3",
           ""]),
    ("zq", ["",
           "E ak; ss a 0; ss a 1",
           "qkT b 0; nrm a 0",
           "qkT b 1",
           "qkT b 2; nrm a 1; rope a",
           "qkT b 3",
           "qkT b 4",
           "qkT b 5"]),
    ("zk", ["E zq; qk b 0; qkT a 0; exp b 0",
           "norm b 0; qk b 1; qkT a 1; exp b 1",
           "norm b 1; qk b 2; qkT a 2",
           "exp b 2; norm b 2; qk b 3; qkT a 3; exp b 3",
           "norm b 3; pT b 0",
           "pv b 0; pT b 1",
           "pv b 1; pT b 2",
           "pv b 2; pT b 3"]),
    ("av", ["E zk; qk a 0; pv b 3; qkT z 0; qk a 1; qkT z 1; exp a 0; exp a 1",
           "qk a 2; qkT z 2; norm a 0",
           "qk a 3; qkT z 3; exp a 2; exp a 3",
           "pT a 0; norm a 1",
           "qk a 4",
           "pT a 1; exp a 4",
           "qk a 5",
           "qk a 6"]),
    ("zv", ["qk a 7; exp a 5; norm a 2; exp a 6; E av; exp a 7; norm a 3",
           "pv a 0; pT a 2",
           "pv a 1; pT a 3",
           "pv a 2; z 0; pv a 3",
           "oss; z 1",
           "onrm; z 2",
           "oT 0; z 3; zln",
           "sp 0"]),
    ("wo0", ["E zv; sp 1; oT 1",
            "sp 2",
            "sp 3",
            "R 0"]),
    ("wo1", ["",
            "R 1; zexp 0; pv z 0; zexp 1",
            "pv z 1; R 2",
            "R 3; zexp 2; pv z 2; zexp 3"]),
    ("wo0", ["pv z 3",
            "",
            "",
            ""]),
    ("wo1", ["X wo 0; xsq wo 0",
            "fT 0",
            "",
            ""]),
    ("wo2", ["X wo 1; xsq wo 1",
            "fT 1",
            "",
            "",
            "",
            "",
            "",
            ""]),
    ("wo3", ["X wo 2; xsq wo 2",
            "fT 2",
            "",
            "",
            "",
            "",
            "",
            ""]),
]


def trunk_kernel(nc, x_in, attn_norm, w_in, diff_qk_norm, diff_lambda, diff_subln, mla_q_a_norm, mla_wq_b,
                 mla_kv_a_norm, mla_wkv_b, mla_qk_norm, dsa_qk_norm, idx_k_norm, w_o, ffn_norm, w_gate, w_up,
                 w_down, constants, out):
    F32, F32R, BF16 = mybir.dt.float32, mybir.dt.float32r, mybir.dt.bfloat16
    ALU, ACT, AX = mybir.AluOpType, mybir.ActivationFunctionType, mybir.AxisListType

    _, SEQ, D = x_in.shape
    DEPTH = w_in.shape[0]
    HIDDEN = w_gate.shape[2]
    P = 128
    TT = SEQ // P
    W = 512
    KD = D // P
    HD, HEADS, GW = 128, 4, 512
    SUB = HD // 2
    ROT = 64
    QD = HD + ROT
    QR, KR = mla_wq_b.shape[1], mla_wkv_b.shape[1]
    LK = QR // 4
    IH, ID = 16, 64
    TOPK = SEQ // 4
    EPS = 1e-6
    MASKED, TAKEN, LOWEST = -1e30, -3e38, -3.3e38
    assert TT == 2 and TOPK % 8 == 0 and QR == 4 * LK and KR == P

    A0, B0, C0, D0 = 0, 3 * GW, 3 * GW + QR + KR + ROT, 6 * GW + QR + KR + ROT
    I0 = D0 + 3 * GW
    COLUMNS = {"aq": A0, "ak": A0 + GW, "av": A0 + 2 * GW, "cq": B0, "ckr": B0 + QR,
               "zq": C0, "zk": C0 + GW, "zv": C0 + 2 * GW, "dq": D0, "dk": D0 + GW, "dv": D0 + 2 * GW,
               "iq0": I0, "iq1": I0 + W, "ikw": I0 + 2 * W}
    WIDTH = {"cq": QR, "ckr": KR + ROT, "ikw": ID + IH, "qb1": HEADS * QD - W}
    GROUP_ORDER = [3, 1, 0, 2]
    FIRST_TILE = {"a": 0, "b": 4, "z": 8, "d": 12}

    class Strip:
        def __init__(s, kind, name, arg=0, halves=8):
            s.kind, s.name, s.arg = kind, name, arg
            s.width = WIDTH.get(name, W)
            s.rows = LK if name in ("qb0", "qb1") else P
            if kind == "kvb":
                s.halves = [([0], 0, W // 2), ([0], W // 2, W)]
            else:
                s.halves = [([2 * i, 2 * i + 1], 0, s.width) for i in range(halves)]

    class Position:
        def __init__(s, strip, i, steps):
            s.strip, s.i, s.steps = strip, i, steps

    def positions(strip, steps):
        return [Position(strip, i, steps.get(i, [])) for i in range(len(strip.halves))]

    head, tail_steps, begun = [], [], {}
    for name, rows in ATTENTION:
        if name in begun:
            s = begun[name]
        elif name[:2] == "wo":
            s = Strip("wo", name, int(name[2]))
        elif name[:2] == "qb":
            s = Strip("qb", name, int(name[2]), halves=2)
        elif name[:3] == "kvb":
            s = Strip("kvb", name, int(name[3]))
        else:
            s = Strip("in", name)
        begun[name] = s
        done = sum(pos.strip is s for pos in head)
        head += [Position(s, done + i, [tuple(x.split()) for x in row.split("; ") if x]) for i, row in enumerate(rows)]
    PARTS = [4, 4, 3]
    assert sum(PARTS) * W == HIDDEN

    def pair_strips(part, pair):
        return Strip("gate", "gate", (part, pair)), Strip("up", "up", (part, pair))

    sections = []
    for part, pairs in enumerate(PARTS):
        gate, up = pair_strips(part, 0)
        before = {0: [("X", "wo", "3")], 2: [("fT", "3"), ("xsq", "wo", "3")], 4: [("xms", "f")]} if part == 0 else \
                 {0: [("X", f"down{part - 1}", "3")]}
        head += positions(gate, before) + positions(up, {0: [("G", "first")]})
        sections.append(("line", head))
        gate, up = pair_strips(part, 1)
        sections.append(("loop", pairs - 1,
                         positions(gate, {0: [("U", "before")], 2: [("hidT", "0", "before")], 3: [("hidT", "1", "before")]})
                         + positions(up, {0: [("G", "this")]})))
        head = []
        final = part == len(PARTS) - 1
        for s in range(4):
            strip = Strip("down", f"down{part}", (part, s), halves=2 * pairs)
            steps = {0: [("X", f"down{part}", str(s - 1))]} if s else \
                    {0: [("U", "last")], 2: [("hidT", "0", "last")], 3: [("hidT", "1", "last")]}
            if s and final:
                steps[2] = [("xsq", f"down{part}", str(s - 1))]
            head += positions(strip, steps)
        if final:
            sections.append(("line", head))
            tail_steps = [("X", f"down{part}", "3"), ("xsq", f"down{part}", "3")]

    BANKS = {"hT": (2, 3), "fT": (2, 3), "iqT": (2,), "ikT": (3,), "qkT": (2,), "latT": (2,), "ckvT": (3,), "pT": (2,),
             "pv": (3,), "oT": (2,)}

    def banks(step):
        kind = step[0]
        if kind == "idx":
            return (0, 1)
        if kind in ("z", "R"):
            return (int(step[1]) % 2,)
        if kind == "qk":
            return (int(step[2]) % 2,)
        if kind == "hidT":
            return (2 + int(step[1]),)
        return BANKS.get(kind, ())

    HIGH = ("latT", "ckvT", "oT", "hidT")
    strips, use, high, ms_event = {}, {}, {}, {}
    n_half = n_strip = n_high = n_ms = 0
    n_use = [0] * 4
    pairs_seen = {}
    for section in sections:
        body = section[-1]
        turns = section[1] if section[0] == "loop" else 1
        start = (n_half, n_strip, n_high, list(n_use))
        for pos in body:
            pos.place = n_half
            n_half += 1
            s = pos.strip
            if pos.i == len(s.halves) - 1:
                s.last_half = pos.place
            if pos.i == 0:
                s.parity, s.turn = n_strip % 2, n_strip // 2
                n_strip += 1
                if s.kind in ("gate", "up"):
                    pairs_seen[s.kind, section[0] == "loop", s.arg[0]] = s
                else:
                    strips[s.name if s.kind != "down" else (s.name, s.arg[1])] = s
                if s.kind == "wo":
                    strips["wo", s.arg] = s
            for step in pos.steps:
                key = (step, section[0] == "loop", pos.strip.name if step[0] in ("hidT",) else "",
                       pos.strip.arg[0] if step[0] == "hidT" else 0)
                pos_key = key
                for b in banks(step):
                    use.setdefault(pos_key, {})[b] = n_use[b]
                    n_use[b] += 1
                if step[0] in ("hT", "fT"):
                    high[pos_key] = n_high
                    n_high += 2
                elif step[0] in HIGH or (step[0] == "pv" and step[1] != "a"):
                    high[pos_key] = n_high
                    n_high += 1
                if step[0] in ("xms", "ikss", "latss", "oss") or (step[0] == "ss" and step[2] == "1"):
                    ms_event[step] = n_ms
                    n_ms += 1
        if turns > 1:
            n_half += (turns - 1) * (n_half - start[0])
            n_strip += (turns - 1) * (n_strip - start[1])
            n_high += (turns - 1) * (n_high - start[2])
            for b in range(4):
                n_use[b] += (turns - 1) * (n_use[b] - start[3][b])
    HALVES, STRIPS, HIGHS, USES, MS = n_half, n_strip, n_high, n_use, n_ms
    assert HALVES % 4 == 0 and STRIPS % 2 == 0
    PAIR_HALVES = 16
    order = [step for section in sections for pos in section[-1] for step in pos.steps]

    def key_of(step, pos):
        loop = pos is not None and pos.strip.kind in ("gate", "up") and pos.strip.arg[1] == 1
        return (step, loop, pos.strip.name if step[0] == "hidT" else "", pos.strip.arg[0] if step[0] == "hidT" else 0)

    def last_of(names):
        by_parity = {}
        for s in sorted((strips[name] for name in names), key=lambda s: s.turn):
            by_parity[s.parity] = s
        return list(by_parity.values())

    def found(kind, *args):
        return ((kind, *args), False, "", 0)

    P_ORDER = [s for s in order if s[0] == "pT"]
    PV_ORDER = [s for s in order if s[0] == "pv"]
    QK_ORDER = [s for s in order if s[0] == "qk"]
    PROBS_ORDER = [s for s in order if s[0] in ("pT", "zexp")]

    def probs_slot(step):
        return PROBS_ORDER.index(step) % 2

    def pv_of(writer):
        return ("pv", "z", writer[1]) if writer[0] == "zexp" else ("pv", writer[1], writer[2])

    def writer_of(pv):
        return ("zexp", pv[2]) if pv[1] == "z" else ("pT", pv[1], pv[2])

    def slot_reader(qk):
        n, slot = order.index(qk), int(qk[2]) % 4
        for s in reversed(order[:n]):
            if s[0] == "pT" and (2 * int(s[2]) if s[1] == "a" else int(s[2])) % 4 == slot:
                return s
        return None

    MAP_DONE = [s for s in order if s[0] == "norm"]
    EXP_ORDER = [s for s in order if s[0] == "exp"]
    ROPE_ORDER = [s for s in order if s[0] in ("iqrope", "iknrm") or (s[0] == "rope" and s[1:] != ("b", "0"))]
    NRM_ORDER = [s for s in order if s[0] in ("iknrm", "onrm") or (s[0] == "nrm" and s[2] == "1")]
    SP_ORDER = [s for s in order if s[0] == "sp"]
    Z_ORDER = [s for s in order if s[0] == "R"]
    ZEXP_ORDER = [s for s in order if s[0] == "zexp"]

    ctx = ExitStack()
    with ctx:
        def sb(name, shape, dt=F32):
            return ctx.enter_context(nc.sbuf_tensor(name, shape, dt))

        def sem(name):
            return ctx.enter_context(nc.semaphore(name))

        raw = sb("raw", [P, 4, 2, W])
        w_hi, w_lo = sb("w_hi", [P, 4, 2, W], F32R), sb("w_lo", [P, 4, 2, W], F32R)
        x = sb("x", [P, TT, D])
        hT_hi, hT_lo = sb("hT_hi", [P, KD, SEQ], F32R), sb("hT_lo", [P, KD, SEQ], F32R)
        mT_hi, mT_lo = sb("mT_hi", [P, KD, SEQ], F32R), sb("mT_lo", [P, KD, SEQ], F32R)
        nat0 = sb("nat0", [P, TT, 1024])
        nat1 = sb("nat1", [P, TT, 1024])
        nat2 = sb("nat2", [P, TT, 1024])
        v_even, v_odd = sb("v_even", [P, TT, GW]), sb("v_odd", [P, TT, GW])
        T0, T1 = sb("T0", [P, 8, SEQ]), sb("T1", [P, 8, SEQ])
        Tr = sb("Tr", [P, 4, SEQ])
        SEG = [(0, P), (P, 3 * P)]
        E = sb("E", [P, 4, 3 * P])
        probs = sb("probs", [P, 2, 3 * P])
        picks, taken = (Tr[:, :, :].rearrange("p a b -> p (a b)")[:, i * 3 * P:(i + 1) * 3 * P] for i in (0, 1))
        ikT = sb("ikT", [P, SEQ])
        ikw = sb("ikw", [P, TT, ID + IH])
        ikd = sb("ikd", [P, TT, 2 * ID])
        iw = sb("iw", [P, TT, IH])
        best = sb("best", [P, TT, 8])
        junk = sb("junk", [P, 1024], BF16)
        rtmp = sb("rtmp", [P, 3, SEQ])
        stat = sb("stat", [P, 4, 4, TT])
        NG = 2 * KD + 5
        gain_rows = T1[:, 0, 0:P]
        gain_all = sb("gain_all", [P, DEPTH * NG])
        gain = sb("gain", [P, NG])
        small = sb("small", [P, 1216])
        cst = sb("cst", [P, constants.shape[1]])
        lam = sb("lam", [P, 8])
        lam_init = sb("lam_init", [P, 2])
        xsq = sb("xsq", [P, TT, 4])
        mean = sb("mean", [P, 96])
        rinv = sb("rinv", [P, 96])
        minus_half = sb("minus_half", [P, 32])
        PS = ctx.enter_context(nc.psum_tensor("PS", [P, 8, W], F32))

        R_X, R_IK, R_D, R_LAT, R_A, R_B, R_O, R_XF = 0, 2, 4, 20, 24, 56, 72, 80
        MS_COLS = {("xms", "a"): (R_X, 2), ("ikss",): (R_IK, 2), ("ss", "d", "1"): (R_D, 16), ("latss",): (R_LAT, 4),
                   ("ss", "a", "1"): (R_A, 32), ("ss", "b", "1"): (R_B, 16), ("oss",): (R_O, 8), ("xms", "f"): (R_XF, 2)}
        S_DIFF, S_SUBLN, S_MLA, S_DSA, S_IDX, S_LAM = 0, 128, 256, 640, 896, 960
        ident, bias_t = cst[:, 0:P], cst[:, P:3 * P]
        strict01, strict_neg, upper, ones = (cst[:, (3 + i) * P:(4 + i) * P] for i in range(4))
        ROPE_AT = {8: 7 * P, 16: 7 * P + 32, 32: 7 * P + 96}
        C_LAM = 7 * P + 224

        def cos_sin(half):
            a = ROPE_AT[half]
            return (cst[:, a + i * 2 * half:a + (i + 1) * 2 * half].rearrange("p (t h) -> p t h", t=TT) for i in (0, 1))

        raw_full = [sem(f"raw_full{i}") for i in range(4)]
        hi_done = sem("hi_done")
        lo_done = sem("lo_done")
        half_used = sem("half_used")
        strip_taken = [sem("strip_taken0"), sem("strip_taken1")]
        bank_full = [sem(f"bank_full{i}") for i in range(4)]
        bank_taken = [sem(f"bank_taken{i}") for i in range(4)]
        high_done = sem("high_done")
        consts_full, x_full, rows_full, small_full = sem("consts_full"), sem("x_full"), sem("rows_full"), sem("small_full")
        small_free = sem("small_free")
        init_done = sem("init_done")
        slot_seen = sem("slot_seen")
        gain_ready = sem("gain_ready")
        xsq_done = sem("xsq_done")
        ms_ready = sem("ms_ready")
        rinv_ready = sem("rinv_ready")
        nrm_done = sem("nrm_done")
        rope_done = sem("rope_done")
        relu_done = sem("relu_done")
        idx_added = sem("idx_added")
        max_done, exp_done, map_done = sem("max_done"), sem("exp_done"), sem("map_done")
        lam_sums, lam_exps = sem("lam_sums"), sem("lam_exps")
        ln_done, sp_done, z_done, zexp_done = sem("ln_done"), sem("sp_done"), sem("z_done"), sem("zexp_done")
        stored = sem("stored")

        block = ctx.enter_context(nc.Block())

        def f(ap):
            return ap.bitcast(F32)

        def w_bank(b, n=W):
            return PS[:, 4 + b, 0:n]

        def raw_source(strip, i, l, pair):
            kts, c0, c1 = strip.halves[i]
            k0, nk = kts[0], len(kts)
            if strip.kind == "in":
                c = COLUMNS[strip.name]
                src = w_in[l, k0 * P:(k0 + nk) * P, c + c0:c + c1]
            elif strip.kind == "qb":
                src = mla_wq_b[l, k0 * LK:(k0 + nk) * LK, strip.arg * W:strip.arg * W + strip.width]
            elif strip.kind == "kvb":
                src = mla_wkv_b[l, :, strip.arg * W + c0:strip.arg * W + c1]
            elif strip.kind == "wo":
                r = GROUP_ORDER[k0 // 4] * GW + (k0 % 4) * P
                src = w_o[l, r:r + nk * P, strip.arg * W:(strip.arg + 1) * W]
            elif strip.kind in ("gate", "up"):
                part, p = strip.arg
                w = w_gate if strip.kind == "gate" else w_up
                c = (sum(PARTS[:part]) + p) * W
                src = w[l, k0 * P:(k0 + nk) * P, c:c + W] if pair is None else \
                    w[l, k0 * P:(k0 + nk) * P, bass.ds(pair * W + c, W)]
            else:
                part, s = strip.arg
                r = sum(PARTS[:part]) * W + k0 * P
                src = w_down[l, r:r + nk * P, s * W:(s + 1) * W]
            return src.rearrange("(t p) n -> p t n", p=strip.rows)

        def ahead(k, j, by):
            body = sections[k][-1]
            if j + by < len(body):
                pos = body[j + by]
                return pos.strip, pos.i, pos.place
            if sections[k][0] == "loop":
                pos = body[j + by - len(body)]
                return pos.strip, pos.i, pos.place + len(body)
            if k + 1 < len(sections):
                pos = sections[k + 1][-1][j + by - len(body)]
                return pos.strip, pos.i, pos.place
            return None

        LEAD = 2

        def starts_tensor(strip, i):
            k0, c0 = strip.halves[i][0][0], strip.halves[i][1]
            if strip.kind == "in":
                return COLUMNS[strip.name] == 0 and k0 == 0
            if strip.kind == "wo":
                return strip.arg == 0 and GROUP_ORDER[k0 // 4] == 0 and k0 % 4 == 0
            return strip.arg in (0, (0, 0)) and k0 == 0 and c0 == 0

        def walk(fori, line):
            for k, section in enumerate(sections):
                body = section[-1]
                if section[0] == "line":
                    for j, pos in enumerate(body):
                        line(pos, ahead(k, j, LEAD), None)
                else:
                    with fori(0, section[1]) as pair:
                        for j, pos in enumerate(body):
                            line(pos, ahead(k, j, LEAD), pair)

        class Place:
            def __init__(s, l):
                s.l, s.pair = l, None

            def __call__(s, n, per_layer, per_pair=0):
                v = s.l * per_layer + n
                if s.pair is not None and per_pair:
                    v = v + s.pair * per_pair
                return v

            def half(s, n):
                return s(n, HALVES, PAIR_HALVES)

            def strip(s, n):
                return s(n, STRIPS, 2)

            def bank(s, b, n):
                return s(n, USES[b], 1)

            def high(s, n):
                return s(n, HIGHS, 2)

        def split_view(strip, i, u):
            kts, c0, c1 = strip.halves[i]
            return slice(0, strip.rows), u % 4, slice(0, len(kts)), slice(0, c1 - c0)

        def pair_strip(kind, which, part):
            return pairs_seen[kind, False if which in ("first", "before") else True, part]

        @block.sync
        def _(sp):
            sp.dma_start(cst[:, :], constants).then_inc(consts_full, 16)
            for t in range(TT):
                sp.dma_start(x[:, t, :], x_in[0, t * P:(t + 1) * P, :]).then_inc(x_full, 16)
            sp.wait_ge(init_done, 1)
            for l in range(DEPTH):
                r = l * NG
                sp.dma_start(gain_rows[r:r + KD, :], attn_norm[l].rearrange("(k p) -> k p", p=P)).then_inc(rows_full, 16)
                sp.dma_start(gain_rows[r + KD:r + 2 * KD, :], ffn_norm[l].rearrange("(k p) -> k p", p=P)).then_inc(rows_full, 16)
                sp.dma_start(gain_rows[r + 2 * KD:r + 2 * KD + 4, 0:LK],
                             mla_q_a_norm[l].rearrange("(k p) -> k p", p=LK)).then_inc(rows_full, 16)
                sp.dma_start(gain_rows[r + 2 * KD + 4:r + 2 * KD + 5, :], mla_kv_a_norm[l:l + 1, :]).then_inc(rows_full, 16)
            with sp.Fori(0, DEPTH) as l:
                at = Place(l)
                sp.wait_ge(small_free, at(1, 1))
                for a, src in ((S_DIFF, diff_qk_norm), (S_MLA, mla_qk_norm), (S_DSA, dsa_qk_norm), (S_LAM, diff_lambda)):
                    n = src.shape[1] * src.shape[2]
                    rows = src[l].rearrange("(o a) b -> o (a b)", o=1).to_broadcast([P, n])
                    sp.dma_start(small[:, a:a + n], rows).then_inc(small_full, 16)
                for a, src in ((S_SUBLN, diff_subln), (S_IDX, idx_k_norm)):
                    n = src.shape[1]
                    rows = src[l].rearrange("(o a) -> o a", o=1).to_broadcast([P, n])
                    sp.dma_start(small[:, a:a + n], rows).then_inc(small_full, 16)

                def line(pos, nxt, pair):
                    at.pair = pair
                    strip, i, u = pos.strip, pos.i, pos.place
                    r, slot, k, c = split_view(strip, i, u)
                    source = raw_source(strip, i, l, pair)
                    sp.wait_ge(lo_done, at.half(u + 1))
                    if pair is None and starts_tensor(strip, i):
                        sp.sem_inc(slot_seen, 1)
                    sp.dma_start(raw[r, slot, k, c], source).then_inc(raw_full[slot], 16)
                    at.pair = None

                walk(sp.Fori, line)
            for s in range(4):
                strip = strips[f"down{len(PARTS) - 1}", s]
                sp.wait_ge(strip_taken[strip.parity], (DEPTH - 1) * STRIPS + 2 * strip.turn + 10)
                sp.dma_start(out[0, :, s * W:(s + 1) * W].rearrange("(t p) n -> p t n", p=P),
                             x[:, :, s * W:(s + 1) * W]).then_inc(stored, 16)
            sp.wait_ge(stored, 64)

        @block.tensor
        def _(pe):
            pe.wait_ge(consts_full, 16)
            pe.wait_ge(rows_full, 64 * DEPTH)
            pe.transpose(w_bank(0, DEPTH * NG), gain_rows[0:DEPTH * NG, :], cst[0:DEPTH * NG, 0:DEPTH * NG]).then_inc(init_done, 1)
            pe.wait_ge(x_full, 16 * TT)
            with pe.Fori(0, DEPTH) as l:
                at = Place(l)

                def begin(b, key):
                    pe.wait_ge(bank_taken[b], at.bank(b, use[key][b] + 1))

                def turn(bank, tiles, source, rows=P):
                    for j, tile in enumerate(tiles):
                        for t in range(TT):
                            o = j * SEQ + t * P
                            last = pe.transpose(PS[0:rows, 4 + bank, o:o + P], source(tile, t), ident)
                    return last

                def step(s, pos, key):
                    kind = s[0]
                    if kind in ("hT", "fT"):
                        q = int(s[1])
                        if kind == "hT":
                            d = strips[f"down{len(PARTS) - 1}", q]
                            pe.wait_ge(strip_taken[d.parity], at(2 * d.turn + 10 - STRIPS, STRIPS))
                        else:
                            d = strips["wo", q]
                            pe.wait_ge(strip_taken[d.parity], at(2 * d.turn + 10, STRIPS))
                        for i, b in enumerate((2, 3)):
                            begin(b, key)
                            turn(b, (4 * q + 2 * i, 4 * q + 2 * i + 1),
                                 lambda k, t: x[:, t, k * P:(k + 1) * P]).then_inc(bank_full[b], 1)
                    elif kind == "iqT":
                        pe.wait_ge(rope_done, at(ROPE_ORDER.index(("iqrope",)) + 1, len(ROPE_ORDER)))
                        begin(2, key)
                        i = int(s[1])
                        turn(2, (2 * i, 2 * i + 1), lambda k, t: nat0[:, t, k * P:(k + 1) * P]).then_inc(bank_full[2], 1)
                    elif kind == "ikT":
                        pe.wait_ge(rope_done, at(ROPE_ORDER.index(("iknrm",)) + 1, len(ROPE_ORDER)))
                        begin(3, key)
                        turn(3, (0,), lambda k, t: ikd[:, t, :]).then_inc(bank_full[3], 1)
                    elif kind == "idx":
                        for e in (0, 1):
                            rows = slice(e * ID, (e + 1) * ID)
                            if s[1] == "0" and e == 0:
                                pe.wait_ge(bank_taken[3], at.bank(3, use[found("ikT")][3] + 2))
                                pe.wait_ge(bank_taken[2], at.bank(2, use[found("iqT", "3")][2] + 2))
                            begin(e, key)
                            for t in range(TT):
                                a, z = SEG[t]
                                last = pe.matmul(PS[:, 4 + e, a:z], T0[rows, int(s[1]), t * P:(t + 1) * P],
                                                 ikT[rows, 0:z - a], start=True, stop=True)
                            last.then_inc(bank_full[e], 1)
                    elif kind == "qkT":
                        g, i = s[1], int(s[2])
                        if g == "z":
                            for st in last_of(("zq", "zk")):
                                pe.wait_ge(strip_taken[st.parity], at(2 * st.turn + 10, STRIPS))
                        else:
                            last_rope = ("rope", "b", "1") if g == "b" else ("rope", g)
                            pe.wait_ge(rope_done, at(ROPE_ORDER.index(last_rope) + 1, len(ROPE_ORDER)))
                        begin(2, key)
                        if g == "b":
                            nat = (nat0, nat0, nat2, nat2, nat0, nat2)[i]
                            src = (lambda k, t: nat[:, t, (k % 4) * QD:(k % 4) * QD + HD]) if i < 4 else \
                                (lambda k, t: nat[:, t, HEADS * QD + (k % 2) * P:HEADS * QD + (k % 2 + 1) * P])
                        else:
                            nat = nat0 if g == "z" else nat1
                            src = lambda k, t: nat[:, t, k * P:(k + 1) * P]
                        turn(2, (2 * i, 2 * i + 1), src).then_inc(bank_full[2], 1)
                    elif kind == "latT":
                        i = int(s[1])
                        st = strips["cq"]
                        pe.wait_ge(strip_taken[st.parity], at(2 * st.turn + 10, STRIPS))
                        begin(2, key)
                        turn(2, (2 * i, 2 * i + 1), lambda k, t: nat0[:, t, k * LK:(k + 1) * LK], rows=LK).then_inc(bank_full[2], 1)
                    elif kind == "ckvT":
                        st = strips["ckr"]
                        pe.wait_ge(strip_taken[st.parity], at(2 * st.turn + 10, STRIPS))
                        begin(3, key)
                        turn(3, (0,), lambda k, t: nat2[:, t, 832:832 + KR]).then_inc(bank_full[3], 1)
                    elif kind == "qk":
                        g, m = s[1], int(s[2])
                        b = m % 2
                        if m == 0:
                            i = 5 if g == "b" else 3
                            pe.wait_ge(bank_taken[2], at.bank(2, use[found("qkT", g, str(i))][2] + 2))
                        begin(b, key)
                        for t in range(TT):
                            a, z = SEG[t]
                            o, q = PS[:, 4 + b, a:z], slice(t * P, (t + 1) * P)
                            if g == "d":
                                last = pe.matmul(o, T1[:, m, q], T1[:, HEADS + m, 0:z - a], start=True, stop=True)
                            elif g == "a":
                                rows = slice((m % 2) * SUB, (m % 2 + 1) * SUB)
                                last = pe.matmul(o, T1[rows, m // 2, q], T1[rows, HEADS + m // 2, 0:z - a], start=True, stop=True)
                            else:
                                rows = slice((m % 2) * ROT, (m % 2 + 1) * ROT)
                                pe.matmul(o, T0[:, m, q], T0[:, HEADS + m, 0:z - a], start=True, stop=False)
                                last = pe.matmul(o, Tr[rows, m // 2, q], Tr[rows, 2 + m // 2, 0:z - a], start=False, stop=True)
                        last.then_inc(bank_full[b], 1)
                    elif kind == "pT":
                        g, h = s[1], int(s[2])
                        slot = (2 * h if g == "a" else h) % 4
                        pe.wait_ge(map_done, at(MAP_DONE.index(("norm", g, s[2])) + 1, len(MAP_DONE)))
                        begin(2, key)
                        for i in range(3):
                            last = pe.transpose(PS[:, 6, i * P:(i + 1) * P], E[:, slot, i * P:(i + 1) * P], ident)
                        last.then_inc(bank_full[2], 1)
                    elif kind == "pv":
                        g, h = s[1], int(s[2])
                        v = v_even if g in ("d", "a") else v_odd
                        for st in last_of({"d": ("dv",), "a": ("av",), "z": ("zv",), "b": ("kvb0", "kvb1")}[g]):
                            pe.wait_ge(strip_taken[st.parity], at(2 * st.turn + 10, STRIPS))
                        w = writer_of(s)
                        if g == "z":
                            pe.wait_ge(zexp_done, at(ZEXP_ORDER.index(w) + 1, len(ZEXP_ORDER)))
                        else:
                            pe.wait_ge(bank_taken[2], at.bank(2, use[found(*w)][2] + 2))
                        begin(3, key)
                        pr, cols = probs[:, probs_slot(w), :], slice(h * HD, (h + 1) * HD)
                        if g == "a":
                            pe.matmul(PS[:, 7, 0:P], pr[:, 0:P], v[:, 0, cols], start=True, stop=True)
                            pe.matmul(PS[:, 7, P:2 * P], pr[:, P:2 * P], v[:, 0, cols], start=True, stop=False)
                            last = pe.matmul(PS[:, 7, P:2 * P], pr[:, 2 * P:3 * P], v[:, 1, cols], start=False, stop=True)
                        else:
                            pe.matmul(PS[:, 7, 0:SEQ], v[:, 0, cols], pr[:, 0:SEQ], start=True, stop=False)
                            last = pe.matmul(PS[:, 7, P:SEQ], v[:, 1, cols], pr[:, SEQ:3 * P], start=False, stop=True)
                        last.then_inc(bank_full[3], 1)
                    elif kind == "oT":
                        i = int(s[1])
                        pe.wait_ge(nrm_done, at(NRM_ORDER.index(("onrm",)) + 1, len(NRM_ORDER)))
                        begin(2, key)
                        turn(2, (2 * i, 2 * i + 1), lambda k, t: nat1[:, t, k * P:(k + 1) * P]).then_inc(bank_full[2], 1)
                    elif kind == "z":
                        h = int(s[1])
                        b = h % 2
                        if h == 0:
                            pe.wait_ge(bank_taken[2], at.bank(2, use[found("qkT", "z", "3")][2] + 2))
                        begin(b, key)
                        pe.matmul(PS[:, 4 + b, 0:SEQ], T0[:, HEADS + h, 0:P], T0[:, h, :], start=True, stop=True)
                        pe.matmul(PS[:, 4 + b, SEQ:3 * P], T0[:, HEADS + h, P:SEQ], T0[:, h, P:SEQ],
                                  start=True, stop=True).then_inc(bank_full[b], 1)
                    elif kind == "R":
                        h = int(s[1])
                        b = h % 2
                        pe.wait_ge(sp_done, at(SP_ORDER.index(("sp", s[1])) + 1, len(SP_ORDER)))
                        begin(b, key)
                        pe.matmul(PS[:, 4 + b, 0:3 * P], upper, E[:, h, :], start=True, stop=False)
                        pe.matmul(PS[:, 4 + b, P:SEQ], ones, E[:, h, SEQ:3 * P], start=False, stop=True).then_inc(bank_full[b], 1)
                    elif kind == "hidT":
                        i = int(s[1])
                        up = pair_strip("up", s[2], pos.strip.arg[0])
                        turns = PARTS[up.arg[0]] - 2 if s[2] == "last" else 0
                        pe.wait_ge(strip_taken[1], at.strip(2 * (up.turn + turns) + 10))
                        begin(2 + i, key)
                        turn(2 + i, (2 * i, 2 * i + 1), lambda k, t: nat1[:, t, k * P:(k + 1) * P]).then_inc(bank_full[2 + i], 1)

                def operand(strip, kt):
                    if strip.kind in ("in", "gate", "up"):
                        return hT_hi[:, kt, :], hT_lo[:, kt, :]
                    if strip.kind == "qb":
                        return mT_hi[0:LK, 4 + kt, :], mT_lo[0:LK, 4 + kt, :]
                    if strip.kind == "kvb":
                        return mT_hi[:, 8, :], mT_lo[:, 8, :]
                    if strip.kind == "wo":
                        kt = 4 * GROUP_ORDER[kt // 4] + kt % 4
                    return mT_hi[:, kt, :], mT_lo[:, kt, :]

                def operand_wait(pos):
                    strip, i = pos.strip, pos.i
                    if strip is sections[0][1][0].strip and i % 2 == 0:
                        k = found("hT", str(i // 2))
                        pe.wait_ge(bank_taken[2], at.bank(2, use[k][2] + 2))
                        pe.wait_ge(bank_taken[3], at.bank(3, use[k][3] + 2))
                    elif strip.kind == "gate" and strip.arg == (0, 0) and i % 2 == 0:
                        k = found("fT", str(i // 2))
                        pe.wait_ge(bank_taken[2], at.bank(2, use[k][2] + 2))
                        pe.wait_ge(bank_taken[3], at.bank(3, use[k][3] + 2))
                    elif strip.kind == "qb" and i == 0:
                        pe.wait_ge(bank_taken[2], at.bank(2, use[found("latT", "1")][2] + 2))
                    elif strip.kind == "kvb" and i == 0:
                        pe.wait_ge(bank_taken[3], at.bank(3, use[found("ckvT")][3] + 2))
                    elif strip.kind == "wo" and strip.arg == 0 and i % 2 == 0:
                        g = {3: "d", 1: "b", 0: "a", 2: "z"}[GROUP_ORDER[i // 2]]
                        if g == "a":
                            pe.wait_ge(bank_taken[2], at.bank(2, use[found("oT", "1")][2] + 2))
                        else:
                            pe.wait_ge(bank_taken[3], at.bank(3, use[found("pv", g, "3")][3] + 2))
                    elif strip.kind == "down" and strip.arg[1] == 0 and i == len(strip.halves) - 2:
                        for j in (0, 1):
                            k = (("hidT", str(j), "last"), False, strip.name, strip.arg[0])
                            pe.wait_ge(bank_taken[2 + j], at.bank(2 + j, use[k][2 + j] + 2))

                def line(pos, nxt, pair):
                    at.pair = pair
                    for s in pos.steps:
                        step(s, pos, key_of(s, pos))
                    strip = pos.strip
                    if pos.i == 0:
                        pe.wait_ge(strip_taken[strip.parity], at.strip(2 * strip.turn + 8))
                    operand_wait(pos)
                    n, i = len(strip.halves), pos.i
                    r, slot, _, _ = split_view(strip, i, pos.place)
                    kts, c0, c1 = strip.halves[i]
                    pe.wait_ge(lo_done, at.half(pos.place + 5))
                    for j, kt in enumerate(kts):
                        hi, lo = operand(strip, kt)
                        w1, w2 = w_hi[r, slot, j, 0:c1 - c0], w_lo[r, slot, j, 0:c1 - c0]
                        first = (i == 0 and j == 0) or strip.kind == "kvb"
                        final = (i == n - 1 and j == len(kts) - 1) or strip.kind == "kvb"
                        for t in range(TT):
                            o, q = PS[:, 2 * strip.parity + t, c0:c1], slice(t * P, (t + 1) * P)
                            pe.matmul(o, hi[:, q], w1, start=first, stop=False)
                            pe.matmul(o, hi[:, q], w2, start=False, stop=False)
                            last = pe.matmul(o, lo[:, q], w1, start=False, stop=final)
                    last.then_inc(half_used, 1)
                    at.pair = None

                walk(pe.Fori, line)

        @block.scalar
        def _(act):
            def square(s):
                for t in range(TT):
                    last = act.activation(nat0[:, t, 0:W], x[:, t, s * W:(s + 1) * W], ACT.Square, accum_out=xsq[:, t, s:s + 1])
                last.then_inc(xsq_done, 1)

            act.wait_ge(x_full, 16 * TT)
            for s in range(4):
                square(s)
                act.drain()
            with act.Fori(0, DEPTH) as l:
                at = Place(l)

                def split(strip, i, u):
                    r, slot, k, c = split_view(strip, i, u)
                    act.wait_ge(raw_full[slot], at(16 * (u // 4 + 1), 4 * HALVES, 4 * PAIR_HALVES))
                    act.wait_ge(half_used, at.half(u + 1))
                    act.activation(w_hi[r, slot, k, c], raw[r, slot, k, c], ACT.Copy).then_inc(hi_done, 1)

                def full(b, key):
                    act.wait_ge(bank_full[b], at.bank(b, use[key][b] + 1))

                def step(s, pos, key):
                    kind = s[0]
                    if kind == "E":
                        st = strips[s[1]]
                        act.wait_ge(half_used, at.half(st.last_half + 5))
                        ev = ("latss",) if st.kind in ("qb", "kvb") else ("xms", "a")
                        act.wait_ge(rinv_ready, at(ms_event[ev] + 1, MS))
                        for t in range(TT):
                            src = PS[:, 2 * st.parity + t, 0:st.width]
                            col = R_X + t if st.kind == "in" else R_LAT + t + (2 if st.kind == "kvb" else 0)
                            r = rinv[:, col:col + 1]
                            if st.kind == "kvb":
                                heads = src.rearrange("p (h c) -> p h c", h=2)
                                k = nat2[:, t, 0:HEADS * QD].rearrange("p (h c) -> p h c", h=HEADS)
                                v = v_odd[:, t, :].rearrange("p (h c) -> p h c", h=HEADS)
                                hs = slice(2 * st.arg, 2 * st.arg + 2)
                                act.activation(k[:, hs, 0:HD], heads[:, :, 0:HD], ACT.Copy, scale=r)
                                last = act.activation(v[:, hs, :], heads[:, :, HD:2 * HD], ACT.Copy, scale=r)
                            else:
                                dst = {"iq0": nat0[:, t, 0:W], "iq1": nat0[:, t, W:2 * W], "ikw": ikw[:, t, :],
                                       "dq": nat1[:, t, 0:W], "dk": nat1[:, t, W:2 * W], "dv": v_even[:, t, :],
                                       "cq": nat0[:, t, 0:QR], "ckr": nat2[:, t, 832:832 + KR + ROT],
                                       "aq": nat1[:, t, 0:W], "ak": nat1[:, t, W:2 * W], "av": v_even[:, t, :],
                                       "qb0": nat0[:, t, 0:W], "qb1": nat0[:, t, W:HEADS * QD],
                                       "zq": nat0[:, t, 0:W], "zk": nat0[:, t, W:2 * W], "zv": v_odd[:, t, :]}[st.name]
                                last = act.activation(dst, src, ACT.Copy, scale=r)
                            last.then_inc(strip_taken[st.parity], 1)
                    elif kind in ("hT", "fT"):
                        q = int(s[1])
                        if kind == "hT" and q == 0:
                            act.wait_ge(gain_ready, at(1, 1))
                        for i, b in enumerate((2, 3)):
                            full(b, key)
                            for j in (0, 1):
                                k = 4 * q + 2 * i + j
                                g = k + (KD if kind == "fT" else 0)
                                last = act.activation(hT_hi[:, k, :], PS[:, 4 + b, j * SEQ:(j + 1) * SEQ], ACT.Copy,
                                                      scale=gain[:, g:g + 1])
                            last.then_inc(high_done, 1)
                    elif kind == "latT":
                        full(2, key)
                        for j in (0, 1):
                            k = 2 * int(s[1]) + j
                            last = act.activation(mT_hi[0:LK, 4 + k, :], PS[0:LK, 6, j * SEQ:(j + 1) * SEQ], ACT.Copy,
                                                  scale=gain[0:LK, 2 * KD + k:2 * KD + k + 1])
                        last.then_inc(high_done, 1)
                    elif kind == "ckvT":
                        full(3, key)
                        act.activation(mT_hi[:, 8, :], w_bank(3, SEQ), ACT.Copy,
                                       scale=gain[:, 2 * KD + 4:2 * KD + 5]).then_inc(high_done, 1)
                    elif kind in ("iqT", "qkT"):
                        full(2, key)
                        if kind == "iqT":
                            dst = T0[:, 2 * int(s[1]):2 * int(s[1]) + 2, :]
                        else:
                            g, i = s[1], int(s[2])
                            dst = Tr[:, 2 * (i - 4):2 * (i - 4) + 2, :] if i >= 4 else \
                                (T1 if g in ("d", "a") else T0)[:, 2 * i:2 * i + 2, :]
                        act.activation(dst, w_bank(2).rearrange("p (j n) -> p j n", j=2), ACT.Copy).then_inc(bank_taken[2], 1)
                    elif kind == "ikT":
                        full(3, key)
                        act.activation(ikT[:, :], w_bank(3, SEQ), ACT.Copy).then_inc(bank_taken[3], 1)
                    elif kind == "idx":
                        for e in (0, 1):
                            head = 2 * int(s[1]) + e
                            full(e, key)
                            act.wait_ge(idx_added, at(head + 1, IH))
                            act.activation(E[:, 2 + e, :], w_bank(e, 3 * P), ACT.Relu).then_inc(relu_done, 1)
                    elif kind == "lam":
                        if s[1] == "1":
                            act.wait_ge(lam_sums, at(1, 1))
                            act.activation(lam[:, 2:4], lam[:, 0:2], ACT.Exp).then_inc(lam_exps, 1)
                    elif kind == "exp":
                        g, m = s[1], int(s[2])
                        slot = m % 4
                        scale = {"d": HD, "a": SUB, "b": QD}[g] ** -0.5
                        act.wait_ge(max_done, at(QK_ORDER.index(("qk", g, s[2])) + 1, len(QK_ORDER)))
                        for t in range(TT):
                            a, z = SEG[t]
                            last = act.activation(E[:, slot, a:z], E[:, slot, a:z], ACT.Exp, bias=stat[:, slot, 1, t:t + 1],
                                                  scale=scale, accum_out=stat[:, slot, 2, t:t + 1])
                        last.then_inc(exp_done, 1)
                    elif kind == "pT":
                        full(2, key)
                        n = PROBS_ORDER.index(s)
                        if n >= 2:
                            act.wait_ge(bank_full[3], at.bank(3, use[found(*pv_of(PROBS_ORDER[n - 2]))][3] + 1))
                        act.activation(probs[:, n % 2, :], w_bank(2, 3 * P), ACT.Copy).then_inc(bank_taken[2], 1)
                    elif kind == "pv":
                        g, h = s[1], int(s[2])
                        full(3, key)
                        if g == "a":
                            act.activation(nat1[:, :, h * HD:(h + 1) * HD], w_bank(3, SEQ).rearrange("p (t d) -> p t d", t=TT),
                                           ACT.Copy).then_inc(bank_taken[3], 1)
                        else:
                            act.activation(mT_hi[:, FIRST_TILE[g] + h, :], w_bank(3, SEQ), ACT.Copy).then_inc(high_done, 1)
                    elif kind == "oT":
                        full(2, key)
                        i = int(s[1])
                        act.activation(mT_hi[:, 2 * i:2 * i + 2, :], w_bank(2).rearrange("p (j n) -> p j n", j=2),
                                       ACT.Copy).then_inc(high_done, 1)
                    elif kind == "z":
                        h = int(s[1])
                        b = h % 2
                        full(b, key)
                        logits = nat2[:, :, :].rearrange("p t n -> p (t n)")[:, h * 3 * P:(h + 1) * 3 * P]
                        act.activation(logits, w_bank(b, 3 * P), ACT.Copy, scale=HD ** -0.5)
                        act.activation(E[:, h, :], w_bank(b, 3 * P), ACT.Abs, scale=HD ** -0.5).then_inc(bank_taken[b], 1)
                        act.drain()
                        act.activation(E[:, h, :], E[:, h, :], ACT.Exp, scale=-1.0)
                    elif kind == "zln":
                        act.drain()
                        act.activation(E[:, :, :], E[:, :, :], ACT.Ln, bias=1.0).then_inc(ln_done, 1)
                    elif kind == "zexp":
                        h = int(s[1])
                        n = PROBS_ORDER.index(s)
                        logits = nat2[:, :, :].rearrange("p t n -> p (t n)")[:, h * 3 * P:(h + 1) * 3 * P]
                        act.wait_ge(z_done, at(Z_ORDER.index(("R", s[1])) + 1, len(Z_ORDER)))
                        if n >= 2:
                            act.wait_ge(bank_full[3], at.bank(3, use[found(*pv_of(PROBS_ORDER[n - 2]))][3] + 1))
                        act.activation(probs[:, n % 2, :], logits, ACT.Exp).then_inc(zexp_done, 1)
                    elif kind == "xsq":
                        d = strips[s[1], int(s[2])]
                        act.drain()
                        act.wait_ge(strip_taken[d.parity], at(2 * d.turn + 10, STRIPS))
                        square(int(s[2]))
                    elif kind == "G":
                        gate = pair_strip("gate", s[1], pos.strip.arg[0])
                        act.wait_ge(half_used, at.half(gate.last_half + 5))
                        act.wait_ge(rinv_ready, at(ms_event["xms", "f"] + 1, MS))
                        for t in range(TT):
                            act.activation(nat0[:, t, 0:W], PS[:, 2 * gate.parity + t, :], ACT.Silu,
                                           scale=rinv[:, R_XF + t:R_XF + t + 1]).then_inc(strip_taken[gate.parity], 1)
                    elif kind == "hidT":
                        i = int(s[1])
                        b = 2 + i
                        full(b, key)
                        part = pos.strip.arg[0]
                        if s[2] == "last":
                            k = 4 * (PARTS[part] - 1) + 2 * i
                            dst = mT_hi[:, k:k + 2, :]
                        else:
                            dst = mT_hi[:, bass.ds(at.pair * 4 + 2 * i, 2), :]
                        act.activation(dst, w_bank(b).rearrange("p (j n) -> p j n", j=2), ACT.Copy).then_inc(high_done, 1)

                def line(pos, nxt, pair):
                    at.pair = pair
                    if pos is sections[0][1][0]:
                        for by in range(LEAD):
                            split(*ahead(0, 0, by))
                    if nxt is not None:
                        split(*nxt)
                    for s in pos.steps:
                        step(s, pos, key_of(s, pos))
                    at.pair = None

                walk(act.Fori, line)
                for s in tail_steps:
                    step(s, None, None)

        @block.vector
        def _(dve):
            dve.sem_inc(lo_done, 4)
            dve.sem_inc(half_used, 4)
            for p in (0, 1):
                dve.sem_inc(strip_taken[p], 8)
            dve.sem_inc(small_free, 1)
            dve.sem_inc(idx_added, 2)
            dve.wait_ge(init_done, 2)
            dve.tensor_copy(gain_all[:, :], w_bank(0, DEPTH * NG))
            dve.drain()
            for b in range(4):
                dve.sem_inc(bank_taken[b], 1)
            dve.wait_ge(consts_full, 16)
            with dve.Fori(0, DEPTH) as l:
                at = Place(l)
                dve.drain()
                dve.tensor_copy(gain[:, :], gain_all[:, bass.ds(l * NG, NG)]).then_inc(gain_ready, 1)
                dve.tensor_copy(lam_init[:, :], cst[:, bass.ds(l * 2 + C_LAM, 2)])
                dve.drain()

                def split(strip, i, u):
                    r, slot, k, c = split_view(strip, i, u)
                    dve.wait_ge(hi_done, at.half(u + 1))
                    dve.tensor_tensor(w_lo[r, slot, k, c], raw[r, slot, k, c], f(w_hi[r, slot, k, c]),
                                      ALU.subtract).then_inc(lo_done, 1)

                def high_ready(key, i=0):
                    dve.wait_ge(high_done, at.high(high[key] + i + 1))

                def squares(src, n, width, col, width0=0):
                    for h in range(n):
                        v = src[:, h * width:(h + 1) * width]
                        dve.tensor_tensor_reduce(out=junk[:, h * width:(h + 1) * width], in0=v, in1=v, scale=1.0, scalar=0.0,
                                                 op0=ALU.mult, op1=ALU.add, accum_out=mean[:, col + h:col + h + 1])

                def to_mean(step, width):
                    col, n = MS_COLS[step]
                    dve.drain()
                    m = mean[:, col:col + n]
                    return dve.tensor_scalar(m, m, 1.0 / width, EPS, ALU.mult, ALU.add)

                def roots(step):
                    dve.wait_ge(rinv_ready, at(ms_event[step] + 1, MS))

                def scale_heads(src, n, width, col, g, goff):
                    for h in range(n):
                        v = src[:, h * width:(h + 1) * width]
                        last = dve.scalar_tensor_tensor(v, v, rinv[:, col + h:col + h + 1], g[:, goff:goff + width], ALU.mult, ALU.mult)
                    return last

                def step(s, pos, key):
                    kind = s[0]
                    if kind in ("hT", "fT"):
                        q = int(s[1])
                        for i, b in enumerate((2, 3)):
                            high_ready(key, i)
                            for j in (0, 1):
                                k = 4 * q + 2 * i + j
                                g = k + (KD if kind == "fT" else 0)
                                last = dve.scalar_tensor_tensor(hT_lo[:, k, :], PS[:, 4 + b, j * SEQ:(j + 1) * SEQ], gain[:, g:g + 1],
                                                                f(hT_hi[:, k, :]), ALU.mult, ALU.subtract)
                            last.then_inc(bank_taken[b], 1)
                    elif kind == "latT":
                        high_ready(key)
                        for j in (0, 1):
                            k = 2 * int(s[1]) + j
                            last = dve.scalar_tensor_tensor(mT_lo[0:LK, 4 + k, :], PS[0:LK, 6, j * SEQ:(j + 1) * SEQ],
                                                            gain[0:LK, 2 * KD + k:2 * KD + k + 1], f(mT_hi[0:LK, 4 + k, :]),
                                                            ALU.mult, ALU.subtract)
                        last.then_inc(bank_taken[2], 1)
                    elif kind == "ckvT":
                        high_ready(key)
                        dve.scalar_tensor_tensor(mT_lo[:, 8, :], w_bank(3, SEQ), gain[:, 2 * KD + 4:2 * KD + 5], f(mT_hi[:, 8, :]),
                                                 ALU.mult, ALU.subtract).then_inc(bank_taken[3], 1)
                    elif kind == "xms":
                        fours = {"a": 1, "f": 2}[s[1]]
                        col = MS_COLS[s][0]
                        dve.wait_ge(xsq_done, at(4 * fours, 8))
                        dve.tensor_reduce(mean[:, col:col + TT], xsq[:, :, :], AX.X, ALU.add)
                        to_mean(s, D).then_inc(ms_ready, 1)
                    elif kind == "lam":
                        if s[1] == "0":
                            dve.wait_ge(small_full, at(96, 96))
                            for i in (0, 1):
                                a = S_LAM + 2 * i * SUB
                                dve.tensor_tensor_reduce(out=junk[:, i * SUB:(i + 1) * SUB], in0=small[:, a:a + SUB],
                                                         in1=small[:, a + SUB:a + 2 * SUB], scale=1.0, scalar=0.0,
                                                         op0=ALU.mult, op1=ALU.add, accum_out=lam[:, i:i + 1])
                            dve.drain()
                            sub = small[:, S_SUBLN:S_SUBLN + HD]
                            dve.tensor_scalar(sub, sub, lam_init[:, 1:2], None, ALU.mult).then_inc(lam_sums, 1)
                        elif s[1] == "2":
                            dve.wait_ge(lam_exps, at(1, 1))
                            dve.tensor_tensor(lam[:, 5:6], lam[:, 3:4], lam[:, 2:3], ALU.subtract)
                            dve.drain()
                            dve.tensor_tensor(lam[:, 4:5], lam[:, 5:6], lam_init[:, 0:1], ALU.subtract)
                            dve.drain()
                    elif kind == "ikss":
                        dve.drain()
                        st = strips["ikw"]
                        dve.wait_ge(strip_taken[st.parity], at(2 * st.turn + 10, STRIPS))
                        for t in range(TT):
                            v = ikw[:, t, 0:ID]
                            dve.tensor_tensor_reduce(out=junk[:, t * ID:(t + 1) * ID], in0=v, in1=v, scale=1.0, scalar=0.0,
                                                     op0=ALU.mult, op1=ALU.add, accum_out=mean[:, R_IK + t:R_IK + t + 1])
                        to_mean(s, ID).then_inc(ms_ready, 1)
                    elif kind == "iknrm":
                        roots(("ikss",))
                        for t in range(TT):
                            dve.scalar_tensor_tensor(ikd[:, t, 0:ID], ikw[:, t, 0:ID], rinv[:, R_IK + t:R_IK + t + 1],
                                                     small[:, S_IDX:S_IDX + ID], ALU.mult, ALU.mult)
                        dve.tensor_scalar(iw[:, :, :], ikw[:, :, ID:ID + IH], ID ** -0.5 * IH ** -0.5, None, ALU.mult).then_inc(nrm_done, 1)
                    elif kind == "idx":
                        dve.drain()
                        for e in (0, 1):
                            head = 2 * int(s[1]) + e
                            acc = (picks, taken)[e]
                            dve.wait_ge(relu_done, at(head + 1, IH))
                            for t in range(TT):
                                a, z = SEG[t]
                                r, w = E[:, 2 + e, a:z], iw[:, t, head:head + 1]
                                if s[1] == "0":
                                    last = dve.tensor_scalar(acc[:, a:z], r, w, None, ALU.mult)
                                else:
                                    last = dve.scalar_tensor_tensor(acc[:, a:z], r, w, acc[:, a:z], ALU.mult, ALU.add)
                            last.then_inc(idx_added, 1)
                            dve.sem_inc(bank_taken[e], 1)
                    elif kind == "topk":
                        if s[1] == "0":
                            dve.drain()
                            dve.tensor_tensor(taken[:, :], taken[:, :], picks[:, :], ALU.add)
                            dve.drain()
                            dve.tensor_tensor(taken[:, 0:P], taken[:, 0:P], bias_t[:, P:2 * P], ALU.add)
                            dve.tensor_tensor(taken[:, P:3 * P], taken[:, P:3 * P], bias_t, ALU.add)
                        dve.drain()
                        for t in range(TT):
                            a, z = SEG[t]
                            dve.max(best[:, t, :], taken[:, a:z])
                        dve.drain()
                        for t in range(TT):
                            a, z = SEG[t]
                            dve.match_replace(taken[:, a:z], best[:, t, :], taken[:, a:z], TAKEN)
                    elif kind == "sel":
                        dve.drain()
                        dve.tensor_scalar(picks[:, :], taken[:, :], TAKEN / 2, MASKED, ALU.is_gt, ALU.mult)
                        dve.drain()
                        dve.tensor_tensor(picks[:, 0:P], picks[:, 0:P], bias_t[:, P:2 * P], ALU.add)
                        dve.tensor_tensor(picks[:, P:3 * P], picks[:, P:3 * P], bias_t, ALU.add)
                        dve.drain()
                    elif kind == "ss":
                        g, t = s[1], int(s[2])
                        dve.drain()
                        for st in last_of({"d": ("dq", "dk"), "a": ("aq", "ak"), "b": ("qb0", "qb1", "kvb0", "kvb1")}[g]):
                            dve.wait_ge(strip_taken[st.parity], at(2 * st.turn + 10, STRIPS))
                        if g == "d":
                            squares(nat1[:, t, :], 2 * HEADS, HD, R_D + t * 8)
                        elif g == "a":
                            squares(nat1[:, t, :], 4 * HEADS, SUB, R_A + t * 16)
                        else:
                            squares(nat0[:, t, :], HEADS, QD, R_B + t * 8)
                            dve.drain()
                            squares(nat2[:, t, :], HEADS, QD, R_B + t * 8 + 4)
                        if t == 1:
                            to_mean(s, {"d": HD, "a": SUB, "b": QD}[g]).then_inc(ms_ready, 1)
                    elif kind == "nrm":
                        g, t = s[1], int(s[2])
                        dve.drain()
                        roots(("ss", g, "1"))
                        if g == "d":
                            scale_heads(nat1[:, t, 0:W], HEADS, HD, R_D + t * 8, small, S_DSA)
                            last = scale_heads(nat1[:, t, W:2 * W], HEADS, HD, R_D + t * 8 + 4, small, S_DSA + HD)
                        elif g == "a":
                            scale_heads(nat1[:, t, 0:W], 2 * HEADS, SUB, R_A + t * 16, small, S_DIFF)
                            last = scale_heads(nat1[:, t, W:2 * W], 2 * HEADS, SUB, R_A + t * 16 + 8, small, S_DIFF + SUB)
                        else:
                            scale_heads(nat0[:, t, :], HEADS, QD, R_B + t * 8, small, S_MLA)
                            last = scale_heads(nat2[:, t, :], HEADS, QD, R_B + t * 8 + 4, small, S_MLA + QD)
                        if t == 1:
                            last.then_inc(nrm_done, 1)
                    elif kind == "latss":
                        dve.drain()
                        for st in last_of(("cq", "ckr")):
                            dve.wait_ge(strip_taken[st.parity], at(2 * st.turn + 10, STRIPS))
                        for t in range(TT):
                            for src, o, c in ((nat0[:, t, 0:QR], 0, R_LAT + t), (nat2[:, t, 832:832 + KR], QR, R_LAT + 2 + t)):
                                n = src.shape[1]
                                j = junk[:, o:o + n] if t == 0 else junk[:, o:o + n]
                                if t == 1 and o == 0:
                                    dve.drain()
                                dve.tensor_tensor_reduce(out=j, in0=src, in1=src, scale=1.0, scalar=0.0, op0=ALU.mult,
                                                         op1=ALU.add, accum_out=mean[:, c:c + 1])
                        dve.drain()
                        dve.tensor_scalar(mean[:, R_LAT:R_LAT + 2], mean[:, R_LAT:R_LAT + 2], 1.0 / QR, EPS, ALU.mult, ALU.add)
                        dve.tensor_scalar(mean[:, R_LAT + 2:R_LAT + 4], mean[:, R_LAT + 2:R_LAT + 4], 1.0 / KR, EPS,
                                          ALU.mult, ALU.add).then_inc(ms_ready, 1)
                    elif kind == "krcp":
                        for st in last_of(("ckr", "kvb0", "kvb1")):
                            dve.wait_ge(strip_taken[st.parity], at(2 * st.turn + 10, STRIPS))
                        for t in range(TT):
                            k = nat2[:, t, 0:HEADS * QD].rearrange("p (h c) -> p h c", h=HEADS)
                            kr = nat2[:, t, 832 + KR:832 + KR + ROT].unsqueeze(1).to_broadcast([P, HEADS, ROT])
                            dve.tensor_copy(k[:, :, HD:QD], kr)
                        dve.drain()
                    elif kind == "qk":
                        g, m = s[1], int(s[2])
                        b, slot = m % 2, m % 4
                        scale = {"d": HD, "a": SUB, "b": QD}[g] ** -0.5
                        reader = slot_reader(s)
                        dve.drain()
                        if reader is not None:
                            dve.wait_ge(bank_full[2], at.bank(2, use[found(*reader)][2] + 1))
                        dve.wait_ge(bank_full[b], at.bank(b, use[key][b] + 1))
                        dve.memset(stat[:, slot, 0, :], LOWEST)
                        dve.drain()
                        for t in range(TT):
                            a, z = SEG[t]
                            mask = picks[:, a:z] if g == "d" else (bias_t[:, P:2 * P] if t == 0 else bias_t)
                            last = dve.tensor_tensor_reduce(out=E[:, slot, a:z], in0=PS[:, 4 + b, a:z], in1=mask, scale=1.0,
                                                            scalar=LOWEST, op0=ALU.add, op1=ALU.max,
                                                            accum_out=stat[:, slot, 0, t:t + 1])
                        last.then_inc(bank_taken[b], 1)
                        dve.drain()
                        dve.tensor_scalar(stat[:, slot, 1, :], stat[:, slot, 0, :], -scale, None, ALU.mult).then_inc(max_done, 1)
                    elif kind == "norm":
                        g, h = s[1], int(s[2])
                        if g == "a":
                            dve.wait_ge(exp_done, at(EXP_ORDER.index(("exp", "a", str(2 * h + 1))) + 1, len(EXP_ORDER)))
                            e1, e2 = (2 * h) % 4, (2 * h + 1) % 4
                            dve.reciprocal(stat[:, e1, 3, :], stat[:, e1, 2, :])
                            dve.reciprocal(stat[:, e2, 3, :], stat[:, e2, 2, :])
                            dve.drain()
                            dve.tensor_scalar(stat[:, e2, 3, :], stat[:, e2, 3, :], lam[:, 4:5], None, ALU.mult)
                            for t in range(TT):
                                a, z = SEG[t]
                                dve.tensor_scalar(E[:, e1, a:z], E[:, e1, a:z], stat[:, e1, 3, t:t + 1], None, ALU.mult)
                            dve.drain()
                            for t in range(TT):
                                a, z = SEG[t]
                                last = dve.scalar_tensor_tensor(E[:, e1, a:z], E[:, e2, a:z], stat[:, e2, 3, t:t + 1],
                                                                E[:, e1, a:z], ALU.mult, ALU.add)
                        else:
                            dve.wait_ge(exp_done, at(EXP_ORDER.index(("exp", g, s[2])) + 1, len(EXP_ORDER)))
                            slot = h % 4
                            dve.reciprocal(stat[:, slot, 3, :], stat[:, slot, 2, :])
                            dve.drain()
                            for t in range(TT):
                                a, z = SEG[t]
                                last = dve.tensor_scalar(E[:, slot, a:z], E[:, slot, a:z], stat[:, slot, 3, t:t + 1], None, ALU.mult)
                        last.then_inc(map_done, 1)
                    elif kind == "pv":
                        g, h = s[1], int(s[2])
                        if g != "a":
                            high_ready(key)
                            k = FIRST_TILE[g] + h
                            dve.tensor_tensor(mT_lo[:, k, :], w_bank(3, SEQ), f(mT_hi[:, k, :]), ALU.subtract).then_inc(bank_taken[3], 1)
                    elif kind == "oss":
                        dve.drain()
                        dve.wait_ge(bank_taken[3], at.bank(3, use[found("pv", "a", "3")][3] + 2))
                        for t in range(TT):
                            o = t * 4 * HD
                            for h in range(HEADS):
                                v = nat1[:, t, h * HD:(h + 1) * HD]
                                dve.tensor_tensor_reduce(out=junk[:, o + h * HD:o + (h + 1) * HD], in0=v, in1=v, scale=1.0, scalar=0.0,
                                                         op0=ALU.mult, op1=ALU.add, accum_out=mean[:, R_O + 4 * t + h:R_O + 4 * t + h + 1])
                        to_mean(s, HD).then_inc(ms_ready, 1)
                    elif kind == "onrm":
                        roots(("oss",))
                        for t in range(TT):
                            last = scale_heads(nat1[:, t, 0:GW], HEADS, HD, R_O + 4 * t, small, S_SUBLN)
                        last.then_inc(nrm_done, 1)
                        dve.drain()
                        dve.sem_inc(small_free, 1)
                    elif kind == "oT":
                        high_ready(key)
                        i = int(s[1])
                        dve.tensor_tensor(mT_lo[:, 2 * i:2 * i + 2, :], w_bank(2).rearrange("p (j n) -> p j n", j=2),
                                          f(mT_hi[:, 2 * i:2 * i + 2, :]), ALU.subtract).then_inc(bank_taken[2], 1)
                    elif kind == "sp":
                        h = int(s[1])
                        logits = nat2[:, :, :].rearrange("p t n -> p (t n)")[:, h * 3 * P:(h + 1) * 3 * P]
                        dve.wait_ge(ln_done, at(1, 1))
                        dve.scalar_tensor_tensor(E[:, h, :], logits, 0.0, E[:, h, :], ALU.max, ALU.add)
                        dve.drain()
                        dve.tensor_tensor(E[:, h, 0:P], E[:, h, 0:P], strict01, ALU.mult)
                        dve.tensor_tensor(E[:, h, SEQ:3 * P], E[:, h, SEQ:3 * P], strict01, ALU.mult).then_inc(sp_done, 1)
                    elif kind == "R":
                        h = int(s[1])
                        b = h % 2
                        logits = nat2[:, :, :].rearrange("p t n -> p (t n)")[:, h * 3 * P:(h + 1) * 3 * P]
                        dve.wait_ge(bank_full[b], at.bank(b, use[key][b] + 1))
                        dve.tensor_tensor(logits, logits, w_bank(b, 3 * P), ALU.subtract).then_inc(bank_taken[b], 1)
                        dve.drain()
                        dve.tensor_tensor(logits[:, 0:P], logits[:, 0:P], strict_neg, ALU.add)
                        dve.tensor_tensor(logits[:, SEQ:3 * P], logits[:, SEQ:3 * P], strict_neg, ALU.add).then_inc(z_done, 1)
                    elif kind == "X":
                        st = strips[s[1], int(s[2])]
                        q = int(s[2])
                        dve.drain()
                        dve.wait_ge(half_used, at.half(st.last_half + 5))
                        for t in range(TT):
                            v = x[:, t, q * W:(q + 1) * W]
                            dve.tensor_tensor(v, v, PS[:, 2 * st.parity + t, :], ALU.add).then_inc(strip_taken[st.parity], 1)
                    elif kind == "U":
                        part = pos.strip.arg[0]
                        gate, up = pair_strip("gate", s[1], part), pair_strip("up", s[1], part)
                        turns = PARTS[part] - 2 if s[1] == "last" else 0
                        dve.wait_ge(half_used, at.half(up.last_half + PAIR_HALVES * turns + 5))
                        dve.wait_ge(strip_taken[0], at.strip(2 * (gate.turn + turns) + 10))
                        for t in range(TT):
                            dve.scalar_tensor_tensor(nat1[:, t, 0:W], PS[:, 2 * up.parity + t, :], rinv[:, R_XF + t:R_XF + t + 1],
                                                     nat0[:, t, 0:W], ALU.mult, ALU.mult).then_inc(strip_taken[up.parity], 1)
                    elif kind == "hidT":
                        i = int(s[1])
                        high_ready(key)
                        part = pos.strip.arg[0]
                        if s[2] == "last":
                            k = 4 * (PARTS[part] - 1) + 2 * i
                            hi, lo = mT_hi[:, k:k + 2, :], mT_lo[:, k:k + 2, :]
                        else:
                            ks = bass.ds(at.pair * 4 + 2 * i, 2)
                            hi, lo = mT_hi[:, ks, :], mT_lo[:, ks, :]
                        dve.tensor_tensor(lo, w_bank(2 + i).rearrange("p (j n) -> p j n", j=2), f(hi), ALU.subtract).then_inc(bank_taken[2 + i], 1)

                def line(pos, nxt, pair):
                    at.pair = pair
                    if pos is sections[0][1][0]:
                        for by in range(LEAD):
                            split(*ahead(0, 0, by))
                    if nxt is not None:
                        split(*nxt)
                    for s in pos.steps:
                        step(s, pos, key_of(s, pos))
                    at.pair = None

                walk(dve.Fori, line)
                for s in tail_steps:
                    step(s, None, None)

        @block.gpsimd
        def _(pool):
            pool.memset(gain_rows, 0.0).then_inc(init_done, 1)
            pool.memset(minus_half[:, :], -0.5)
            pool.drain()
            pool.wait_ge(consts_full, 16)
            with pool.Fori(0, DEPTH) as l:
                at = Place(l)

                def rotate(x1, x2, y1, y2, half, heads):
                    cos, sin = (c.unsqueeze(2).to_broadcast([P, TT, heads, half]) for c in cos_sin(half))
                    n = heads * half
                    t0, t1, t2 = (rtmp[:, i, 0:TT * n].rearrange("p (t h c) -> p t h c", t=TT, h=heads) for i in range(3))
                    pool.tensor_tensor(t0, x1, cos, ALU.mult)
                    pool.tensor_tensor(t1, x2, sin, ALU.mult)
                    pool.tensor_tensor(t2, x1, sin, ALU.mult)
                    pool.drain()
                    pool.tensor_tensor(x2, x2, cos, ALU.mult)
                    pool.tensor_tensor(y1, t0, t1, ALU.subtract)
                    pool.drain()
                    return pool.tensor_tensor(y2, x2, t2, ALU.add)

                def step(s):
                    kind = s[0]
                    if kind in ("iqrope", "iknrm", "rope"):
                        pool.drain()
                    if s in ms_event:
                        col, n = MS_COLS[s]
                        pool.wait_ge(ms_ready, at(ms_event[s] + 1, MS))
                        pool.tensor_tensor(rinv[:, col:col + n], mean[:, col:col + n], minus_half[:, 0:n], ALU.pow).then_inc(rinv_ready, 1)
                    elif kind == "iqrope":
                        for st in last_of(("iq0", "iq1")):
                            pool.wait_ge(strip_taken[st.parity], at(2 * st.turn + 10, STRIPS))
                        v = nat0[:, :, :].rearrange("p t (h c) -> p t h c", h=IH)
                        rotate(v[:, :, :, 0:8], v[:, :, :, 8:16], v[:, :, :, 0:8], v[:, :, :, 8:16], 8, IH).then_inc(rope_done, 1)
                    elif kind == "iknrm":
                        pool.wait_ge(nrm_done, at(NRM_ORDER.index(s) + 1, len(NRM_ORDER)))
                        v = ikd[:, :, :].rearrange("p t (h c) -> p t h c", h=2)[:, :, 0:1, :]
                        rotate(v[:, :, :, 0:8], v[:, :, :, 8:16], v[:, :, :, 0:8], v[:, :, :, 8:16], 8, 1)
                        pool.drain()
                        pool.tensor_copy(ikd[:, :, ID:2 * ID], ikd[:, :, 0:ID]).then_inc(rope_done, 1)
                    elif kind == "rope":
                        g = s[1]
                        pool.wait_ge(nrm_done, at(NRM_ORDER.index(("nrm", g, "1")) + 1, len(NRM_ORDER)))
                        if g == "b":
                            nat = (nat0, nat2)[int(s[2])]
                            v = nat[:, :, 0:HEADS * QD].rearrange("p t (h c) -> p t h c", h=HEADS)
                            y = nat[:, :, HEADS * QD:HEADS * (QD + ROT)].rearrange("p t (h c) -> p t h c", h=HEADS)
                            last = rotate(v[:, :, :, HD:HD + 32], v[:, :, :, HD + 32:QD], y[:, :, :, 0:32], y[:, :, :, 32:64], 32, HEADS)
                            if s[2] == "1":
                                last.then_inc(rope_done, 1)
                        else:
                            n, half = (2 * HEADS, 16) if g == "d" else (4 * HEADS, 8)
                            v = nat1[:, :, :].rearrange("p t (h c) -> p t h c", h=n)
                            rotate(v[:, :, :, 0:half], v[:, :, :, half:2 * half], v[:, :, :, 0:half], v[:, :, :, half:2 * half],
                                   half, n).then_inc(rope_done, 1)

                for section in sections:
                    if section[0] == "line":
                        for pos in section[1]:
                            for s in pos.steps:
                                step(s)


_INS = ["x", "attn_norm", "w_in", "diff_qk_norm", "diff_lambda", "diff_subln", "mla_q_a_norm", "mla_wq_b", "mla_kv_a_norm",
        "mla_wkv_b", "mla_qk_norm", "dsa_qk_norm", "idx_k_norm", "w_o", "ffn_norm", "w_gate", "w_up", "w_down"]
_OUT = ((1, 256, 2048), "float32")


def _constants():
    import math
    import numpy as np
    P, MASKED = 128, -1e30
    r, c = np.arange(P)[:, None], np.arange(P)[None, :]
    parts = [np.eye(P), np.zeros((P, P)), np.where(c <= r, 0.0, MASKED), np.where(r < c, 1.0, 0.0),
             np.where(r < c, 0.0, MASKED), np.where(r >= c, 1.0, 0.0), np.ones((P, P))]
    for half in (8, 16, 32):
        inv = np.float32(500000.0) ** (-np.arange(half, dtype=np.float32) * np.float32(2.0) / np.float32(2 * half))
        ang = np.arange(2 * P, dtype=np.float32)[:, None] * inv.astype(np.float32)[None, :]
        for fn in (np.cos, np.sin):
            table = fn(ang.astype(np.float64))
            parts.append(table.reshape(2, P, half).transpose(1, 0, 2).reshape(P, 2 * half))
    for layer in range(2):
        start = 0.8 - 0.6 * math.exp(-0.3 * layer)
        parts.append(np.tile([[start, 1.0 - start]], (P, 1)))
    return np.ascontiguousarray(np.concatenate(parts, axis=1).astype(np.float32))


def kernel(**inputs):
    import numpy as _np
    import concourse.bacc as _bacc
    from concourse import mybir as _mybir
    from concourse.bass_utils import run_bass_kernel_spmd as _run

    nc = _bacc.Bacc("TRN2", target_bir_lowering=False, num_devices=1)
    arrays, args = {}, []
    for name in _INS + ["constants"]:
        a = _constants() if name == "constants" else _np.ascontiguousarray(inputs[name])
        arrays[f"in_{name}_dram"] = a
        args.append(nc.dram_tensor(f"in_{name}_dram", a.shape, _mybir.dt.from_np(a.dtype), kind="ExternalInput").ap())
    args.append(nc.dram_tensor("out_0_dram", _OUT[0], _mybir.dt.from_np(_np.dtype(_OUT[1])), kind="ExternalOutput").ap())
    trunk_kernel(nc, *args)
    r = _run(nc, [arrays], core_ids=[0])
    return r.results[0]["out_0_dram"]
```

```python
import concourse.bass as bass
from concourse import mybir
from contextlib import ExitStack

ATTENTION = [
    ("iq0", ["lam 0",
            "X down2 3; xsq down2 3",
            "lam 1; lam 2; xms a",
            "hT 3",
            "",
            "",
            "",
            ""]),
    ("iq1", ["",
            "E iq0",
            "",
            "",
            "",
            "",
            "",
            ""]),
    ("dk", ["",
           "E iq1; iqrope",
           "",
           "",
           "iqT 0",
           "iqT 1",
           "iqT 2",
           ""]),
    ("ikw", ["",
            "",
            "",
            "",
            "",
            "",
            "",
            "E dk"]),
    ("cq", ["E ikw; ikss; iqT 3",
           "iknrm",
           "",
           "",
           "ikT",
           "idx 0",
           "",
           ""]),
    ("ckr", ["",
            "",
            "",
            "",
            "",
            "",
            "",
            "E cq; idx 1"]),
    ("dq", ["E ckr; latss",
           "latT 0; ckvT; idx 2",
           "",
           "latT 1; idx 3",
           "",
           "idx 4",
           "",
           ""]),
    ("qb1", ["",
            "E dq; idx 5"]),
    ("qb0", ["E qb1; ss d 0",
            "idx 6; ss d 1"]),
    ("dv", ["E qb0",
           "idx 7; nrm d 0",
           "nrm d 1; rope d",
           "",
           "topk 0",
           "topk 1",
           "topk 2",
           "qkT d 0; topk 3"]),
    ("aq", ["E dv; qkT d 1; topk 4; topk 5",
           "qkT d 2; topk 6",
           "qkT d 3; topk 7; sel",
           "",
           "",
           "qk d 0",
           "qk d 1",
           "exp d 0; norm d 0; qk d 2; exp d 1"]),
    ("kvb0", ["",
             ""]),
    ("kvb1", ["E aq",
             "E kvb0; norm d 1; pT d 0; qk d 3; exp d 2"]),
    ("ak", ["E kvb1; norm d 2",
           "pT d 1; krcp; exp d 3; norm d 3; pv d 0",
           "pT d 2; ss b 0",
           "pv d 1; pT d 3; ss b 1",
           "",
           "pv d 2; nrm b 0",
           "pv d 3; nrm b 1; rope b 0; rope b 1",
           ""]),
    ("zq", ["",
           "E ak; ss a 0",
           "ss a 1",
           "",
           "",
           "qkT b 0",
           "qkT b 1; nrm a 0",
           "qkT b 2; nrm a 1; rope a"]),
    ("zk", ["qkT b 3",
           "qkT b 4",
           "qkT b 5; E zq",
           "qkT a 0; qk b 0; qkT a 1; exp b 0",
           "norm b 0; qkT a 2; qk b 1; qkT a 3",
           "exp b 1; pT b 0; norm b 1; qk b 2; pv b 0; pT b 1; exp b 2",
           "norm b 2; qk b 3; pv b 1",
           "exp b 3; pT b 2; norm b 3"]),
    ("av", ["E zk; pT b 3; pv b 2",
           "pv b 3; qk a 0; qkT z 0; exp a 0",
           "qk a 1; qkT z 1",
           "exp a 1; qk a 2; norm a 0; qkT z 2; exp a 2",
           "qk a 3; pT a 0",
           "exp a 3; qk a 4; qkT z 3; exp a 4; norm a 1",
           "qk a 5; pT a 1",
           "exp a 5; qk a 6; norm a 2"]),
    ("zv", ["exp a 6; E av; qk a 7",
           "pv a 0; exp a 7; pT a 2",
           "pv a 1; norm a 3",
           "pv a 2; pT a 3",
           "z 0; pv a 3",
           "z 1; oss",
           "onrm; z 2",
           "z 3; oT 0"]),
    ("wo0", ["E zv",
            "zln; oT 1",
            "sp 0",
            "sp 1"]),
    ("wo1", ["R 0; sp 2",
            "sp 3",
            "R 1; zexp 0; pv z 0",
            "zexp 1; R 2; pv z 1; zexp 2"]),
    ("wo0", ["R 3; pv z 2; zexp 3",
            "pv z 3",
            "",
            ""]),
    ("wo1", ["X wo 0; xsq wo 0",
            "",
            "fT 0",
            ""]),
    ("wo2", ["X wo 1; xsq wo 1",
            "",
            "fT 1",
            "",
            "",
            "",
            "",
            ""]),
    ("wo3", ["X wo 2; xsq wo 2",
            "",
            "fT 2",
            "",
            "",
            "",
            "",
            ""]),
]


def trunk_kernel(nc, x_in, attn_norm, w_in, diff_qk_norm, diff_lambda, diff_subln, mla_q_a_norm, mla_wq_b,
                 mla_kv_a_norm, mla_wkv_b, mla_qk_norm, dsa_qk_norm, idx_k_norm, w_o, ffn_norm, w_gate, w_up,
                 w_down, constants, out):
    F32, F32R, BF16 = mybir.dt.float32, mybir.dt.float32r, mybir.dt.bfloat16
    ALU, ACT, AX = mybir.AluOpType, mybir.ActivationFunctionType, mybir.AxisListType

    _, SEQ, D = x_in.shape
    DEPTH = w_in.shape[0]
    HIDDEN = w_gate.shape[2]
    P = 128
    TT = SEQ // P
    W = 512
    KD = D // P
    HD, HEADS, GW = 128, 4, 512
    SUB = HD // 2
    ROT = 64
    QD = HD + ROT
    QR, KR = mla_wq_b.shape[1], mla_wkv_b.shape[1]
    LK = QR // 4
    IH, ID = 16, 64
    TOPK = SEQ // 4
    EPS = 1e-6
    MASKED, TAKEN, LOWEST = -1e30, -3e38, -3.3e38
    assert TT == 2 and TOPK % 8 == 0 and QR == 4 * LK and KR == P

    A0, B0, C0, D0 = 0, 3 * GW, 3 * GW + QR + KR + ROT, 6 * GW + QR + KR + ROT
    I0 = D0 + 3 * GW
    COLUMNS = {"aq": A0, "ak": A0 + GW, "av": A0 + 2 * GW, "cq": B0, "ckr": B0 + QR,
               "zq": C0, "zk": C0 + GW, "zv": C0 + 2 * GW, "dq": D0, "dk": D0 + GW, "dv": D0 + 2 * GW,
               "iq0": I0, "iq1": I0 + W, "ikw": I0 + 2 * W}
    WIDTH = {"cq": QR, "ckr": KR + ROT, "ikw": ID + IH, "qb1": HEADS * QD - W}
    GROUP_ORDER = [3, 1, 0, 2]
    FIRST_TILE = {"a": 0, "b": 4, "z": 8, "d": 12}

    class Strip:
        def __init__(s, kind, name, arg=0, halves=8):
            s.kind, s.name, s.arg = kind, name, arg
            s.width = WIDTH.get(name, W)
            s.rows = LK if name in ("qb0", "qb1") else P
            if kind == "kvb":
                s.halves = [([0], 0, W // 2), ([0], W // 2, W)]
            else:
                s.halves = [([2 * i, 2 * i + 1], 0, s.width) for i in range(halves)]

    class Position:
        def __init__(s, strip, i, steps):
            s.strip, s.i, s.steps = strip, i, steps

    def positions(strip, steps):
        return [Position(strip, i, steps.get(i, [])) for i in range(len(strip.halves))]

    head, begun = [], {}
    for name, rows in ATTENTION:
        if name in begun:
            s = begun[name]
        elif name[:2] == "wo":
            s = Strip("wo", name, int(name[2]))
        elif name[:2] == "qb":
            s = Strip("qb", name, int(name[2]), halves=2)
        elif name[:3] == "kvb":
            s = Strip("kvb", name, int(name[3]))
        else:
            s = Strip("in", name)
        begun[name] = s
        done = sum(pos.strip is s for pos in head)
        head += [Position(s, done + i, [tuple(x.split()) for x in row.split("; ") if x]) for i, row in enumerate(rows)]
    PARTS = [4, 4, 3]
    assert sum(PARTS) * W == HIDDEN

    def pair_strips(part, pair):
        return Strip("gate", "gate", (part, pair)), Strip("up", "up", (part, pair))

    sections = []
    for part, pairs in enumerate(PARTS):
        gate, up = pair_strips(part, 0)
        before = {0: [("X", "wo", "3")], 2: [("fT", "3"), ("xsq", "wo", "3")], 4: [("xms", "f")]} if part == 0 else \
                 {0: [("X", f"down{part - 1}", "3")]}
        head += positions(gate, before) + positions(up, {0: [("G", "first")]})
        sections.append(("line", head))
        gate, up = pair_strips(part, 1)
        sections.append(("loop", pairs - 1,
                         positions(gate, {0: [("U", "before")], 2: [("hidT", "0", "before")], 3: [("hidT", "1", "before")]})
                         + positions(up, {0: [("G", "this")]})))
        head = []
        final = part == len(PARTS) - 1
        for s in range(4):
            strip = Strip("down", f"down{part}", (part, s), halves=2 * pairs)
            steps = {0: [("X", f"down{part}", str(s - 1))]} if s else \
                    {0: [("U", "last")], 2: [("hidT", "0", "last")], 3: [("hidT", "1", "last")]}
            if s and final:
                steps[2] = [("xsq", f"down{part}", str(s - 1))]
                steps[3] = [("hT", str(s - 1))]
            if s == 0 and final:
                steps[4] = [("gains",)]
            head += positions(strip, steps)
        if final:
            sections.append(("line", head))
    LAST_STRIP = (f"down{len(PARTS) - 1}", "3")
    EARLY = 3

    def x_banks(q):
        return (2, 3) if q % 2 == 0 else (0, 1)

    BANKS = {"iqT": (2,), "ikT": (3,), "qkT": (2,), "latT": (2,), "ckvT": (3,), "pT": (2,),
             "pv": (3,), "oT": (2,)}

    def banks(step):
        kind = step[0]
        if kind in ("hT", "fT"):
            return x_banks(int(step[1]))
        if kind == "idx":
            return (0, 1)
        if kind in ("z", "R"):
            return (int(step[1]) % 2,)
        if kind == "qk":
            return (int(step[2]) % 2,)
        if kind == "hidT":
            return (2 + int(step[1]),)
        return BANKS.get(kind, ())

    HIGH = ("latT", "ckvT", "oT", "hidT")
    strips, use, high, ms_event = {}, {}, {}, {}
    n_half = n_strip = n_high = n_ms = 0
    n_use = [0] * 4
    pairs_seen = {}
    for section in sections:
        body = section[-1]
        turns = section[1] if section[0] == "loop" else 1
        start = (n_half, n_strip, n_high, list(n_use))
        for pos in body:
            pos.place = n_half
            n_half += 1
            s = pos.strip
            if pos.i == len(s.halves) - 1:
                s.last_half = pos.place
            if pos.i == 0:
                s.parity, s.turn = n_strip % 2, n_strip // 2
                n_strip += 1
                if s.kind in ("gate", "up"):
                    pairs_seen[s.kind, section[0] == "loop", s.arg[0]] = s
                else:
                    strips[s.name if s.kind != "down" else (s.name, s.arg[1])] = s
                if s.kind == "wo":
                    strips["wo", s.arg] = s
            for step in pos.steps:
                key = (step, section[0] == "loop", pos.strip.name if step[0] in ("hidT",) else "",
                       pos.strip.arg[0] if step[0] == "hidT" else 0)
                pos_key = key
                for b in banks(step):
                    use.setdefault(pos_key, {})[b] = n_use[b]
                    n_use[b] += 1
                if step[0] in ("hT", "fT"):
                    high[pos_key] = n_high
                    n_high += 2
                elif step[0] in HIGH or (step[0] == "pv" and step[1] != "a"):
                    high[pos_key] = n_high
                    n_high += 1
                if step[0] in ("xms", "ikss", "latss", "oss") or (step[0] == "ss" and step[2] == "1"):
                    ms_event[step] = n_ms
                    n_ms += 1
        if turns > 1:
            n_half += (turns - 1) * (n_half - start[0])
            n_strip += (turns - 1) * (n_strip - start[1])
            n_high += (turns - 1) * (n_high - start[2])
            for b in range(4):
                n_use[b] += (turns - 1) * (n_use[b] - start[3][b])
    HALVES, STRIPS, HIGHS, USES, MS = n_half, n_strip, n_high, n_use, n_ms
    assert HALVES % 4 == 0 and STRIPS % 2 == 0
    PAIR_HALVES = 16
    order = [step for section in sections for pos in section[-1] for step in pos.steps]

    def key_of(step, pos):
        loop = pos is not None and pos.strip.kind in ("gate", "up") and pos.strip.arg[1] == 1
        return (step, loop, pos.strip.name if step[0] == "hidT" else "", pos.strip.arg[0] if step[0] == "hidT" else 0)

    def last_of(names):
        by_parity = {}
        for s in sorted((strips[name] for name in names), key=lambda s: s.turn):
            by_parity[s.parity] = s
        return list(by_parity.values())

    def found(kind, *args):
        return ((kind, *args), False, "", 0)

    P_ORDER = [s for s in order if s[0] == "pT"]
    PV_ORDER = [s for s in order if s[0] == "pv"]
    QK_ORDER = [s for s in order if s[0] == "qk"]
    PROBS_ORDER = [s for s in order if s[0] in ("pT", "zexp")]

    def probs_slot(step):
        return PROBS_ORDER.index(step) % 2

    def pv_of(writer):
        return ("pv", "z", writer[1]) if writer[0] == "zexp" else ("pv", writer[1], writer[2])

    def writer_of(pv):
        return ("zexp", pv[2]) if pv[1] == "z" else ("pT", pv[1], pv[2])

    def slot_reader(qk):
        n, slot = order.index(qk), int(qk[2]) % 4
        for s in reversed(order[:n]):
            if s[0] == "pT" and (2 * int(s[2]) if s[1] == "a" else int(s[2])) % 4 == slot:
                return s
        return None

    MAP_DONE = [s for s in order if s[0] == "norm"]
    EXP_ORDER = [s for s in order if s[0] == "exp"]
    ROPE_ORDER = [s for s in order if s[0] in ("iqrope", "iknrm") or (s[0] == "rope" and s[1:] != ("b", "0"))]
    NRM_ORDER = [s for s in order if s[0] in ("iknrm", "onrm") or (s[0] == "nrm" and s[2] == "1")]
    SP_ORDER = [s for s in order if s[0] == "sp"]
    Z_ORDER = [s for s in order if s[0] == "R"]
    ZEXP_ORDER = [s for s in order if s[0] == "zexp"]

    ctx = ExitStack()
    with ctx:
        def sb(name, shape, dt=F32):
            return ctx.enter_context(nc.sbuf_tensor(name, shape, dt))

        def sem(name):
            return ctx.enter_context(nc.semaphore(name))

        raw = sb("raw", [P, 4, 2, W])
        w_hi, w_lo = sb("w_hi", [P, 4, 2, W], F32R), sb("w_lo", [P, 4, 2, W], F32R)
        x = sb("x", [P, TT, D])
        hT_hi, hT_lo = sb("hT_hi", [P, KD, SEQ], F32R), sb("hT_lo", [P, KD, SEQ], F32R)
        mT_hi, mT_lo = sb("mT_hi", [P, KD, SEQ], F32R), sb("mT_lo", [P, KD, SEQ], F32R)
        nat0 = sb("nat0", [P, TT, 1024])
        nat1 = sb("nat1", [P, TT, 1024])
        nat2 = sb("nat2", [P, TT, 1024])
        v_even, v_odd = sb("v_even", [P, TT, GW]), sb("v_odd", [P, TT, GW])
        T0, T1 = sb("T0", [P, 8, SEQ]), sb("T1", [P, 8, SEQ])
        Tr = sb("Tr", [P, 4, SEQ])
        SEG = [(0, P), (P, 3 * P)]
        E = sb("E", [P, 4, 3 * P])
        probs = sb("probs", [P, 2, 3 * P])
        picks, taken = (Tr[:, :, :].rearrange("p a b -> p (a b)")[:, i * 3 * P:(i + 1) * 3 * P] for i in (0, 1))
        ikT = sb("ikT", [P, SEQ])
        ikw = sb("ikw", [P, TT, ID + IH])
        ikd = sb("ikd", [P, TT, 2 * ID])
        iw = sb("iw", [P, TT, IH])
        best = sb("best", [P, TT, 8])
        junk = sb("junk", [P, 1024], BF16)
        rtmp = sb("rtmp", [P, 3, SEQ])
        stat = sb("stat", [P, 4, 4, TT])
        G_FFN, G_QA, G_KVA = DEPTH * KD, 2 * DEPTH * KD, 2 * DEPTH * KD + 4 * DEPTH
        NG = G_KVA + DEPTH
        gain_rows = T1[:, 0, 0:P]
        gain_all = sb("gain_all", [P, NG])
        gain = sb("gain", [P, KD + 5])
        hgain = sb("hgain", [P, KD])
        small = sb("small", [P, 1216])
        cst = sb("cst", [P, constants.shape[1]])
        lam = sb("lam", [P, 8])
        lam_init = sb("lam_init", [P, 2])
        xsq = sb("xsq", [P, TT, 4])
        mean = sb("mean", [P, 96])
        rinv = sb("rinv", [P, 96])
        minus_half = sb("minus_half", [P, 32])
        PS = ctx.enter_context(nc.psum_tensor("PS", [P, 8, W], F32))

        R_X, R_IK, R_D, R_LAT, R_A, R_B, R_O, R_XF = 0, 2, 4, 20, 24, 56, 72, 80
        MS_COLS = {("xms", "a"): (R_X, 2), ("ikss",): (R_IK, 2), ("ss", "d", "1"): (R_D, 16), ("latss",): (R_LAT, 4),
                   ("ss", "a", "1"): (R_A, 32), ("ss", "b", "1"): (R_B, 16), ("oss",): (R_O, 8), ("xms", "f"): (R_XF, 2)}
        S_DIFF, S_SUBLN, S_MLA, S_DSA, S_IDX, S_LAM = 0, 128, 256, 640, 896, 960
        ident, bias_t = cst[:, 0:P], cst[:, P:3 * P]
        strict01, strict_neg, upper, ones = (cst[:, (3 + i) * P:(4 + i) * P] for i in range(4))
        ROPE_AT = {8: 7 * P, 16: 7 * P + 32, 32: 7 * P + 96}
        C_LAM = 7 * P + 224

        def cos_sin(half):
            a = ROPE_AT[half]
            return (cst[:, a + i * 2 * half:a + (i + 1) * 2 * half].rearrange("p (t h) -> p t h", t=TT) for i in (0, 1))

        raw_full = [sem(f"raw_full{i}") for i in range(4)]
        hi_done = sem("hi_done")
        lo_done = sem("lo_done")
        half_used = sem("half_used")
        strip_taken = [sem("strip_taken0"), sem("strip_taken1")]
        bank_full = [sem(f"bank_full{i}") for i in range(4)]
        bank_taken = [sem(f"bank_taken{i}") for i in range(4)]
        high_done = sem("high_done")
        ident_full, tables_full, rows_full, small_full = sem("ident_full"), sem("tables_full"), sem("rows_full"), sem("small_full")
        x_full = [sem(f"x_full{q}") for q in range(4)]
        small_free = sem("small_free")
        init_done = sem("init_done")
        slot_seen = sem("slot_seen")
        gain_ready = sem("gain_ready")
        xsq_done = sem("xsq_done")
        ms_ready = sem("ms_ready")
        rinv_ready = sem("rinv_ready")
        nrm_done = sem("nrm_done")
        rope_done = sem("rope_done")
        relu_done = sem("relu_done")
        idx_added = sem("idx_added")
        max_done, exp_done, map_done = sem("max_done"), sem("exp_done"), sem("map_done")
        lam_sums, lam_exps = sem("lam_sums"), sem("lam_exps")
        ln_done, sp_done, z_done, zexp_done = sem("ln_done"), sem("sp_done"), sem("z_done"), sem("zexp_done")
        stored = sem("stored")

        last_strip = strips[LAST_STRIP[0], int(LAST_STRIP[1])]
        block = ctx.enter_context(nc.Block())

        def f(ap):
            return ap.bitcast(F32)

        def w_bank(b, n=W):
            return PS[:, 4 + b, 0:n]

        def raw_source(strip, i, l, pair):
            kts, c0, c1 = strip.halves[i]
            k0, nk = kts[0], len(kts)
            if strip.kind == "in":
                c = COLUMNS[strip.name]
                src = w_in[l, k0 * P:(k0 + nk) * P, c + c0:c + c1]
            elif strip.kind == "qb":
                src = mla_wq_b[l, k0 * LK:(k0 + nk) * LK, strip.arg * W:strip.arg * W + strip.width]
            elif strip.kind == "kvb":
                src = mla_wkv_b[l, :, strip.arg * W + c0:strip.arg * W + c1]
            elif strip.kind == "wo":
                r = GROUP_ORDER[k0 // 4] * GW + (k0 % 4) * P
                src = w_o[l, r:r + nk * P, strip.arg * W:(strip.arg + 1) * W]
            elif strip.kind in ("gate", "up"):
                part, p = strip.arg
                w = w_gate if strip.kind == "gate" else w_up
                c = (sum(PARTS[:part]) + p) * W
                src = w[l, k0 * P:(k0 + nk) * P, c:c + W] if pair is None else \
                    w[l, k0 * P:(k0 + nk) * P, bass.ds(pair * W + c, W)]
            else:
                part, s = strip.arg
                r = sum(PARTS[:part]) * W + k0 * P
                src = w_down[l, r:r + nk * P, s * W:(s + 1) * W]
            return src.rearrange("(t p) n -> p t n", p=strip.rows)

        def ahead(k, j, by):
            body = sections[k][-1]
            if j + by < len(body):
                pos = body[j + by]
                return pos.strip, pos.i, pos.place
            if sections[k][0] == "loop":
                pos = body[j + by - len(body)]
                return pos.strip, pos.i, pos.place + len(body)
            if k + 1 < len(sections):
                pos = sections[k + 1][-1][j + by - len(body)]
                return pos.strip, pos.i, pos.place
            return None

        LEAD = 2

        def starts_tensor(strip, i):
            k0, c0 = strip.halves[i][0][0], strip.halves[i][1]
            if strip.kind == "in":
                return COLUMNS[strip.name] == 0 and k0 == 0
            if strip.kind == "wo":
                return strip.arg == 0 and GROUP_ORDER[k0 // 4] == 0 and k0 % 4 == 0
            return strip.arg in (0, (0, 0)) and k0 == 0 and c0 == 0

        def walk(fori, line):
            for k, section in enumerate(sections):
                body = section[-1]
                if section[0] == "line":
                    for j, pos in enumerate(body):
                        line(pos, ahead(k, j, LEAD), None)
                else:
                    with fori(0, section[1]) as pair:
                        for j, pos in enumerate(body):
                            line(pos, ahead(k, j, LEAD), pair)

        class Place:
            def __init__(s, l):
                s.l, s.pair = l, None

            def __call__(s, n, per_layer, per_pair=0):
                v = s.l * per_layer + n
                if s.pair is not None and per_pair:
                    v = v + s.pair * per_pair
                return v

            def half(s, n):
                return s(n, HALVES, PAIR_HALVES)

            def strip(s, n):
                return s(n, STRIPS, 2)

            def bank(s, b, n):
                return s(n + sum(b in x_banks(q) for q in range(EARLY)), USES[b], 1)

            def high(s, n):
                return s(n + 2 * EARLY, HIGHS, 2)

        def split_view(strip, i, u):
            kts, c0, c1 = strip.halves[i]
            return slice(0, strip.rows), u % 4, slice(0, len(kts)), slice(0, c1 - c0)

        def pair_strip(kind, which, part):
            return pairs_seen[kind, False if which in ("first", "before") else True, part]

        @block.sync
        def _(sp):
            sp.dma_start(cst[:, 0:P], constants[:, 0:P]).then_inc(ident_full, 16)

            def load_x(q):
                sp.dma_start(x[:, :, q * W:(q + 1) * W],
                             x_in[0, :, q * W:(q + 1) * W].rearrange("(t p) n -> p t n", p=P)).then_inc(x_full[q], 16)

            load_x(0)
            sp.wait_ge(init_done, 1)
            for r, n, rows in ((0, P, attn_norm.rearrange("l (k p) -> (l k) p", p=P)),
                               (G_FFN, P, ffn_norm.rearrange("l (k p) -> (l k) p", p=P)),
                               (G_QA, LK, mla_q_a_norm.rearrange("l (k p) -> (l k) p", p=LK)), (G_KVA, P, mla_kv_a_norm)):
                sp.dma_start(gain_rows[r:r + rows.shape[0], 0:n], rows).then_inc(rows_full, 16)
            for q in range(1, 4):
                load_x(q)
            sp.dma_start(cst[:, P:], constants[:, P:]).then_inc(tables_full, 16)
            with sp.Fori(0, DEPTH) as l:
                at = Place(l)

                def load_small():
                    sp.wait_ge(small_free, at(1, 1))
                    for a, src in ((S_DIFF, diff_qk_norm), (S_MLA, mla_qk_norm), (S_DSA, dsa_qk_norm), (S_LAM, diff_lambda)):
                        n = src.shape[1] * src.shape[2]
                        rows = src[l].rearrange("(o a) b -> o (a b)", o=1).to_broadcast([P, n])
                        sp.dma_start(small[:, a:a + n], rows).then_inc(small_full, 16)
                    for a, src in ((S_SUBLN, diff_subln), (S_IDX, idx_k_norm)):
                        n = src.shape[1]
                        rows = src[l].rearrange("(o a) -> o a", o=1).to_broadcast([P, n])
                        sp.dma_start(small[:, a:a + n], rows).then_inc(small_full, 16)

                def line(pos, nxt, pair):
                    at.pair = pair
                    strip, i, u = pos.strip, pos.i, pos.place
                    if u == 4:
                        load_small()
                    r, slot, k, c = split_view(strip, i, u)
                    source = raw_source(strip, i, l, pair)
                    sp.wait_ge(lo_done, at.half(u + 1))
                    if pair is None and starts_tensor(strip, i):
                        sp.sem_inc(slot_seen, 1)
                    sp.dma_start(raw[r, slot, k, c], source).then_inc(raw_full[slot], 16)
                    at.pair = None

                walk(sp.Fori, line)
            for s in range(4):
                strip = strips[LAST_STRIP[0], s]
                for t in range(TT):
                    sp.wait_ge(strip_taken[strip.parity], (DEPTH - 1) * STRIPS + 2 * strip.turn + 9 + t)
                    sp.dma_start(out[0, t * P:(t + 1) * P, s * W:(s + 1) * W],
                                 x[:, t, s * W:(s + 1) * W]).then_inc(stored, 16)
            sp.wait_ge(stored, 16 * 4 * TT)

        @block.tensor
        def _(pe):
            pe.wait_ge(ident_full, 16)

            def turn(bank, tiles, source, rows=P):
                for j, tile in enumerate(tiles):
                    for t in range(TT):
                        o = j * SEQ + t * P
                        last = pe.transpose(PS[0:rows, 4 + bank, o:o + P], source(tile, t), ident)
                return last

            def turn_x(q, i, b):
                k = 4 * q + 2 * i
                turn(b, (k, k + 1), lambda k, t: x[:, t, k * P:(k + 1) * P]).then_inc(bank_full[b], 1)

            pe.wait_ge(rows_full, 64)
            pe.transpose(w_bank(0, NG), gain_rows[0:NG, :], cst[0:NG, 0:NG]).then_inc(init_done, 1)
            for q in range(EARLY):
                pe.wait_ge(x_full[q], 16)
                for i, b in enumerate(x_banks(q)):
                    pe.wait_ge(bank_taken[b], q // 2 + 1)
                    turn_x(q, i, b)
            pe.wait_ge(x_full[EARLY], 16)
            pe.wait_ge(tables_full, 16)
            with pe.Fori(0, DEPTH) as l:
                at = Place(l)

                def begin(b, key):
                    pe.wait_ge(bank_taken[b], at.bank(b, use[key][b] + 1))

                def step(s, pos, key):
                    kind = s[0]
                    if kind in ("hT", "fT"):
                        q = int(s[1])
                        if kind == "fT":
                            d, before = strips["wo", q], 0
                        else:
                            d, before = strips[LAST_STRIP[0], q], STRIPS if q == EARLY else 0
                        pe.wait_ge(strip_taken[d.parity], at(2 * d.turn + 10 - before, STRIPS))
                        for i, b in enumerate(x_banks(q)):
                            begin(b, key)
                            turn_x(q, i, b)
                    elif kind == "iqT":
                        pe.wait_ge(rope_done, at(ROPE_ORDER.index(("iqrope",)) + 1, len(ROPE_ORDER)))
                        begin(2, key)
                        i = int(s[1])
                        turn(2, (2 * i, 2 * i + 1), lambda k, t: nat0[:, t, k * P:(k + 1) * P]).then_inc(bank_full[2], 1)
                    elif kind == "ikT":
                        pe.wait_ge(rope_done, at(ROPE_ORDER.index(("iknrm",)) + 1, len(ROPE_ORDER)))
                        begin(3, key)
                        turn(3, (0,), lambda k, t: ikd[:, t, :]).then_inc(bank_full[3], 1)
                    elif kind == "idx":
                        for e in (0, 1):
                            rows = slice(e * ID, (e + 1) * ID)
                            if s[1] == "0" and e == 0:
                                pe.wait_ge(bank_taken[3], at.bank(3, use[found("ikT")][3] + 2))
                                pe.wait_ge(bank_taken[2], at.bank(2, use[found("iqT", "3")][2] + 2))
                            begin(e, key)
                            for t in range(TT):
                                a, z = SEG[t]
                                last = pe.matmul(PS[:, 4 + e, a:z], T0[rows, int(s[1]), t * P:(t + 1) * P],
                                                 ikT[rows, 0:z - a], start=True, stop=True)
                            last.then_inc(bank_full[e], 1)
                    elif kind == "qkT":
                        g, i = s[1], int(s[2])
                        if g == "z":
                            for st in last_of(("zq", "zk")):
                                pe.wait_ge(strip_taken[st.parity], at(2 * st.turn + 10, STRIPS))
                        else:
                            last_rope = ("rope", "b", "1") if g == "b" else ("rope", g)
                            pe.wait_ge(rope_done, at(ROPE_ORDER.index(last_rope) + 1, len(ROPE_ORDER)))
                        begin(2, key)
                        if g == "b":
                            nat = (nat0, nat0, nat2, nat2, nat0, nat2)[i]
                            src = (lambda k, t: nat[:, t, (k % 4) * QD:(k % 4) * QD + HD]) if i < 4 else \
                                (lambda k, t: nat[:, t, HEADS * QD + (k % 2) * P:HEADS * QD + (k % 2 + 1) * P])
                        else:
                            nat = nat0 if g == "z" else nat1
                            src = lambda k, t: nat[:, t, k * P:(k + 1) * P]
                        turn(2, (2 * i, 2 * i + 1), src).then_inc(bank_full[2], 1)
                    elif kind == "latT":
                        i = int(s[1])
                        st = strips["cq"]
                        pe.wait_ge(strip_taken[st.parity], at(2 * st.turn + 10, STRIPS))
                        begin(2, key)
                        turn(2, (2 * i, 2 * i + 1), lambda k, t: nat0[:, t, k * LK:(k + 1) * LK], rows=LK).then_inc(bank_full[2], 1)
                    elif kind == "ckvT":
                        st = strips["ckr"]
                        pe.wait_ge(strip_taken[st.parity], at(2 * st.turn + 10, STRIPS))
                        begin(3, key)
                        turn(3, (0,), lambda k, t: nat2[:, t, 832:832 + KR]).then_inc(bank_full[3], 1)
                    elif kind == "qk":
                        g, m = s[1], int(s[2])
                        b = m % 2
                        if m == 0:
                            i = 5 if g == "b" else 3
                            pe.wait_ge(bank_taken[2], at.bank(2, use[found("qkT", g, str(i))][2] + 2))
                        begin(b, key)
                        for t in range(TT):
                            a, z = SEG[t]
                            o, q = PS[:, 4 + b, a:z], slice(t * P, (t + 1) * P)
                            if g == "d":
                                last = pe.matmul(o, T1[:, m, q], T1[:, HEADS + m, 0:z - a], start=True, stop=True)
                            elif g == "a":
                                rows = slice((m % 2) * SUB, (m % 2 + 1) * SUB)
                                last = pe.matmul(o, T1[rows, m // 2, q], T1[rows, HEADS + m // 2, 0:z - a], start=True, stop=True)
                            else:
                                rows = slice((m % 2) * ROT, (m % 2 + 1) * ROT)
                                pe.matmul(o, T0[:, m, q], T0[:, HEADS + m, 0:z - a], start=True, stop=False)
                                last = pe.matmul(o, Tr[rows, m // 2, q], Tr[rows, 2 + m // 2, 0:z - a], start=False, stop=True)
                        last.then_inc(bank_full[b], 1)
                    elif kind == "pT":
                        g, h = s[1], int(s[2])
                        slot = (2 * h if g == "a" else h) % 4
                        pe.wait_ge(map_done, at(MAP_DONE.index(("norm", g, s[2])) + 1, len(MAP_DONE)))
                        begin(2, key)
                        for i in range(3):
                            last = pe.transpose(PS[:, 6, i * P:(i + 1) * P], E[:, slot, i * P:(i + 1) * P], ident)
                        last.then_inc(bank_full[2], 1)
                    elif kind == "pv":
                        g, h = s[1], int(s[2])
                        v = v_even if g in ("d", "a") else v_odd
                        for st in last_of({"d": ("dv",), "a": ("av",), "z": ("zv",), "b": ("kvb0", "kvb1")}[g]):
                            pe.wait_ge(strip_taken[st.parity], at(2 * st.turn + 10, STRIPS))
                        w = writer_of(s)
                        if g == "z":
                            pe.wait_ge(zexp_done, at(ZEXP_ORDER.index(w) + 1, len(ZEXP_ORDER)))
                        else:
                            pe.wait_ge(bank_taken[2], at.bank(2, use[found(*w)][2] + 2))
                        begin(3, key)
                        pr, cols = probs[:, probs_slot(w), :], slice(h * HD, (h + 1) * HD)
                        if g == "a":
                            pe.matmul(PS[:, 7, 0:P], pr[:, 0:P], v[:, 0, cols], start=True, stop=True)
                            pe.matmul(PS[:, 7, P:2 * P], pr[:, P:2 * P], v[:, 0, cols], start=True, stop=False)
                            last = pe.matmul(PS[:, 7, P:2 * P], pr[:, 2 * P:3 * P], v[:, 1, cols], start=False, stop=True)
                        else:
                            pe.matmul(PS[:, 7, 0:SEQ], v[:, 0, cols], pr[:, 0:SEQ], start=True, stop=False)
                            last = pe.matmul(PS[:, 7, P:SEQ], v[:, 1, cols], pr[:, SEQ:3 * P], start=False, stop=True)
                        last.then_inc(bank_full[3], 1)
                    elif kind == "oT":
                        i = int(s[1])
                        pe.wait_ge(nrm_done, at(NRM_ORDER.index(("onrm",)) + 1, len(NRM_ORDER)))
                        begin(2, key)
                        turn(2, (2 * i, 2 * i + 1), lambda k, t: nat1[:, t, k * P:(k + 1) * P]).then_inc(bank_full[2], 1)
                    elif kind == "z":
                        h = int(s[1])
                        b = h % 2
                        if h == 0:
                            pe.wait_ge(bank_taken[2], at.bank(2, use[found("qkT", "z", "3")][2] + 2))
                        begin(b, key)
                        pe.matmul(PS[:, 4 + b, 0:SEQ], T0[:, HEADS + h, 0:P], T0[:, h, :], start=True, stop=True)
                        pe.matmul(PS[:, 4 + b, SEQ:3 * P], T0[:, HEADS + h, P:SEQ], T0[:, h, P:SEQ],
                                  start=True, stop=True).then_inc(bank_full[b], 1)
                    elif kind == "R":
                        h = int(s[1])
                        b = h % 2
                        pe.wait_ge(sp_done, at(SP_ORDER.index(("sp", s[1])) + 1, len(SP_ORDER)))
                        begin(b, key)
                        pe.matmul(PS[:, 4 + b, 0:3 * P], upper, E[:, h, :], start=True, stop=False)
                        pe.matmul(PS[:, 4 + b, P:SEQ], ones, E[:, h, SEQ:3 * P], start=False, stop=True).then_inc(bank_full[b], 1)
                    elif kind == "hidT":
                        i = int(s[1])
                        up = pair_strip("up", s[2], pos.strip.arg[0])
                        turns = PARTS[up.arg[0]] - 2 if s[2] == "last" else 0
                        pe.wait_ge(strip_taken[1], at.strip(2 * (up.turn + turns) + 10))
                        begin(2 + i, key)
                        turn(2 + i, (2 * i, 2 * i + 1), lambda k, t: nat1[:, t, k * P:(k + 1) * P]).then_inc(bank_full[2 + i], 1)

                def operand(strip, kt):
                    if strip.kind in ("in", "gate", "up"):
                        return hT_hi[:, kt, :], hT_lo[:, kt, :]
                    if strip.kind == "qb":
                        return mT_hi[0:LK, 4 + kt, :], mT_lo[0:LK, 4 + kt, :]
                    if strip.kind == "kvb":
                        return mT_hi[:, 8, :], mT_lo[:, 8, :]
                    if strip.kind == "wo":
                        kt = 4 * GROUP_ORDER[kt // 4] + kt % 4
                    return mT_hi[:, kt, :], mT_lo[:, kt, :]

                def operand_wait(pos):
                    strip, i = pos.strip, pos.i
                    if strip is sections[0][1][0].strip and i % 2 == 0:
                        k = found("hT", str(i // 2))
                        for b in x_banks(i // 2):
                            pe.wait_ge(bank_taken[b], at.bank(b, use[k][b] + 2 - (USES[b] if i // 2 < EARLY else 0)))
                    elif strip.kind == "gate" and strip.arg == (0, 0) and i % 2 == 0:
                        k = found("fT", str(i // 2))
                        for b in x_banks(i // 2):
                            pe.wait_ge(bank_taken[b], at.bank(b, use[k][b] + 2))
                    elif strip.kind == "qb" and i == 0:
                        pe.wait_ge(bank_taken[2], at.bank(2, use[found("latT", "1")][2] + 2))
                    elif strip.kind == "kvb" and i == 0:
                        pe.wait_ge(bank_taken[3], at.bank(3, use[found("ckvT")][3] + 2))
                    elif strip.kind == "wo" and strip.arg == 0 and i % 2 == 0:
                        g = {3: "d", 1: "b", 0: "a", 2: "z"}[GROUP_ORDER[i // 2]]
                        if g == "a":
                            pe.wait_ge(bank_taken[2], at.bank(2, use[found("oT", "1")][2] + 2))
                        else:
                            pe.wait_ge(bank_taken[3], at.bank(3, use[found("pv", g, "3")][3] + 2))
                    elif strip.kind == "down" and strip.arg[1] == 0 and i == len(strip.halves) - 2:
                        for j in (0, 1):
                            k = (("hidT", str(j), "last"), False, strip.name, strip.arg[0])
                            pe.wait_ge(bank_taken[2 + j], at.bank(2 + j, use[k][2 + j] + 2))

                def line(pos, nxt, pair):
                    at.pair = pair
                    for s in pos.steps:
                        step(s, pos, key_of(s, pos))
                    strip = pos.strip
                    if pos.i == 0:
                        pe.wait_ge(strip_taken[strip.parity], at.strip(2 * strip.turn + 8))
                    operand_wait(pos)
                    n, i = len(strip.halves), pos.i
                    r, slot, _, _ = split_view(strip, i, pos.place)
                    kts, c0, c1 = strip.halves[i]
                    pe.wait_ge(lo_done, at.half(pos.place + 5))
                    for j, kt in enumerate(kts):
                        hi, lo = operand(strip, kt)
                        w1, w2 = w_hi[r, slot, j, 0:c1 - c0], w_lo[r, slot, j, 0:c1 - c0]
                        first = (i == 0 and j == 0) or strip.kind == "kvb"
                        final = (i == n - 1 and j == len(kts) - 1) or strip.kind == "kvb"
                        for t in range(TT):
                            o, q = PS[:, 2 * strip.parity + t, c0:c1], slice(t * P, (t + 1) * P)
                            pe.matmul(o, hi[:, q], w1, start=first, stop=False)
                            pe.matmul(o, hi[:, q], w2, start=False, stop=False)
                            last = pe.matmul(o, lo[:, q], w1, start=False, stop=final)
                    last.then_inc(half_used, 1)
                    at.pair = None

                walk(pe.Fori, line)

        @block.scalar
        def _(act):
            def square(s):
                for t in range(TT):
                    last = act.activation(nat0[:, t, 0:W], x[:, t, s * W:(s + 1) * W], ACT.Square, accum_out=xsq[:, t, s:s + 1])
                last.then_inc(xsq_done, 1)

            def x_high(q, i, b, g):
                for j in (0, 1):
                    k = 4 * q + 2 * i + j
                    last = act.activation(hT_hi[:, k, :], PS[:, 4 + b, j * SEQ:(j + 1) * SEQ], ACT.Copy, scale=g[:, k:k + 1])
                last.then_inc(high_done, 1)

            act.wait_ge(ident_full, 16)
            act.activation(lam[:, 6:7], cst[:, 0:1], ACT.Copy)
            act.wait_ge(gain_ready, 1)
            for q in range(EARLY):
                for i, b in enumerate(x_banks(q)):
                    act.wait_ge(bank_full[b], q // 2 + 1)
                    x_high(q, i, b, hgain)
            with act.Fori(0, DEPTH) as l:
                at = Place(l)

                def split(strip, i, u):
                    r, slot, k, c = split_view(strip, i, u)
                    act.wait_ge(raw_full[slot], at(16 * (u // 4 + 1), 4 * HALVES, 4 * PAIR_HALVES))
                    act.wait_ge(half_used, at.half(u + 1))
                    act.activation(w_hi[r, slot, k, c], raw[r, slot, k, c], ACT.Copy).then_inc(hi_done, 1)

                def full(b, key):
                    act.wait_ge(bank_full[b], at.bank(b, use[key][b] + 1))

                def step(s, pos, key):
                    kind = s[0]
                    if kind == "E":
                        st = strips[s[1]]
                        act.wait_ge(half_used, at.half(st.last_half + 5))
                        ev = ("latss",) if st.kind in ("qb", "kvb") else ("xms", "a")
                        act.wait_ge(rinv_ready, at(ms_event[ev] + 1, MS))
                        for t in range(TT):
                            src = PS[:, 2 * st.parity + t, 0:st.width]
                            col = R_X + t if st.kind == "in" else R_LAT + t + (2 if st.kind == "kvb" else 0)
                            r = rinv[:, col:col + 1]
                            if st.kind == "kvb":
                                heads = src.rearrange("p (h c) -> p h c", h=2)
                                k = nat2[:, t, 0:HEADS * QD].rearrange("p (h c) -> p h c", h=HEADS)
                                v = v_odd[:, t, :].rearrange("p (h c) -> p h c", h=HEADS)
                                hs = slice(2 * st.arg, 2 * st.arg + 2)
                                act.activation(k[:, hs, 0:HD], heads[:, :, 0:HD], ACT.Copy, scale=r)
                                last = act.activation(v[:, hs, :], heads[:, :, HD:2 * HD], ACT.Copy, scale=r)
                            else:
                                dst = {"iq0": nat0[:, t, 0:W], "iq1": nat0[:, t, W:2 * W], "ikw": ikw[:, t, :],
                                       "dq": nat1[:, t, 0:W], "dk": nat1[:, t, W:2 * W], "dv": v_even[:, t, :],
                                       "cq": nat0[:, t, 0:QR], "ckr": nat2[:, t, 832:832 + KR + ROT],
                                       "aq": nat1[:, t, 0:W], "ak": nat1[:, t, W:2 * W], "av": v_even[:, t, :],
                                       "qb0": nat0[:, t, 0:W], "qb1": nat0[:, t, W:HEADS * QD],
                                       "zq": nat0[:, t, 0:W], "zk": nat0[:, t, W:2 * W], "zv": v_odd[:, t, :]}[st.name]
                                last = act.activation(dst, src, ACT.Copy, scale=r)
                            last.then_inc(strip_taken[st.parity], 1)
                    elif kind in ("hT", "fT"):
                        q = int(s[1])
                        act.wait_ge(gain_ready, at(2 if kind == "fT" else 1 if q == EARLY else 3, 2))
                        for i, b in enumerate(x_banks(q)):
                            full(b, key)
                            x_high(q, i, b, gain if kind == "fT" else hgain)
                    elif kind == "latT":
                        act.wait_ge(gain_ready, at(2, 2))
                        full(2, key)
                        for j in (0, 1):
                            k = 2 * int(s[1]) + j
                            last = act.activation(mT_hi[0:LK, 4 + k, :], PS[0:LK, 6, j * SEQ:(j + 1) * SEQ], ACT.Copy,
                                                  scale=gain[0:LK, KD + k:KD + k + 1])
                        last.then_inc(high_done, 1)
                    elif kind == "ckvT":
                        act.wait_ge(gain_ready, at(2, 2))
                        full(3, key)
                        act.activation(mT_hi[:, 8, :], w_bank(3, SEQ), ACT.Copy,
                                       scale=gain[:, KD + 4:KD + 5]).then_inc(high_done, 1)
                    elif kind in ("iqT", "qkT"):
                        full(2, key)
                        if kind == "iqT":
                            dst = T0[:, 2 * int(s[1]):2 * int(s[1]) + 2, :]
                        else:
                            g, i = s[1], int(s[2])
                            dst = Tr[:, 2 * (i - 4):2 * (i - 4) + 2, :] if i >= 4 else \
                                (T1 if g in ("d", "a") else T0)[:, 2 * i:2 * i + 2, :]
                        act.activation(dst, w_bank(2).rearrange("p (j n) -> p j n", j=2), ACT.Copy).then_inc(bank_taken[2], 1)
                    elif kind == "ikT":
                        full(3, key)
                        act.activation(ikT[:, :], w_bank(3, SEQ), ACT.Copy).then_inc(bank_taken[3], 1)
                    elif kind == "idx":
                        for e in (0, 1):
                            head = 2 * int(s[1]) + e
                            full(e, key)
                            act.wait_ge(idx_added, at(head + 1, IH))
                            act.activation(E[:, 2 + e, :], w_bank(e, 3 * P), ACT.Relu).then_inc(relu_done, 1)
                    elif kind == "lam":
                        if s[1] == "1":
                            act.wait_ge(lam_sums, at(1, 1))
                            act.activation(lam[:, 2:4], lam[:, 0:2], ACT.Exp).then_inc(lam_exps, 1)
                    elif kind == "exp":
                        g, m = s[1], int(s[2])
                        slot = m % 4
                        scale = {"d": HD, "a": SUB, "b": QD}[g] ** -0.5
                        act.wait_ge(max_done, at(QK_ORDER.index(("qk", g, s[2])) + 1, len(QK_ORDER)))
                        for t in range(TT):
                            a, z = SEG[t]
                            last = act.activation(E[:, slot, a:z], E[:, slot, a:z], ACT.Exp, bias=stat[:, slot, 1, t:t + 1],
                                                  scale=scale, accum_out=stat[:, slot, 2, t:t + 1])
                        last.then_inc(exp_done, 1)
                    elif kind == "pT":
                        full(2, key)
                        n = PROBS_ORDER.index(s)
                        if n >= 2:
                            act.wait_ge(bank_full[3], at.bank(3, use[found(*pv_of(PROBS_ORDER[n - 2]))][3] + 1))
                        act.activation(probs[:, n % 2, :], w_bank(2, 3 * P), ACT.Copy).then_inc(bank_taken[2], 1)
                    elif kind == "pv":
                        g, h = s[1], int(s[2])
                        full(3, key)
                        if g == "a":
                            act.activation(nat1[:, :, h * HD:(h + 1) * HD], w_bank(3, SEQ).rearrange("p (t d) -> p t d", t=TT),
                                           ACT.Copy).then_inc(bank_taken[3], 1)
                        else:
                            act.activation(mT_hi[:, FIRST_TILE[g] + h, :], w_bank(3, SEQ), ACT.Copy).then_inc(high_done, 1)
                    elif kind == "oT":
                        full(2, key)
                        i = int(s[1])
                        act.activation(mT_hi[:, 2 * i:2 * i + 2, :], w_bank(2).rearrange("p (j n) -> p j n", j=2),
                                       ACT.Copy).then_inc(high_done, 1)
                    elif kind == "z":
                        h = int(s[1])
                        b = h % 2
                        full(b, key)
                        logits = nat2[:, :, :].rearrange("p t n -> p (t n)")[:, h * 3 * P:(h + 1) * 3 * P]
                        act.activation(logits, w_bank(b, 3 * P), ACT.Copy, scale=HD ** -0.5)
                        act.activation(E[:, h, :], w_bank(b, 3 * P), ACT.Abs, scale=HD ** -0.5).then_inc(bank_taken[b], 1)
                        act.drain()
                        act.activation(E[:, h, :], E[:, h, :], ACT.Exp, scale=-1.0)
                    elif kind == "zln":
                        act.drain()
                        act.activation(E[:, :, :], E[:, :, :], ACT.Ln, bias=1.0).then_inc(ln_done, 1)
                    elif kind == "zexp":
                        h = int(s[1])
                        n = PROBS_ORDER.index(s)
                        logits = nat2[:, :, :].rearrange("p t n -> p (t n)")[:, h * 3 * P:(h + 1) * 3 * P]
                        act.wait_ge(z_done, at(Z_ORDER.index(("R", s[1])) + 1, len(Z_ORDER)))
                        if n >= 2:
                            act.wait_ge(bank_full[3], at.bank(3, use[found(*pv_of(PROBS_ORDER[n - 2]))][3] + 1))
                        act.activation(probs[:, n % 2, :], logits, ACT.Exp).then_inc(zexp_done, 1)
                    elif kind == "xsq":
                        d = strips[s[1], int(s[2])]
                        act.drain()
                        before = STRIPS if d is last_strip else 0
                        act.wait_ge(strip_taken[d.parity], at(2 * d.turn + 10 - before, STRIPS))
                        square(int(s[2]))
                    elif kind == "G":
                        gate = pair_strip("gate", s[1], pos.strip.arg[0])
                        act.wait_ge(half_used, at.half(gate.last_half + 5))
                        act.wait_ge(rinv_ready, at(ms_event["xms", "f"] + 1, MS))
                        for t in range(TT):
                            act.activation(nat0[:, t, 0:W], PS[:, 2 * gate.parity + t, :], ACT.Silu,
                                           scale=rinv[:, R_XF + t:R_XF + t + 1]).then_inc(strip_taken[gate.parity], 1)
                    elif kind == "hidT":
                        i = int(s[1])
                        b = 2 + i
                        full(b, key)
                        part = pos.strip.arg[0]
                        if s[2] == "last":
                            k = 4 * (PARTS[part] - 1) + 2 * i
                            dst = mT_hi[:, k:k + 2, :]
                        else:
                            dst = mT_hi[:, bass.ds(at.pair * 4 + 2 * i, 2), :]
                        act.activation(dst, w_bank(b).rearrange("p (j n) -> p j n", j=2), ACT.Copy).then_inc(high_done, 1)

                def line(pos, nxt, pair):
                    at.pair = pair
                    if pos is sections[0][1][0]:
                        for by in range(LEAD):
                            split(*ahead(0, 0, by))
                    if nxt is not None:
                        split(*nxt)
                    for s in pos.steps:
                        step(s, pos, key_of(s, pos))
                    at.pair = None

                walk(act.Fori, line)

        @block.vector
        def _(dve):
            dve.sem_inc(lo_done, 4)
            dve.sem_inc(half_used, 4)
            dve.memset(PS[:, 2 * last_strip.parity:2 * last_strip.parity + 2, :], 0.0)
            dve.sem_inc(strip_taken[last_strip.parity], 6)
            dve.sem_inc(strip_taken[1 - last_strip.parity], 8)
            dve.sem_inc(small_free, 1)
            dve.sem_inc(idx_added, 2)
            dve.wait_ge(init_done, 2)
            dve.tensor_copy(gain_all[:, :], w_bank(0, NG))
            dve.drain()
            dve.tensor_copy(hgain[:, :], gain_all[:, 0:KD]).then_inc(gain_ready, 1)
            for b in range(4):
                dve.sem_inc(bank_taken[b], 1)

            def x_low(q, i, b, g):
                for j in (0, 1):
                    k = 4 * q + 2 * i + j
                    last = dve.scalar_tensor_tensor(hT_lo[:, k, :], PS[:, 4 + b, j * SEQ:(j + 1) * SEQ], g[:, k:k + 1],
                                                    f(hT_hi[:, k, :]), ALU.mult, ALU.subtract)
                last.then_inc(bank_taken[b], 1)

            for q in range(EARLY):
                dve.drain()
                dve.wait_ge(x_full[q], 16)
                for t in range(TT):
                    v = x[:, t, q * W:(q + 1) * W]
                    last = dve.tensor_tensor_reduce(out=junk[:, t * W:(t + 1) * W], in0=v, in1=v, scale=1.0, scalar=0.0,
                                                    op0=ALU.mult, op1=ALU.add, accum_out=xsq[:, t, q:q + 1])
                last.then_inc(xsq_done, 1)
                for i, b in enumerate(x_banks(q)):
                    dve.wait_ge(high_done, 2 * q + i + 1)
                    x_low(q, i, b, hgain)
            dve.wait_ge(x_full[EARLY], 16)
            dve.wait_ge(tables_full, 16)
            with dve.Fori(0, DEPTH) as l:
                at = Place(l)
                dve.drain()
                dve.tensor_copy(gain[:, 0:KD], gain_all[:, bass.ds(l * KD + G_FFN, KD)])
                dve.tensor_copy(gain[:, KD:KD + 4], gain_all[:, bass.ds(l * 4 + G_QA, 4)])
                dve.tensor_copy(gain[:, KD + 4:KD + 5], gain_all[:, bass.ds(l + G_KVA, 1)]).then_inc(gain_ready, 1)
                dve.tensor_copy(lam_init[:, :], cst[:, bass.ds(l * 2 + C_LAM, 2)])
                dve.drain()

                def split(strip, i, u):
                    r, slot, k, c = split_view(strip, i, u)
                    dve.wait_ge(hi_done, at.half(u + 1))
                    dve.tensor_tensor(w_lo[r, slot, k, c], raw[r, slot, k, c], f(w_hi[r, slot, k, c]),
                                      ALU.subtract).then_inc(lo_done, 1)

                def high_ready(key, i=0):
                    dve.wait_ge(high_done, at.high(high[key] + i + 1))

                def squares(src, n, width, col, width0=0):
                    for h in range(n):
                        v = src[:, h * width:(h + 1) * width]
                        dve.tensor_tensor_reduce(out=junk[:, h * width:(h + 1) * width], in0=v, in1=v, scale=1.0, scalar=0.0,
                                                 op0=ALU.mult, op1=ALU.add, accum_out=mean[:, col + h:col + h + 1])

                def to_mean(step, width):
                    col, n = MS_COLS[step]
                    dve.drain()
                    m = mean[:, col:col + n]
                    return dve.tensor_scalar(m, m, 1.0 / width, EPS, ALU.mult, ALU.add)

                def roots(step):
                    dve.wait_ge(rinv_ready, at(ms_event[step] + 1, MS))

                def scale_heads(src, n, width, col, g, goff):
                    for h in range(n):
                        v = src[:, h * width:(h + 1) * width]
                        last = dve.scalar_tensor_tensor(v, v, rinv[:, col + h:col + h + 1], g[:, goff:goff + width], ALU.mult, ALU.mult)
                    return last

                def step(s, pos, key):
                    kind = s[0]
                    if kind in ("hT", "fT"):
                        q = int(s[1])
                        for i, b in enumerate(x_banks(q)):
                            high_ready(key, i)
                            x_low(q, i, b, gain if kind == "fT" else hgain)
                    elif kind == "gains":
                        dve.tensor_copy(hgain[:, :], gain_all[:, bass.ds(l * KD + KD, KD)]).then_inc(gain_ready, 1)
                        dve.drain()
                    elif kind == "latT":
                        high_ready(key)
                        for j in (0, 1):
                            k = 2 * int(s[1]) + j
                            last = dve.scalar_tensor_tensor(mT_lo[0:LK, 4 + k, :], PS[0:LK, 6, j * SEQ:(j + 1) * SEQ],
                                                            gain[0:LK, KD + k:KD + k + 1], f(mT_hi[0:LK, 4 + k, :]),
                                                            ALU.mult, ALU.subtract)
                        last.then_inc(bank_taken[2], 1)
                    elif kind == "ckvT":
                        high_ready(key)
                        dve.scalar_tensor_tensor(mT_lo[:, 8, :], w_bank(3, SEQ), gain[:, KD + 4:KD + 5], f(mT_hi[:, 8, :]),
                                                 ALU.mult, ALU.subtract).then_inc(bank_taken[3], 1)
                    elif kind == "xms":
                        fours = {"a": 1, "f": 2}[s[1]]
                        col = MS_COLS[s][0]
                        dve.wait_ge(xsq_done, at(4 * fours, 8))
                        dve.tensor_reduce(mean[:, col:col + TT], xsq[:, :, :], AX.X, ALU.add)
                        to_mean(s, D).then_inc(ms_ready, 1)
                    elif kind == "lam":
                        if s[1] == "0":
                            dve.wait_ge(small_full, at(96, 96))
                            for i in (0, 1):
                                a = S_LAM + 2 * i * SUB
                                dve.tensor_tensor_reduce(out=junk[:, i * SUB:(i + 1) * SUB], in0=small[:, a:a + SUB],
                                                         in1=small[:, a + SUB:a + 2 * SUB], scale=1.0, scalar=0.0,
                                                         op0=ALU.mult, op1=ALU.add, accum_out=lam[:, i:i + 1])
                            dve.drain()
                            sub = small[:, S_SUBLN:S_SUBLN + HD]
                            dve.tensor_scalar(sub, sub, lam_init[:, 1:2], None, ALU.mult).then_inc(lam_sums, 1)
                        elif s[1] == "2":
                            dve.wait_ge(lam_exps, at(1, 1))
                            dve.tensor_tensor(lam[:, 5:6], lam[:, 3:4], lam[:, 2:3], ALU.subtract)
                            dve.drain()
                            dve.tensor_tensor(lam[:, 4:5], lam[:, 5:6], lam_init[:, 0:1], ALU.subtract)
                            dve.drain()
                    elif kind == "ikss":
                        dve.drain()
                        st = strips["ikw"]
                        dve.wait_ge(strip_taken[st.parity], at(2 * st.turn + 10, STRIPS))
                        for t in range(TT):
                            v = ikw[:, t, 0:ID]
                            dve.tensor_tensor_reduce(out=junk[:, t * ID:(t + 1) * ID], in0=v, in1=v, scale=1.0, scalar=0.0,
                                                     op0=ALU.mult, op1=ALU.add, accum_out=mean[:, R_IK + t:R_IK + t + 1])
                        to_mean(s, ID).then_inc(ms_ready, 1)
                    elif kind == "iknrm":
                        roots(("ikss",))
                        for t in range(TT):
                            dve.scalar_tensor_tensor(ikd[:, t, 0:ID], ikw[:, t, 0:ID], rinv[:, R_IK + t:R_IK + t + 1],
                                                     small[:, S_IDX:S_IDX + ID], ALU.mult, ALU.mult)
                        dve.tensor_scalar(iw[:, :, :], ikw[:, :, ID:ID + IH], ID ** -0.5 * IH ** -0.5, None, ALU.mult).then_inc(nrm_done, 1)
                    elif kind == "idx":
                        dve.drain()
                        for e in (0, 1):
                            head = 2 * int(s[1]) + e
                            acc = (picks, taken)[e]
                            dve.wait_ge(relu_done, at(head + 1, IH))
                            for t in range(TT):
                                a, z = SEG[t]
                                r, w = E[:, 2 + e, a:z], iw[:, t, head:head + 1]
                                if s[1] == "0":
                                    last = dve.tensor_scalar(acc[:, a:z], r, w, None, ALU.mult)
                                else:
                                    last = dve.scalar_tensor_tensor(acc[:, a:z], r, w, acc[:, a:z], ALU.mult, ALU.add)
                            last.then_inc(idx_added, 1)
                            dve.sem_inc(bank_taken[e], 1)
                    elif kind == "topk":
                        if s[1] == "0":
                            dve.drain()
                            dve.tensor_tensor(taken[:, :], taken[:, :], picks[:, :], ALU.add)
                            dve.drain()
                            dve.tensor_tensor(taken[:, 0:P], taken[:, 0:P], bias_t[:, P:2 * P], ALU.add)
                            dve.tensor_tensor(taken[:, P:3 * P], taken[:, P:3 * P], bias_t, ALU.add)
                        dve.drain()
                        for t in range(TT):
                            a, z = SEG[t]
                            dve.max(best[:, t, :], taken[:, a:z])
                        dve.drain()
                        for t in range(TT):
                            a, z = SEG[t]
                            dve.match_replace(taken[:, a:z], best[:, t, :], taken[:, a:z], TAKEN)
                    elif kind == "sel":
                        dve.drain()
                        dve.tensor_scalar(picks[:, :], taken[:, :], TAKEN / 2, MASKED, ALU.is_gt, ALU.mult)
                        dve.drain()
                        dve.tensor_tensor(picks[:, 0:P], picks[:, 0:P], bias_t[:, P:2 * P], ALU.add)
                        dve.tensor_tensor(picks[:, P:3 * P], picks[:, P:3 * P], bias_t, ALU.add)
                        dve.drain()
                    elif kind == "ss":
                        g, t = s[1], int(s[2])
                        dve.drain()
                        for st in last_of({"d": ("dq", "dk"), "a": ("aq", "ak"), "b": ("qb0", "qb1", "kvb0", "kvb1")}[g]):
                            dve.wait_ge(strip_taken[st.parity], at(2 * st.turn + 10, STRIPS))
                        if g == "d":
                            squares(nat1[:, t, :], 2 * HEADS, HD, R_D + t * 8)
                        elif g == "a":
                            squares(nat1[:, t, :], 4 * HEADS, SUB, R_A + t * 16)
                        else:
                            squares(nat0[:, t, :], HEADS, QD, R_B + t * 8)
                            dve.drain()
                            squares(nat2[:, t, :], HEADS, QD, R_B + t * 8 + 4)
                        if t == 1:
                            to_mean(s, {"d": HD, "a": SUB, "b": QD}[g]).then_inc(ms_ready, 1)
                    elif kind == "nrm":
                        g, t = s[1], int(s[2])
                        dve.drain()
                        roots(("ss", g, "1"))
                        if g == "d":
                            scale_heads(nat1[:, t, 0:W], HEADS, HD, R_D + t * 8, small, S_DSA)
                            last = scale_heads(nat1[:, t, W:2 * W], HEADS, HD, R_D + t * 8 + 4, small, S_DSA + HD)
                        elif g == "a":
                            scale_heads(nat1[:, t, 0:W], 2 * HEADS, SUB, R_A + t * 16, small, S_DIFF)
                            last = scale_heads(nat1[:, t, W:2 * W], 2 * HEADS, SUB, R_A + t * 16 + 8, small, S_DIFF + SUB)
                        else:
                            scale_heads(nat0[:, t, :], HEADS, QD, R_B + t * 8, small, S_MLA)
                            last = scale_heads(nat2[:, t, :], HEADS, QD, R_B + t * 8 + 4, small, S_MLA + QD)
                        if t == 1:
                            last.then_inc(nrm_done, 1)
                    elif kind == "latss":
                        dve.drain()
                        for st in last_of(("cq", "ckr")):
                            dve.wait_ge(strip_taken[st.parity], at(2 * st.turn + 10, STRIPS))
                        for t in range(TT):
                            for src, o, c in ((nat0[:, t, 0:QR], 0, R_LAT + t), (nat2[:, t, 832:832 + KR], QR, R_LAT + 2 + t)):
                                n = src.shape[1]
                                j = junk[:, o:o + n] if t == 0 else junk[:, o:o + n]
                                if t == 1 and o == 0:
                                    dve.drain()
                                dve.tensor_tensor_reduce(out=j, in0=src, in1=src, scale=1.0, scalar=0.0, op0=ALU.mult,
                                                         op1=ALU.add, accum_out=mean[:, c:c + 1])
                        dve.drain()
                        dve.tensor_scalar(mean[:, R_LAT:R_LAT + 2], mean[:, R_LAT:R_LAT + 2], 1.0 / QR, EPS, ALU.mult, ALU.add)
                        dve.tensor_scalar(mean[:, R_LAT + 2:R_LAT + 4], mean[:, R_LAT + 2:R_LAT + 4], 1.0 / KR, EPS,
                                          ALU.mult, ALU.add).then_inc(ms_ready, 1)
                    elif kind == "krcp":
                        for st in last_of(("ckr", "kvb0", "kvb1")):
                            dve.wait_ge(strip_taken[st.parity], at(2 * st.turn + 10, STRIPS))
                        for t in range(TT):
                            k = nat2[:, t, 0:HEADS * QD].rearrange("p (h c) -> p h c", h=HEADS)
                            kr = nat2[:, t, 832 + KR:832 + KR + ROT].unsqueeze(1).to_broadcast([P, HEADS, ROT])
                            dve.tensor_copy(k[:, :, HD:QD], kr)
                        dve.drain()
                    elif kind == "qk":
                        g, m = s[1], int(s[2])
                        b, slot = m % 2, m % 4
                        scale = {"d": HD, "a": SUB, "b": QD}[g] ** -0.5
                        reader = slot_reader(s)
                        dve.drain()
                        if reader is not None:
                            dve.wait_ge(bank_full[2], at.bank(2, use[found(*reader)][2] + 1))
                        dve.wait_ge(bank_full[b], at.bank(b, use[key][b] + 1))
                        dve.memset(stat[:, slot, 0, :], LOWEST)
                        dve.drain()
                        for t in range(TT):
                            a, z = SEG[t]
                            mask = picks[:, a:z] if g == "d" else (bias_t[:, P:2 * P] if t == 0 else bias_t)
                            last = dve.tensor_tensor_reduce(out=E[:, slot, a:z], in0=PS[:, 4 + b, a:z], in1=mask, scale=1.0,
                                                            scalar=LOWEST, op0=ALU.add, op1=ALU.max,
                                                            accum_out=stat[:, slot, 0, t:t + 1])
                        last.then_inc(bank_taken[b], 1)
                        dve.drain()
                        dve.tensor_scalar(stat[:, slot, 1, :], stat[:, slot, 0, :], -scale, None, ALU.mult).then_inc(max_done, 1)
                    elif kind == "norm":
                        g, h = s[1], int(s[2])
                        if g == "a":
                            both = max(EXP_ORDER.index(("exp", "a", str(2 * h + i))) for i in (0, 1))
                            dve.wait_ge(exp_done, at(both + 1, len(EXP_ORDER)))
                            e1, e2 = (2 * h) % 4, (2 * h + 1) % 4
                            dve.reciprocal(stat[:, e1, 3, :], stat[:, e1, 2, :])
                            dve.reciprocal(stat[:, e2, 3, :], stat[:, e2, 2, :])
                            dve.drain()
                            dve.tensor_scalar(stat[:, e2, 3, :], stat[:, e2, 3, :], lam[:, 4:5], None, ALU.mult)
                            for t in range(TT):
                                a, z = SEG[t]
                                dve.tensor_scalar(E[:, e1, a:z], E[:, e1, a:z], stat[:, e1, 3, t:t + 1], None, ALU.mult)
                            dve.drain()
                            for t in range(TT):
                                a, z = SEG[t]
                                last = dve.scalar_tensor_tensor(E[:, e1, a:z], E[:, e2, a:z], stat[:, e2, 3, t:t + 1],
                                                                E[:, e1, a:z], ALU.mult, ALU.add)
                        else:
                            dve.wait_ge(exp_done, at(EXP_ORDER.index(("exp", g, s[2])) + 1, len(EXP_ORDER)))
                            slot = h % 4
                            dve.reciprocal(stat[:, slot, 3, :], stat[:, slot, 2, :])
                            dve.drain()
                            for t in range(TT):
                                a, z = SEG[t]
                                last = dve.tensor_scalar(E[:, slot, a:z], E[:, slot, a:z], stat[:, slot, 3, t:t + 1], None, ALU.mult)
                        last.then_inc(map_done, 1)
                    elif kind == "pv":
                        g, h = s[1], int(s[2])
                        if g != "a":
                            high_ready(key)
                            k = FIRST_TILE[g] + h
                            dve.tensor_tensor(mT_lo[:, k, :], w_bank(3, SEQ), f(mT_hi[:, k, :]), ALU.subtract).then_inc(bank_taken[3], 1)
                    elif kind == "oss":
                        dve.drain()
                        dve.wait_ge(bank_taken[3], at.bank(3, use[found("pv", "a", "3")][3] + 2))
                        for t in range(TT):
                            o = t * 4 * HD
                            for h in range(HEADS):
                                v = nat1[:, t, h * HD:(h + 1) * HD]
                                dve.tensor_tensor_reduce(out=junk[:, o + h * HD:o + (h + 1) * HD], in0=v, in1=v, scale=1.0, scalar=0.0,
                                                         op0=ALU.mult, op1=ALU.add, accum_out=mean[:, R_O + 4 * t + h:R_O + 4 * t + h + 1])
                        to_mean(s, HD).then_inc(ms_ready, 1)
                    elif kind == "onrm":
                        roots(("oss",))
                        for t in range(TT):
                            last = scale_heads(nat1[:, t, 0:GW], HEADS, HD, R_O + 4 * t, small, S_SUBLN)
                        last.then_inc(nrm_done, 1)
                    elif kind == "oT":
                        high_ready(key)
                        i = int(s[1])
                        dve.tensor_tensor(mT_lo[:, 2 * i:2 * i + 2, :], w_bank(2).rearrange("p (j n) -> p j n", j=2),
                                          f(mT_hi[:, 2 * i:2 * i + 2, :]), ALU.subtract).then_inc(bank_taken[2], 1)
                    elif kind == "sp":
                        h = int(s[1])
                        logits = nat2[:, :, :].rearrange("p t n -> p (t n)")[:, h * 3 * P:(h + 1) * 3 * P]
                        dve.wait_ge(ln_done, at(1, 1))
                        dve.scalar_tensor_tensor(E[:, h, :], logits, 0.0, E[:, h, :], ALU.max, ALU.add)
                        dve.drain()
                        dve.tensor_tensor(E[:, h, 0:P], E[:, h, 0:P], strict01, ALU.mult)
                        dve.tensor_tensor(E[:, h, SEQ:3 * P], E[:, h, SEQ:3 * P], strict01, ALU.mult).then_inc(sp_done, 1)
                    elif kind == "R":
                        h = int(s[1])
                        b = h % 2
                        logits = nat2[:, :, :].rearrange("p t n -> p (t n)")[:, h * 3 * P:(h + 1) * 3 * P]
                        dve.wait_ge(bank_full[b], at.bank(b, use[key][b] + 1))
                        dve.tensor_tensor(logits, logits, w_bank(b, 3 * P), ALU.subtract).then_inc(bank_taken[b], 1)
                        dve.drain()
                        dve.tensor_tensor(logits[:, 0:P], logits[:, 0:P], strict_neg, ALU.add)
                        dve.tensor_tensor(logits[:, SEQ:3 * P], logits[:, SEQ:3 * P], strict_neg, ALU.add).then_inc(z_done, 1)
                    elif kind == "X":
                        st = strips[s[1], int(s[2])]
                        q = int(s[2])
                        dve.drain()
                        before = HALVES if st is last_strip else 0
                        dve.wait_ge(half_used, at.half(st.last_half + 5 - before))
                        for t in range(TT):
                            v = x[:, t, q * W:(q + 1) * W]
                            dve.tensor_tensor(v, v, PS[:, 2 * st.parity + t, :], ALU.add).then_inc(strip_taken[st.parity], 1)
                    elif kind == "U":
                        part = pos.strip.arg[0]
                        gate, up = pair_strip("gate", s[1], part), pair_strip("up", s[1], part)
                        turns = PARTS[part] - 2 if s[1] == "last" else 0
                        dve.wait_ge(half_used, at.half(up.last_half + PAIR_HALVES * turns + 5))
                        dve.wait_ge(strip_taken[0], at.strip(2 * (gate.turn + turns) + 10))
                        for t in range(TT):
                            dve.scalar_tensor_tensor(nat1[:, t, 0:W], PS[:, 2 * up.parity + t, :], rinv[:, R_XF + t:R_XF + t + 1],
                                                     nat0[:, t, 0:W], ALU.mult, ALU.mult).then_inc(strip_taken[up.parity], 1)
                    elif kind == "hidT":
                        i = int(s[1])
                        high_ready(key)
                        part = pos.strip.arg[0]
                        if s[2] == "last":
                            k = 4 * (PARTS[part] - 1) + 2 * i
                            hi, lo = mT_hi[:, k:k + 2, :], mT_lo[:, k:k + 2, :]
                        else:
                            ks = bass.ds(at.pair * 4 + 2 * i, 2)
                            hi, lo = mT_hi[:, ks, :], mT_lo[:, ks, :]
                        dve.tensor_tensor(lo, w_bank(2 + i).rearrange("p (j n) -> p j n", j=2), f(hi), ALU.subtract).then_inc(bank_taken[2 + i], 1)

                def line(pos, nxt, pair):
                    at.pair = pair
                    if pos is sections[0][1][0]:
                        for by in range(LEAD):
                            split(*ahead(0, 0, by))
                    if nxt is not None:
                        split(*nxt)
                    for s in pos.steps:
                        step(s, pos, key_of(s, pos))
                        if s == NRM_ORDER[-1]:
                            dve.drain()
                            dve.sem_inc(small_free, 1)
                    at.pair = None

                walk(dve.Fori, line)
            at = Place(DEPTH)
            step(("X", *LAST_STRIP), None, None)

        @block.gpsimd
        def _(pool):
            pool.memset(gain_rows, 0.0).then_inc(init_done, 1)
            pool.memset(minus_half[:, :], -0.5)
            pool.drain()
            pool.wait_ge(tables_full, 16)
            with pool.Fori(0, DEPTH) as l:
                at = Place(l)

                def rotate(x1, x2, y1, y2, half, heads):
                    cos, sin = (c.unsqueeze(2).to_broadcast([P, TT, heads, half]) for c in cos_sin(half))
                    n = heads * half
                    t0, t1, t2 = (rtmp[:, i, 0:TT * n].rearrange("p (t h c) -> p t h c", t=TT, h=heads) for i in range(3))
                    pool.tensor_tensor(t0, x1, cos, ALU.mult)
                    pool.tensor_tensor(t1, x2, sin, ALU.mult)
                    pool.tensor_tensor(t2, x1, sin, ALU.mult)
                    pool.drain()
                    pool.tensor_tensor(x2, x2, cos, ALU.mult)
                    pool.tensor_tensor(y1, t0, t1, ALU.subtract)
                    pool.drain()
                    return pool.tensor_tensor(y2, x2, t2, ALU.add)

                def step(s):
                    kind = s[0]
                    if kind in ("iqrope", "iknrm", "rope"):
                        pool.drain()
                    if s in ms_event:
                        col, n = MS_COLS[s]
                        pool.wait_ge(ms_ready, at(ms_event[s] + 1, MS))
                        pool.tensor_tensor(rinv[:, col:col + n], mean[:, col:col + n], minus_half[:, 0:n], ALU.pow).then_inc(rinv_ready, 1)
                    elif kind == "iqrope":
                        for st in last_of(("iq0", "iq1")):
                            pool.wait_ge(strip_taken[st.parity], at(2 * st.turn + 10, STRIPS))
                        v = nat0[:, :, :].rearrange("p t (h c) -> p t h c", h=IH)
                        rotate(v[:, :, :, 0:8], v[:, :, :, 8:16], v[:, :, :, 0:8], v[:, :, :, 8:16], 8, IH).then_inc(rope_done, 1)
                    elif kind == "iknrm":
                        pool.wait_ge(nrm_done, at(NRM_ORDER.index(s) + 1, len(NRM_ORDER)))
                        v = ikd[:, :, :].rearrange("p t (h c) -> p t h c", h=2)[:, :, 0:1, :]
                        rotate(v[:, :, :, 0:8], v[:, :, :, 8:16], v[:, :, :, 0:8], v[:, :, :, 8:16], 8, 1)
                        pool.drain()
                        pool.tensor_copy(ikd[:, :, ID:2 * ID], ikd[:, :, 0:ID]).then_inc(rope_done, 1)
                    elif kind == "rope":
                        g = s[1]
                        pool.wait_ge(nrm_done, at(NRM_ORDER.index(("nrm", g, "1")) + 1, len(NRM_ORDER)))
                        if g == "b":
                            nat = (nat0, nat2)[int(s[2])]
                            v = nat[:, :, 0:HEADS * QD].rearrange("p t (h c) -> p t h c", h=HEADS)
                            y = nat[:, :, HEADS * QD:HEADS * (QD + ROT)].rearrange("p t (h c) -> p t h c", h=HEADS)
                            last = rotate(v[:, :, :, HD:HD + 32], v[:, :, :, HD + 32:QD], y[:, :, :, 0:32], y[:, :, :, 32:64], 32, HEADS)
                            if s[2] == "1":
                                last.then_inc(rope_done, 1)
                        else:
                            n, half = (2 * HEADS, 16) if g == "d" else (4 * HEADS, 8)
                            v = nat1[:, :, :].rearrange("p t (h c) -> p t h c", h=n)
                            rotate(v[:, :, :, 0:half], v[:, :, :, half:2 * half], v[:, :, :, 0:half], v[:, :, :, half:2 * half],
                                   half, n).then_inc(rope_done, 1)

                for section in sections:
                    if section[0] == "line":
                        for pos in section[1]:
                            for s in pos.steps:
                                step(s)


_INS = ["x", "attn_norm", "w_in", "diff_qk_norm", "diff_lambda", "diff_subln", "mla_q_a_norm", "mla_wq_b", "mla_kv_a_norm",
        "mla_wkv_b", "mla_qk_norm", "dsa_qk_norm", "idx_k_norm", "w_o", "ffn_norm", "w_gate", "w_up", "w_down"]
_OUT = ((1, 256, 2048), "float32")


def _constants():
    import math
    import numpy as np
    P, MASKED = 128, -1e30
    r, c = np.arange(P)[:, None], np.arange(P)[None, :]
    parts = [np.eye(P), np.zeros((P, P)), np.where(c <= r, 0.0, MASKED), np.where(r < c, 1.0, 0.0),
             np.where(r < c, 0.0, MASKED), np.where(r >= c, 1.0, 0.0), np.ones((P, P))]
    for half in (8, 16, 32):
        inv = np.float32(500000.0) ** (-np.arange(half, dtype=np.float32) * np.float32(2.0) / np.float32(2 * half))
        ang = np.arange(2 * P, dtype=np.float32)[:, None] * inv.astype(np.float32)[None, :]
        for fn in (np.cos, np.sin):
            table = fn(ang.astype(np.float64))
            parts.append(table.reshape(2, P, half).transpose(1, 0, 2).reshape(P, 2 * half))
    for layer in range(2):
        start = 0.8 - 0.6 * math.exp(-0.3 * layer)
        parts.append(np.tile([[start, 1.0 - start]], (P, 1)))
    return np.ascontiguousarray(np.concatenate(parts, axis=1).astype(np.float32))


def kernel(**inputs):
    import numpy as _np
    import concourse.bacc as _bacc
    from concourse import mybir as _mybir
    from concourse.bass_utils import run_bass_kernel_spmd as _run

    nc = _bacc.Bacc("TRN2", target_bir_lowering=False, num_devices=1)
    arrays, args = {}, []
    for name in _INS + ["constants"]:
        a = _constants() if name == "constants" else _np.ascontiguousarray(inputs[name])
        arrays[f"in_{name}_dram"] = a
        args.append(nc.dram_tensor(f"in_{name}_dram", a.shape, _mybir.dt.from_np(a.dtype), kind="ExternalInput").ap())
    args.append(nc.dram_tensor("out_0_dram", _OUT[0], _mybir.dt.from_np(_np.dtype(_OUT[1])), kind="ExternalOutput").ap())
    trunk_kernel(nc, *args)
    r = _run(nc, [arrays], core_ids=[0])
    return r.results[0]["out_0_dram"]
```
